# Optimizing a Trainium2 kernel written in Bass

```python
import jax, jax.numpy as jnp
from jax import lax
import numpy as np

D_MODEL = 1024
BATCH = 1
SEQ = 256
DEPTH = 1

CHUNK = 64
Q_BLOCK = 128
DSA_HEADS = 8
DSA_HEAD_DIM = D_MODEL // DSA_HEADS
IDX_HEADS = 8
IDX_DIM = 64
IDX_TOPK_MAX = 256
GLA_HEADS = 4
GLA_DK = D_MODEL // 2 // GLA_HEADS
GLA_DV = D_MODEL // GLA_HEADS
GATE_RANK = 16
GATE_TAU = 16.0
N_EXPERTS = 32
TOP_K = 4
D_FF = D_MODEL
SWIGLU_LIMIT = 7.0
SWIGLU_ALPHA = 1.702
EXPERT_BLOCK = 128
EPS = 1e-6

IN_SIZES = (DSA_HEADS * DSA_HEAD_DIM, DSA_HEADS * DSA_HEAD_DIM, DSA_HEADS * DSA_HEAD_DIM,
            IDX_HEADS * IDX_DIM, IDX_DIM, IDX_HEADS,
            GLA_HEADS * GLA_DK, GLA_HEADS * GLA_DK, GLA_HEADS * GLA_DV, GLA_HEADS * GLA_DV,
            GATE_RANK, D_MODEL, D_MODEL)
IN_WIDTH = sum(IN_SIZES)

kernel_name = 'hybrid_dsa_gla_moe_adaln_block'

def _rmsnorm(x, g):
    xf = x.astype(jnp.float32)
    y = xf * lax.rsqrt(jnp.mean(xf * xf, axis=-1, keepdims=True) + EPS)
    return (y * g.astype(jnp.float32)).astype(x.dtype)

def _dsa(q, k, v, qi, ki, wi):
    B, T, H, dh = q.shape
    topk = min(IDX_TOPK_MAX, T // 4)
    nb = T // Q_BLOCK
    kchunk = jnp.arange(T) // CHUNK
    qi = qi * (IDX_DIM ** -0.5)
    wi = wi * (IDX_HEADS ** -0.5)
    gather = jax.vmap(lambda t, i: t[i])

    def blocks(t):
        return t.reshape((B, nb, Q_BLOCK) + t.shape[2:]).swapaxes(0, 1)

    def one_block(args):
        qb, qib, wb, blk = args
        qchunk = (blk * Q_BLOCK + jnp.arange(Q_BLOCK)) // CHUNK
        vis = kchunk[None, :] <= qchunk[:, None]
        rel = jax.nn.relu(jnp.einsum('bqhd,bsd->bqhs', qib, ki).astype(jnp.float32))
        score = jnp.einsum('bqhs,bqh->bqs', rel, wb.astype(jnp.float32))
        score = jnp.where(vis[None], score, -jnp.inf)
        _, sel = lax.top_k(score, topk)
        sel_vis = kchunk[sel] <= qchunk[None, :, None]
        ks = gather(k, sel)
        vs = gather(v, sel)
        logits = jnp.einsum('bqhd,bqkhd->bqhk', qb, ks).astype(jnp.float32) * (dh ** -0.5)
        logits = jnp.where(sel_vis[:, :, None, :], logits, -jnp.inf)
        p = jax.nn.softmax(logits, axis=-1).astype(vs.dtype)
        return jnp.einsum('bqhk,bqkhd->bqhd', p, vs)

    out = lax.map(one_block, (blocks(q), blocks(qi), blocks(wi), jnp.arange(nb)))
    return out.swapaxes(0, 1).reshape(B, T, H * dh)

def _gla(q, k, v, log_a):
    dtype = v.dtype
    B, T, H, DK = q.shape
    DV = v.shape[-1]
    n = T // CHUNK

    def chunks(t):
        return t.astype(jnp.float32).reshape(B, n, CHUNK, H, t.shape[-1]).transpose(1, 0, 3, 2, 4)

    qc = chunks(q) * (DK ** -0.5)
    kc = chunks(k)
    vc = chunks(v)
    G = jnp.cumsum(chunks(log_a), axis=-2)
    causal = jnp.tril(jnp.ones((CHUNK, CHUNK), dtype=bool))

    def step(S, inp):
        qn, kn, vn, gn = inp
        g_last = gn[:, :, -1:, :]
        qe = qn * jnp.exp(gn)
        A = jnp.einsum('bhid,bhjd->bhij', qe, kn * jnp.exp(-gn))
        A = jnp.where(causal, A, 0.0)
        o = jnp.einsum('bhij,bhjv->bhiv', A, vn) + jnp.einsum('bhid,bhdv->bhiv', qe, S)
        S = S * jnp.exp(g_last).swapaxes(-1, -2) + jnp.einsum('bhjd,bhjv->bhdv', kn * jnp.exp(g_last - gn), vn)
        return S, o

    S0 = jnp.zeros((B, H, DK, DV), jnp.float32)
    _, o = lax.scan(step, S0, (qc, kc, vc, G))
    return o.transpose(1, 0, 3, 2, 4).reshape(B, T, H, DV).astype(dtype)

def _moe(h, router_w, router_b, w_gate_up, b_gate_up, w_down, b_down):
    B, T, D = h.shape
    N = B * T
    xt = h.reshape(N, D)
    logits = (xt @ router_w + router_b).astype(jnp.float32)
    top_v, top_e = lax.top_k(logits, TOP_K)
    wts = jax.nn.softmax(top_v, axis=-1)
    n_assign = N * TOP_K
    flat_e = top_e.reshape(-1)
    order = jnp.argsort(flat_e)
    sorted_e = flat_e[order]
    tok = (order // TOP_K).astype(jnp.int32)
    sorted_w = wts.reshape(-1)[order]
    gs = jnp.bincount(flat_e, length=N_EXPERTS).astype(jnp.int32)
    ps = ((gs + EXPERT_BLOCK - 1) // EXPERT_BLOCK) * EXPERT_BLOCK
    off = jnp.cumsum(gs) - gs
    poff = jnp.cumsum(ps) - ps
    pad_pos = poff[sorted_e] + (jnp.arange(n_assign, dtype=jnp.int32) - off[sorted_e])
    n_blocks = -(-n_assign // EXPERT_BLOCK) + N_EXPERTS
    P = n_blocks * EXPERT_BLOCK
    ptok = jnp.full((P,), N, jnp.int32).at[pad_pos].set(tok)
    pw = jnp.zeros((P,), jnp.float32).at[pad_pos].set(sorted_w)
    blk_e = jnp.minimum(jnp.searchsorted(jnp.cumsum(ps), jnp.arange(n_blocks) * EXPERT_BLOCK, side='right'),
                        N_EXPERTS - 1)
    xpad = jnp.concatenate([xt, jnp.zeros((1, D), xt.dtype)], axis=0)
    xs = xpad[ptok].reshape(n_blocks, EXPERT_BLOCK, D)

    def expert_block(args):
        xb, e = args
        hgu = xb @ w_gate_up[e] + b_gate_up[e]
        gate, up = jnp.split(hgu, 2, axis=-1)
        gate = jnp.minimum(gate, SWIGLU_LIMIT)
        up = jnp.clip(up, -SWIGLU_LIMIT, SWIGLU_LIMIT)
        act = (up + 1.0) * (gate * jax.nn.sigmoid(SWIGLU_ALPHA * gate))
        return act @ w_down[e] + b_down[e]

    ys = lax.map(expert_block, (xs, blk_e)).reshape(P, D)
    out = jax.ops.segment_sum(ys * pw[:, None].astype(ys.dtype), ptok, num_segments=N + 1)[:N]
    return out.reshape(B, T, D)

def _layer(x, c, w_ada, b_ada, norm1_g, w_in, w_gate_lr, b_gate, gla_norm_g, w_branch_a, w_branch_b,
           w_out, norm2_g, router_w, router_b, w_gate_up, b_gate_up, w_down, b_down):
    B, T, _ = x.shape
    mod = (jax.nn.silu(c) @ w_ada + b_ada)[:, None, :]
    sh1, sc1, gt1, sh2, sc2, gt2 = jnp.split(mod, 6, axis=-1)
    h = _rmsnorm(x, norm1_g) * (1.0 + sc1) + sh1
    proj = h @ w_in
    split_pts = np.cumsum(IN_SIZES)[:-1].tolist()
    qa, ka, va, qi, ki, wi, qb, kb, vb, gb, lr, ga, gbm = jnp.split(proj, split_pts, axis=-1)

    def heads(t, nh):
        return t.reshape(B, T, nh, -1)

    ya = _dsa(heads(qa, DSA_HEADS), heads(ka, DSA_HEADS), heads(va, DSA_HEADS),
              heads(qi, IDX_HEADS), ki, wi)
    log_a = jax.nn.log_sigmoid((lr @ w_gate_lr + b_gate).astype(jnp.float32)) / GATE_TAU
    ob = _gla(heads(qb, GLA_HEADS), heads(kb, GLA_HEADS), heads(vb, GLA_HEADS), heads(log_a, GLA_HEADS))
    yb = (_rmsnorm(ob, gla_norm_g) * jax.nn.silu(heads(gb, GLA_HEADS))).reshape(B, T, -1)
    merged = jax.nn.sigmoid(ga) * (ya @ w_branch_a) + jax.nn.sigmoid(gbm) * (yb @ w_branch_b)
    x = x + gt1 * (merged @ w_out)
    h2 = _rmsnorm(x, norm2_g) * (1.0 + sc2) + sh2
    x = x + gt2 * _moe(h2, router_w, router_b, w_gate_up, b_gate_up, w_down, b_down)
    return x

def setup_inputs(seed: int = 0) -> dict:
    key = jax.random.key(seed)
    ks = jax.random.split(key, 24)
    D = D_MODEL

    def nrm(k, shape, scale):
        return jax.random.normal(k, shape, jnp.float32) * scale

    return {
        'x': nrm(ks[0], (BATCH, SEQ, D), 1.0),
        'c': nrm(ks[1], (BATCH, D), 1.0),
        'w_ada': nrm(ks[2], (DEPTH, D, 6 * D), D ** -0.5),
        'b_ada': nrm(ks[3], (DEPTH, 6 * D), 0.02),
        'norm1_g': 1.0 + nrm(ks[4], (DEPTH, D), 0.02),
        'w_in': nrm(ks[5], (DEPTH, D, IN_WIDTH), D ** -0.5),
        'w_gate_lr': nrm(ks[6], (DEPTH, GATE_RANK, GLA_HEADS * GLA_DK), GATE_RANK ** -0.5),
        'b_gate': nrm(ks[7], (DEPTH, GLA_HEADS * GLA_DK), 0.1),
        'gla_norm_g': 1.0 + nrm(ks[8], (DEPTH, GLA_DV), 0.02),
        'w_branch_a': nrm(ks[9], (DEPTH, DSA_HEADS * DSA_HEAD_DIM, D), (DSA_HEADS * DSA_HEAD_DIM) ** -0.5),
        'w_branch_b': nrm(ks[10], (DEPTH, GLA_HEADS * GLA_DV, D), (GLA_HEADS * GLA_DV) ** -0.5),
        'w_out': nrm(ks[11], (DEPTH, D, D), D ** -0.5),
        'norm2_g': 1.0 + nrm(ks[12], (DEPTH, D), 0.02),
        'router_w': nrm(ks[13], (DEPTH, D, N_EXPERTS), D ** -0.5),
        'router_b': nrm(ks[14], (DEPTH, N_EXPERTS), 0.01),
        'w_gate_up': nrm(ks[15], (DEPTH, N_EXPERTS, D, 2 * D_FF), D ** -0.5),
        'b_gate_up': nrm(ks[16], (DEPTH, N_EXPERTS, 2 * D_FF), 0.02),
        'w_down': nrm(ks[17], (DEPTH, N_EXPERTS, D_FF, D), D_FF ** -0.5),
        'b_down': nrm(ks[18], (DEPTH, N_EXPERTS, D), 0.02),
        'final_g': 1.0 + nrm(ks[19], (D,), 0.02),
    }

def reference(x, c, w_ada, b_ada, norm1_g, w_in, w_gate_lr, b_gate, gla_norm_g, w_branch_a, w_branch_b,
              w_out, norm2_g, router_w, router_b, w_gate_up, b_gate_up, w_down, b_down, final_g):
    for l in range(DEPTH):
        x = _layer(x, c, w_ada[l], b_ada[l], norm1_g[l], w_in[l], w_gate_lr[l], b_gate[l], gla_norm_g[l],
                   w_branch_a[l], w_branch_b[l], w_out[l], norm2_g[l], router_w[l], router_b[l],
                   w_gate_up[l], b_gate_up[l], w_down[l], b_down[l])
    return _rmsnorm(x, final_g)


_drawn_inputs = setup_inputs


def setup_inputs(seed=0):
    import zlib

    import numpy as np

    out = dict(_drawn_inputs(seed))
    spreads = {}
    factors = {'gla_norm_g': 3.889,
     'b_gate_up': 6.732,
     'b_down': 8.0,
     'final_g': 7.897,
     'router_b': 3.764}
    for name, (base, spread) in spreads.items():
        noise = np.random.default_rng([zlib.crc32(name.encode()), seed]).standard_normal(out[name].shape)
        drawn = base * np.exp(spread * noise) if base else spread * noise
        out[name] = __import__('jax').numpy.asarray(drawn.astype(out[name].dtype))
    for name, factor in factors.items():
        out[name] = (out[name] * factor).astype(out[name].dtype)
    return out
```

```python
from contextlib import ExitStack

import concourse.bass as bass
from concourse import mybir

F32 = mybir.dt.float32
I32 = mybir.dt.int32
ALU = mybir.AluOpType
ACT = mybir.ActivationFunctionType
AX = mybir.AxisListType
ds = bass.ds

P = 128
CHUNK = 64
EPS = 1e-6
IDX_DIM = 64
GATE_TAU = 16.0
TOP_K = 4
LIMIT = 7.0
ALPHA = 1.702
HIDDEN = -1.0e30
TAKEN = -3.0e38
PAD = -2.0e38
SLOTS = 64

PLAN = (
    [(f"ada{i}", "A") for i in range(4)] + [("cols", "V")] + [(f"xT{i}", "V") for i in range(4)]
    + [("small", "A"), ("wi", "A"), ("qi0", "A"), ("qi1", "A"), ("z0", "A"), ("z1", "A"), ("qa0", "A"), ("qa1", "A")]
    + [("sx0", "A"), ("sx1", "A")] + [(f"sy{i}", "A") for i in range(4)] + [("qa2", "A"), ("qa3", "A")]
    + [("qb0", "V"), ("qb1", "V"), ("kb0", "V"), ("kb1", "V"), ("ka0", "A"), ("ka1", "A")]
    + [("kdT0", "A"), ("kdT1", "A"), ("AT", "A"), ("ka2", "A"), ("ka3", "A")]
    + [(f"vb{i}", "A") for i in range(4)] + [("s1a", "V"), ("s1b", "V"), ("va0", "A"), ("va1", "A")]
    + [("s2a", "V"), ("s2b", "V"), ("va2", "A"), ("va3", "A"), ("s3a", "V"), ("s3b", "V")]
    + [("lg0", "V"), ("lg1", "V"), ("gb0", "V"), ("gb1", "V"), ("pt0", "A"), ("pt1", "A"), ("lg2", "V"), ("lg3", "V")]
    + [("ya0", "A"), ("ya1", "A"), ("lg4", "V"), ("lg5", "V"), ("gb2", "V"), ("gb3", "V")]
    + [(f"pt{i}", "A") for i in range(2, 6)] + [(f"o{i}", "V") for i in range(4)] + [("ya2", "A"), ("ya3", "A")]
    + [(f"ga{i}", "A") for i in range(4)] + [(f"yT{i}", "A") for i in range(4)] + [(f"gm{i}", "A") for i in range(4)]
    + [t for r in range(8) for t in ((f"ap{r}", "A"), (f"ab{r}", "V"))]
    + [(f"wa{i}", "V") for i in range(4)] + [(f"wb{i}", "V") for i in range(4)] + [(f"wo{i}", "V") for i in range(4)]
    + [(f"hh{i}", "A") for i in range(4)] + [("rl", "A"), ("rt", "V"), ("wT", "A")] + [(f"bd{i}", "V") for i in range(4)]
)
NUMBER = {name: n for n, (name, _) in enumerate(PLAN)}
TAKER = dict(PLAN)
OUT_COUNT = {name: 1 + sum(1 for m, (_, w) in enumerate(PLAN) if w == who and m < n) for n, (name, who) in enumerate(PLAN)}

PIECES = (
    [("ada", i, f"ada{i}") for i in range(4)]
    + [("qi", 0, "qi1"), ("qa", 0, "qa1"), ("qa", 1, "qa3"), ("qb", 0, "qb1"), ("kb", 0, "kb1"), ("ka", 0, "ka1"),
       ("ka", 1, "ka3"), ("vb", 0, "vb1"), ("vb", 1, "vb3"), ("va", 0, "va1"), ("va", 1, "va3"), ("gb", 0, "gb1"),
       ("gb", 1, "gb3"), ("ga", 0, "ga1"), ("ga", 1, "ga3"), ("gm", 0, "gm1"), ("gm", 1, "gm3")]
    + [("ada", 4 + r, f"ap{r}") for r in range(8)]
    + [("wa", 0, "wa1"), ("wa", 1, "wa3"), ("wb", 0, "wb1"), ("wb", 1, "wb3"), ("wo", 0, "wo1"), ("wo", 1, "wo3")]
)
PIECE_NO = {(kind, c): n for n, (kind, c, _) in enumerate(PIECES)}


def hybrid_block(nc, x, c, w_ada, b_ada, norm1_g, w_in, w_gate_lr, b_gate, gla_norm_g, w_branch_a, w_branch_b, w_out,
                 norm2_g, router_w, router_b, w_gate_up, b_gate_up, w_down, b_down, final_g, out):
    _, T, D = x.shape
    TT, KT = T // P, D // P
    H = D // P
    IH = 8
    GH = 4
    DV = D // GH
    NCH = T // CHUNK
    RANK = w_gate_lr.shape[1]
    E = w_gate_up.shape[1]
    NA = w_ada.shape[2] // 512
    MAXB = E + T * TOP_K // SLOTS
    NP2 = 4
    assert TT == 2 and KT == 8 and D // GH // 2 == P and w_gate_lr.shape[2] == GH * P and E == 32

    sizes = dict(qa=D, ka=D, va=D, qi=IH * IDX_DIM, ki=IDX_DIM, wi=IH, qb=GH * P, kb=GH * P, vb=D, gb=D, lr=RANK, ga=D, gm=D)
    col, at = {}, 0
    for name, n in sizes.items():
        col[name] = at
        at += n

    def columns(w, a, n):
        return w[0, :, a:a + n].rearrange("(k p) n -> p k n", p=P)

    def piece_source(kind, i):
        w = {"ada": w_ada, "wa": w_branch_a, "wb": w_branch_b, "wo": w_out}.get(kind, w_in)
        return columns(w, col.get(kind, 0) + 512 * i, 512)

    with ExitStack() as ctx:
        KB = 1024
        base = 16512

        def sb(name, at_kb, shape, dt=F32):
            return nc.alloc_sbuf_tensor_at(name, shape, dt, offset=base + int(at_kb * KB))

        def sem(name):
            return ctx.enter_context(nc.semaphore(name))

        piece = [sb(f"piece{i}", 16 * i, [P, KT, 512]) for i in range(NP2)]
        gu_slot = [sb(f"gu_slot{j}", 8 * j, [P, 2048]) for j in range(8)]
        dn_slot = [sb(f"dn_slot{j}", 64 + 8 * j, [P, 2, D]) for j in range(4)]
        bgu_row = sb("bgu_row", 96, [1, 2 * D])
        vb = sb("vb", 64, [P, TT, D])
        G = sb("G", 72, [P, GH * T])
        qe = sb("qe", 76, [P, GH, T])
        ke = sb("ke", 80, [P, GH, T])
        kd = sb("kd", 84, [P, GH, T])
        kdt = sb("kdt", 88, [P, TT, GH * P])
        S = [None, sb("S1", 72, [P, GH * DV]), sb("S2", 84, [P, GH * DV]), sb("S3", 92, [P, GH * DV])]
        z = sb("z", 84, [P, GH * T])
        softp = sb("softp", 88, [P, GH * T])
        reset = sb("reset", 92, [P, GH * T])
        AT = sb("AT", 96, [P, 512])
        qiT = sb("qiT", 98, [P, IH // 2, T])
        kiT = sb("kiT", 102, [P, T])
        xs = sb("xs", 104, [P, TT, D])
        hT = sb("hT", 112, [P, KT, T])
        h2 = sb("h2", 112, [P, TT, D])
        modp = [sb(f"modp{i}", 120 + 2 * i, [P, 512]) for i in range(4)]
        qaT = sb("qaT", 120, [P, H, T])
        gaT = sb("gaT", 120, [P, KT, T])
        junk = sb("junk", 120, [P, D])
        kaT = sb("kaT", 128, [P, H, T])
        gmT = sb("gmT", 128, [P, KT, T])
        va = sb("va", 136, [P, TT, D])
        mergedT = sb("mergedT", 136, [P, KT, T])
        yb = sb("yb", 144, [P, TT, D])
        xn = sb("xn", 152, [P, TT, D])
        rel = [sb(f"rel{i}", 152 + 2 * i, [P, 512]) for i in range(2)]
        ojunk = sb("ojunk", 166, [P, DV])
        yaT = sb("yaT", 152, [P, H, T])
        ybT = sb("ybT", 160, [P, KT, T])
        h2T = sb("h2T", 160, [P, KT, T])
        wgl = sb("wgl", 160, [RANK, GH * P])
        wsm = sb("wsm", 162, [P, KT, IDX_DIM + IH + RANK])
        lrT = sb("lrT", 165, [RANK, T])
        prob = [sb(f"prob{i}", 168 + 2 * i, [P, 512]) for i in range(4)]
        probT = [sb(f"probT{i}", 176 + 2 * i, [P, 512]) for i in range(4)]
        gt1 = sb("gt1", 168, [P, D])
        sc2g = sb("sc2g", 172, [P, D])
        sh2 = sb("sh2", 176, [P, D])
        gt2 = sb("gt2", 180, [P, D])
        score = [sb("score0", 184, [P, P]), sb("score1", 184.5, [P, T])]
        work = [[sb("work00", 185.5, [P, P]), sb("work01", 186, [P, P])],
                [sb("work10", 186.5, [P, T]), sb("work11", 187.5, [P, T])]]
        keep = [sb("keep0", 188.5, [P, P]), sb("keep1", 189, [P, T])]
        modq = [sb(f"modq{i}", 184 + 2 * i, [P, 512]) for i in range(2)]
        tmp = sb("tmp", 184, [P, 512])
        fgb = sb("fgb", 190, [P, D])
        ident = sb("ident", 194, [P, P])
        ones = sb("ones", 194.5, [P, P])
        inv32 = sb("inv32", 195, [P, P])
        before = sb("before", 195.5, [P, P])
        silc = sb("silc", 196, [P, KT, 32])
        pick = sb("pick", 197, [NA, NA, 32])
        bada = sb("bada", 198.5, [NA, 512])
        iota = sb("iota", 200.5, [P, SLOTS])
        gng = sb("gng", 200.75, [P, DV])
        wr = sb("wr", 201.75, [P, KT, E])
        rb = sb("rb", 202.75, [1, E])
        m_at = [203.0]

        def small(name, shape, dt=F32):
            n = 1
            for s in shape[1:]:
                n *= s
            t = sb(name, m_at[0], shape, dt)
            m_at[0] += (n * 4 + 31) // 32 * 32 / KB
            assert base + m_at[0] * KB <= 229368
            return t

        ccol = small("ccol", [P, KT])
        csig = small("csig", [P, KT])
        g1 = small("g1", [P, KT])
        gain1 = small("gain1", [P, KT])
        shift1 = small("shift1", [P, KT])
        wis = small("wis", [P, TT, IH])
        bg = small("bg", [P, GH])
        gsum = small("gsum", [P, GH, NCH])
        decay = small("decay", [P, GH, NCH])
        top8 = [small(f"top8_{i}", [P, 8]) for i in range(2)]
        mx = small("mx", [P, 24])
        nmx = small("nmx", [P, 24])
        esum = small("esum", [P, 24])
        erec = small("erec", [P, 24])
        sq = small("sq", [P, 8])
        sqe = small("sqe", [P, 8])
        root = small("root", [P, 8])
        rs = small("rs", [P, 8])
        rt_a = small("rt_a", [P, 8])
        rt_b = small("rt_b", [P, 8])
        lg = sb("lg", 152, [P, TT, E + TOP_K])
        lgw = sb("lgw", 152.5, [P, TT, E + TOP_K])
        r8 = sb("r8", 153, [P, TT, 8])
        nr8 = sb("nr8", 153.25, [P, TT])
        chosen = sb("chosen", 153.5, [P, TT, E])
        eexp = sb("eexp", 153.75, [P, TT, E])
        wts = sb("wts", 154, [P, TT, E])
        slot_id = sb("slot_id", 154.25, [P, TT, E])
        blocks = sb("blocks", 154.5, [P, E])
        blk_t = sb("blk_t", 154.75, [P, E])
        cum = sb("cum", 155, [P, E])
        cumx = sb("cumx", 155.25, [P, E])
        le = sb("le", 155.5, [1, MAXB + 1, E])
        wT = sb("wT", 145, [E, T])
        bdn = sb("bdn", 146, [E, D])
        eof = small("eof", [1, MAXB + 1])
        need_w = small("need_w", [1, MAXB + 1])
        table_e = small("table_e", [1, MAXB + 1], I32)
        table_w = small("table_w", [1, MAXB + 1], I32)
        table_used = small("table_used", [1, E], I32)
        table_n = small("table_n", [1, 1], I32)
        primer = small("primer", [P, 14])
        usedf = small("usedf", [1, E])
        acc = sb("acc", 120, [P, TT, D])
        xg = sb("xg", 128, [P, KT, SLOTS])
        gcl = sb("gcl", 130, [P, 512])
        sig = sb("sig", 132, [P, 512])
        ucl = sb("ucl", 134, [P, 512])
        act_t = sb("act_t", 136, [P, 512])
        actT = sb("actT", 138, [P, 4, P])
        ysb = sb("ysb", 140, [P, 512])
        sel = sb("sel", 142, [P, TT, SLOTS])
        selw = sb("selw", 142.5, [P, TT, 2, SLOTS])
        selwT = sb("selwT", 143.5, [P, T])
        final = sb("final", 0, [P, TT, D])
        junk2 = sb("junk2", 160, [P, D])

        bank = [ctx.enter_context(nc.psum_tensor(f"bank{i}", [P, 512], F32)) for i in range(8)]

        tile_full = sem("tile_full")
        out_act = sem("out_act")
        out_dve = sem("out_dve")
        piece_in = [sem(f"piece_in{i}") for i in range(NP2)]
        x_in, c_in, g1_in, bada_in, wsm_in, wgl_in, misc_in, late_in = (
            sem(n) for n in ("x_in", "c_in", "g1_in", "bada_in", "wsm_in", "wgl_in", "misc_in", "late_in"))
        g2_in, fg_in, bdn_in = sem("g2_in"), sem("fg_in"), sem("bdn_in")
        pool_step, dve_step, act_step = sem("pool_step"), sem("dve_step"), sem("act_step")
        consts_ready, pick_ready = sem("consts_ready"), sem("pick_ready")
        csig_ready, silc_ready, xss_ready, xvar_ready, xroot_ready, xn_ready = (
            sem(n) for n in ("csig_ready", "silc_ready", "xss_ready", "xvar_ready", "xroot_ready", "xn_ready"))
        softp_ready, gsum_ready, gexp_ready, gdiff_ready, gdec_ready, kd_ready = (
            sem(n) for n in ("softp_ready", "gsum_ready", "gexp_ready", "gdiff_ready", "gdec_ready", "kd_ready"))
        rel_used, at_masked, s_ready = sem("rel_used"), sem("at_masked"), sem("s_ready")
        nmx_ready, exp_ready, prob_ready, gsig_ready = sem("nmx_ready"), sem("exp_ready"), sem("prob_ready"), sem("gsig_ready")
        oss_ready, ovar_ready, oroot_ready, yb_ready = (sem(n) for n in ("oss_ready", "ovar_ready", "oroot_ready", "yb_ready"))
        merged_ready, x2_ready, x2ss_ready, x2var_ready, x2root_ready, h2_ready = (
            sem(n) for n in ("merged_ready", "x2_ready", "x2ss_ready", "x2var_ready", "x2root_ready", "h2_ready"))
        rneg_ready, rexp_ready, chosen_ready, wts_ready, tables_ready = (
            sem(n) for n in ("rneg_ready", "rexp_ready", "chosen_ready", "wts_ready", "tables_ready"))
        gu_in = [sem(f"gu_in{j}") for j in range(8)]
        dn_in = [sem(f"dn_in{j}") for j in range(4)]
        bgu_in = sem("bgu_in")
        gu_used = [sem(f"gu_used{j}") for j in range(8)]
        dn_used = [sem(f"dn_used{j}") for j in range(4)]
        bgu_used = sem("bgu_used")
        sel_ready, gath_full, xg_out, selw_out = (sem(n) for n in ("sel_ready", "gath_full", "xg_out", "selw_out"))
        gu_full, gcl_ready, ucl_ready, sig_ready, gs_ready, act_ready = (
            sem(n) for n in ("gu_full", "gcl_ready", "ucl_ready", "sig_ready", "gs_ready", "act_ready"))
        actT_full, actT_out, y_full, y_out, sc_full, acc_out = (
            sem(n) for n in ("actT_full", "actT_out", "y_full", "y_out", "sc_full", "acc_out"))
        iota_ready, add_done = sem("iota_ready"), sem("add_done")
        fss_ready, fvar_ready, froot_ready, fin_ready, stored = (
            sem(n) for n in ("fss_ready", "fvar_ready", "froot_ready", "fin_ready", "stored"))

        def tile(name):
            return bank[NUMBER[name] % 8]

        def wait_tile(eng, name):
            eng.wait_ge(tile_full, NUMBER[name] + 1)

        def wait_out(eng, name):
            eng.wait_ge(out_act if TAKER[name] == "A" else out_dve, OUT_COUNT[name])

        class Steps:

            def __init__(self, eng, own):
                self.eng, self.own, self.count, self.last = eng, own, {}, None

            def __call__(self, ins, signal=None):
                signal = signal or self.own
                ins.then_inc(signal, 1)
                self.count[signal.name] = self.count.get(signal.name, 0) + 1
                self.last = (signal, self.count[signal.name])

            def settle(self):
                self.eng.wait_ge(*self.last)

        block = ctx.enter_context(nc.Block())

        @block.sync
        def _(sp):
            def load_expert_piece(e, j):
                if j < 8:
                    sp.dma_start(gu_slot[j][:], w_gate_up[0, e, j * P:(j + 1) * P, :] if isinstance(e, int) else
                                 w_gate_up[0, ds(e, 1), j * P:(j + 1) * P, :].rearrange("a p n -> p (a n)")).then_inc(gu_in[j], 16)
                elif j < 12:
                    i = j - 8
                    rows = slice(2 * i * P, 2 * (i + 1) * P)
                    sp.dma_start(dn_slot[i][:], w_down[0, e, rows, :].rearrange("(i p) n -> p i n", p=P) if isinstance(e, int) else
                                 w_down[0, ds(e, 1), rows, :].rearrange("a (i p) n -> p (a i) n", p=P)).then_inc(dn_in[i], 16)
                else:
                    sp.dma_start(bgu_row[:], b_gate_up[0, e:e + 1, :] if isinstance(e, int) else
                                 b_gate_up[0, ds(e, 1), :]).then_inc(bgu_in, 16)

            for n, (kind, i, last) in enumerate(PIECES):
                if n >= NP2:
                    wait_tile(sp, PIECES[n - NP2][2])
                sp.dma_start(piece[n % NP2][:], piece_source(kind, i)).then_inc(piece_in[n % NP2], 16)
                if n == PIECE_NO["ada", 9]:
                    wait_tile(sp, "o3")
                    for j in (12, 8, 9, 10, 11):
                        load_expert_piece(0, j)
            for j in range(8):
                user = [last for n, (_, _, last) in enumerate(PIECES) if n % NP2 == j // 2][-1]
                wait_tile(sp, user)
                load_expert_piece(0, j)
            sp.wait_ge(tables_ready, 1)
            with sp.Fori(1, E) as e:
                free = sp.value_load(table_used[0:1, ds(e, 1)], min_val=1, max_val=MAXB + 1)
                for j in (12, 0, 1, 2, 3, 4, 5, 6, 7, 8, 9, 10, 11):
                    here, used = ((gu_in[j], gu_used[j]) if j < 8 else (dn_in[j - 8], dn_used[j - 8]) if j < 12 else
                                  (bgu_in, bgu_used))
                    sp.wait_ge(here, 16 * e)
                    sp.wait_ge(used, free)
                    load_expert_piece(e, j)
            sp.wait_ge(fin_ready, TT)
            sp.dma_start(out[0].rearrange("(t p) n -> p t n", p=P), final[:]).then_inc(stored, 16)
            sp.wait_ge(stored, 16)

        @block.gpsimd
        def _(pool):
            step = Steps(pool, pool_step)
            step(nc.gpsimd.memset(ident[:], 0.0))
            step(nc.gpsimd.memset(ones[:], 1.0))
            step(nc.gpsimd.memset(inv32[:], 1.0 / 32))
            step(nc.gpsimd.memset(pick[:], 0.0))
            step(nc.gpsimd.iota(iota[:], [[1, SLOTS]], base=0, channel_multiplier=0, allow_small_or_imprecise_dtypes=True))
            step.settle()
            step(nc.gpsimd.affine_select(out=ident[:], in_=ident[:], compare_op=ALU.not_equal, fill=1.0, base=0,
                                         pattern=[[-1, P]], channel_multiplier=1))
            step(nc.gpsimd.affine_select(out=pick[:], in_=pick[:], compare_op=ALU.not_equal, fill=1.0, base=0,
                                         pattern=[[-1, NA], [0, 32]], channel_multiplier=1))
            step(nc.gpsimd.affine_select(out=before[:], in_=ones[:], compare_op=ALU.is_gt, fill=0.0, base=0,
                                         pattern=[[1, P]], channel_multiplier=-1))
            step(nc.gpsimd.memset(reset[:], 1.0))
            step.settle()
            step(nc.gpsimd.memset(reset[:].rearrange("p (c i) -> p c i", i=CHUNK)[:, :, 0:1], 0.0), consts_ready)
            wait_out(pool, "AT")
            for half in range(2):
                v = AT[64 * half:64 * half + 64, :].rearrange("p (c i) -> p c i", i=CHUNK)
                step(nc.gpsimd.affine_select(out=v, in_=v, compare_op=ALU.is_ge, fill=0.0, base=0,
                                             pattern=[[0, 2 * GH], [1, CHUNK]], channel_multiplier=-1), at_masked)
            wait_tile(pool, "ya3")
            pool.dma_start(sc2g[:], norm2_g[0:1, :].to_broadcast([P, D])).then_inc(g2_in, 16)
            wait_tile(pool, "yT3")
            pool.dma_start(bdn[:], b_down[0]).then_inc(bdn_in, 16)

        @block.scalar
        def _(act):
            step = Steps(act, act_step)
            A = nc.scalar.activation

            act.dma_start(ccol[:], c[0].rearrange("(k p) -> p k", p=P), allow_slow_non_contiguous=True).then_inc(c_in, 16)
            act.dma_start(bada[:], b_ada[0].rearrange("(a n) -> a n", n=512)).then_inc(bada_in, 16)
            act.dma_start(xs[:], x[0].rearrange("(t p) n -> p t n", p=P)).then_inc(x_in, 16)
            act.dma_start(g1[:], norm1_g[0].rearrange("(k p) -> p k", p=P), allow_slow_non_contiguous=True).then_inc(g1_in, 16)
            act.dma_start(wsm[:, :, 0:IDX_DIM + IH], columns(w_in, col["ki"], IDX_DIM + IH)).then_inc(wsm_in, 16)
            act.dma_start(wsm[:, :, IDX_DIM + IH:], columns(w_in, col["lr"], RANK)).then_inc(wsm_in, 16)
            act.dma_start(wgl[:], w_gate_lr[0]).then_inc(wgl_in, 16)
            act.dma_start(bg[:], b_gate[0].rearrange("(h p) -> p h", p=P), allow_slow_non_contiguous=True).then_inc(misc_in, 16)
            act.dma_start(gng[:], gla_norm_g[0:1, :].to_broadcast([P, DV])).then_inc(late_in, 16)
            act.dma_start(wr[:], router_w[0].rearrange("(k p) n -> p k n", p=P)).then_inc(late_in, 16)
            act.dma_start(rb[:], router_b[0:1, :]).then_inc(late_in, 16)
            act.dma_start(fgb[:], final_g.rearrange("(a n) -> a n", a=1).to_broadcast([P, D])).then_inc(fg_in, 16)

            def take(name, *ops):
                wait_tile(act, name)
                for n, (o, i, f, kw) in enumerate(ops):
                    ins = A(o, i, f, **kw)
                    if n == len(ops) - 1:
                        step(ins, out_act)
                    else:
                        step(ins)

            act.wait_ge(c_in, 16)
            step(A(csig[:], ccol[:], ACT.Sigmoid), csig_ready)
            act.wait_ge(x_in, 16)
            for t in range(TT):
                step(A(xn[:, t, :], xs[:, t, :], ACT.Square, accum_out=sq[:, t:t + 1]), xss_ready)
            act.wait_ge(xvar_ready, 1)
            step(A(root[:, 0:TT], sqe[:, 0:TT], ACT.Sqrt), xroot_ready)

            for i in range(4):
                take(f"ada{i}", (modp[i][:], tile(f"ada{i}")[:], ACT.Copy, {}))
            take("small", (kiT[:], tile("small")[:, 0:T], ACT.Copy, {}),
                 (lrT[:], tile("small")[0:RANK, T:2 * T], ACT.Copy, {}))
            take("wi", (wis[:].rearrange("p t h -> p (t h)"), tile("wi")[:, 0:TT * IH], ACT.Copy, dict(scale=float(IH) ** -0.5)))
            for i in range(2):
                take(f"qi{i}", (qiT[:, 2 * i:2 * i + 2, :].rearrange("p a b -> p (a b)"), tile(f"qi{i}")[:], ACT.Copy,
                                dict(scale=IDX_DIM ** -0.5)))
            act.wait_ge(misc_in, 16)
            for i in range(2):
                take(f"z{i}", *[(z[:, (2 * i + j) * T:(2 * i + j + 1) * T], tile(f"z{i}")[:, j * T:(j + 1) * T], ACT.Identity,
                                 dict(bias=bg[:, 2 * i + j:2 * i + j + 1])) for j in range(2)])
            step.settle()
            step(A(softp[:], z[:], ACT.Abs))
            step.settle()
            step(A(softp[:], softp[:], ACT.Exp, scale=-1.0))
            step.settle()
            step(A(softp[:], softp[:], ACT.Ln, bias=1.0), softp_ready)

            def take_qk(dst, kind, i):
                take(f"{kind}{i}", (dst[:, 2 * i:2 * i + 2, :].rearrange("p a b -> p (a b)"), tile(f"{kind}{i}")[:], ACT.Copy, {}))

            def take_rows(dst, kind, i):
                cc, t = divmod(i, TT)
                take(f"{kind}{i}", (dst[:, t, 512 * cc:512 * cc + 512], tile(f"{kind}{i}")[:], ACT.Copy, {}))

            take_qk(qaT, "qa", 0)
            take_qk(qaT, "qa", 1)
            for n, name in enumerate(["sx0", "sx1", "sy0", "sy1", "sy2", "sy3"]):
                if n >= 2:
                    act.wait_ge(rel_used, n - 1)
                take(name, (rel[n % 2][:], tile(name)[:], ACT.Relu, {}))
            take_qk(qaT, "qa", 2)
            take_qk(qaT, "qa", 3)
            act.wait_ge(gsum_ready, 1)
            step(A(qe[:].rearrange("p h t -> p (h t)"), G[:], ACT.Exp, scale=1.0 / GATE_TAU))
            step(A(ke[:].rearrange("p h t -> p (h t)"), G[:], ACT.Exp, scale=-1.0 / GATE_TAU), gexp_ready)
            act.wait_ge(gdiff_ready, 1)
            step(A(softp[:], softp[:], ACT.Exp, scale=1.0 / GATE_TAU))
            step(A(decay[:].rearrange("p h n -> p (h n)"), gsum[:].rearrange("p h n -> p (h n)"), ACT.Exp,
                   scale=1.0 / GATE_TAU), gdec_ready)
            take_qk(kaT, "ka", 0)
            take_qk(kaT, "ka", 1)
            for t in range(TT):
                take(f"kdT{t}", (kdt[:, t, :], tile(f"kdT{t}")[:], ACT.Copy, {}))
            take("AT", (AT[:], tile("AT")[:], ACT.Copy, {}))
            take_qk(kaT, "ka", 2)
            take_qk(kaT, "ka", 3)
            for i in range(4):
                take_rows(vb, "vb", i)
            for i in range(4):
                take_rows(va, "va", i)

            def exps(g):
                n, w = (4, P) if g < 2 else (2, 2 * P)
                act.wait_ge(nmx_ready, g + 1)
                for j in range(n):
                    ins = A(prob[g % 4][:, j * w:(j + 1) * w], prob[g % 4][:, j * w:(j + 1) * w], ACT.Exp,
                            bias=nmx[:, 4 * g + j:4 * g + j + 1], accum_out=esum[:, 4 * g + j:4 * g + j + 1])
                    step(ins, exp_ready if j == n - 1 else None)

            def gate_sig(i):
                cc, t = divmod(i, TT)
                wait_tile(act, f"gb{i}")
                step(A(yb[:, t, 512 * cc:512 * cc + 512], tile(f"gb{i}")[:], ACT.Sigmoid), gsig_ready)

            def take_probT(g):
                if g >= 4:
                    wait_tile(act, f"ya{g - 4}")
                take(f"pt{g}", (probT[g % 4][:], tile(f"pt{g}")[:], ACT.Copy, {}))

            def take_ya(i):
                t, half = divmod(i, 2)
                take(f"ya{i}", (yaT[:, 4 * half:4 * half + 4, t * P:(t + 1) * P],
                                tile(f"ya{i}")[:].rearrange("p (h q) -> p h q", h=4), ACT.Copy, {}))

            exps(0)
            exps(1)
            gate_sig(0)
            gate_sig(1)
            take_probT(0)
            take_probT(1)
            exps(2)
            exps(3)
            take_ya(0)
            take_ya(1)
            exps(4)
            exps(5)
            gate_sig(2)
            gate_sig(3)
            for g in range(2, 6):
                take_probT(g)
            for i in range(4):
                wait_tile(act, f"o{i}")
                for j in range(2):
                    step(A(ojunk[:], tile(f"o{i}")[:, j * DV:(j + 1) * DV], ACT.Square,
                           accum_out=sq[:, 2 * i + j:2 * i + j + 1]), oss_ready)
                    step.settle()
            act.wait_ge(ovar_ready, 1)
            step(A(root[:], sqe[:], ACT.Sqrt), oroot_ready)
            take_ya(2)
            take_ya(3)

            def take_sig(dst, kind, i):
                take(f"{kind}{i}", (dst[:, 2 * i:2 * i + 2, :].rearrange("p a b -> p (a b)"), tile(f"{kind}{i}")[:], ACT.Sigmoid, {}))

            def take_T(dst, kind, i):
                t, half = divmod(i, 2)
                take(f"{kind}{i}", (dst[:, 4 * half:4 * half + 4, t * P:(t + 1) * P],
                                    tile(f"{kind}{i}")[:].rearrange("p (h q) -> p h q", h=4), ACT.Copy, {}))

            for i in range(4):
                take_sig(gaT, "ga", i)
            for i in range(4):
                take_T(ybT, "yT", i)
            for i in range(4):
                take_sig(gmT, "gm", i)
            for r in range(8):
                if r >= 2:
                    wait_tile(act, f"ab{r - 2}")
                take(f"ap{r}", (modq[r % 2][:], tile(f"ap{r}")[:], ACT.Copy, {}))
            act.wait_ge(x2_ready, 1)
            for t in range(TT):
                step(A(junk[:], xs[:, t, :], ACT.Square, accum_out=sq[:, t:t + 1]), x2ss_ready)
                step.settle()
            act.wait_ge(x2var_ready, 1)
            step(A(root[:, 0:TT], sqe[:, 0:TT], ACT.Sqrt), x2root_ready)
            for i in range(4):
                take_T(h2T, "hh", i)
            take("rl", (lg[:, :, 0:E], tile("rl")[:, 0:TT * E].rearrange("p (t e) -> p t e", e=E), ACT.Copy, {}))
            act.wait_ge(rneg_ready, 1)
            for t in range(TT):
                step(A(eexp[:, t, :], lg[:, t, 0:E], ACT.Exp, bias=nr8[:, t:t + 1]), rexp_ready)
            take("wT", (wT[:], tile("wT")[0:E, 0:T], ACT.Copy, {}))

            act.wait_ge(gath_full, 1)
            step(A(xg[:].rearrange("p k s -> p (k s)"), bank[2][:], ACT.Copy), xg_out)
            act.wait_ge(tables_ready, 1)
            nb = act.value_load(table_n[0:1, 0:1], min_val=1, max_val=MAXB)
            with act.Fori(0, nb) as g:
                g1_ = act.snap(g + 1)
                g2_ = act.snap(g + 2)
                act.wait_ge(acc_out, g1_)
                A(selwT[:], bank[3][:, 0:T], ACT.Copy).then_inc(selw_out, 1)
                act.wait_ge(gcl_ready, g1_)
                A(sig[:], gcl[:], ACT.Sigmoid, scale=ALPHA).then_inc(sig_ready, 1)
                act.wait_ge(gath_full, g2_)
                A(xg[:].rearrange("p k s -> p (k s)"), bank[2][:], ACT.Copy).then_inc(xg_out, 1)
                act.wait_ge(actT_full, g1_)
                A(actT[:].rearrange("p c s -> p (c s)"), bank[4][:], ACT.Copy).then_inc(actT_out, 1)
                act.wait_ge(y_full, g1_)
                A(ysb[:], bank[5][:], ACT.Copy).then_inc(y_out, 1)
            act.wait_ge(add_done, 1)
            for t in range(TT):
                step(A(junk2[:], xs[:, t, :], ACT.Square, accum_out=sq[:, t:t + 1]), fss_ready)
                step.settle()
            act.wait_ge(fvar_ready, 1)
            step(A(root[:, 0:TT], sqe[:, 0:TT], ACT.Sqrt), froot_ready)

        @block.vector
        def _(dve):
            V = nc.vector
            step = Steps(dve, dve_step)

            def chain(ins, signal=None):
                step(ins, signal)
                step.settle()

            def inverse_root(n, count, seen, var_ready, root_ready):
                dve.wait_ge(*seen)
                chain(V.tensor_scalar(sqe[:, 0:n], sq[:, 0:n], 1.0 / count, EPS, ALU.mult, ALU.add), var_ready)
                dve.wait_ge(root_ready, 1)
                chain(V.reciprocal(rt_a[:, 0:n], root[:, 0:n]))
                chain(V.tensor_tensor(rt_b[:, 0:n], rt_a[:, 0:n], rt_a[:, 0:n], ALU.mult))
                chain(V.tensor_tensor(rt_b[:, 0:n], rt_b[:, 0:n], sqe[:, 0:n], ALU.mult))
                chain(V.tensor_scalar(rt_b[:, 0:n], rt_b[:, 0:n], -0.5, 1.5, ALU.mult, ALU.add))
                chain(V.tensor_tensor(rs[:, 0:n], rt_a[:, 0:n], rt_b[:, 0:n], ALU.mult))

            dve.wait_ge(csig_ready, 1)
            chain(V.tensor_tensor(csig[:], csig[:], ccol[:], ALU.mult))
            step(V.tensor_copy(silc[:], csig[:].unsqueeze(2).to_broadcast([P, KT, 32])), silc_ready)
            inverse_root(TT, D, (xss_ready, TT), xvar_ready, xroot_ready)
            for t in range(TT):
                step(V.tensor_scalar(xn[:, t, :], xs[:, t, :], rs[:, t:t + 1], None, ALU.mult), xn_ready)
            wait_tile(dve, "cols")
            dve.wait_ge(g1_in, 16)
            step(V.tensor_copy(shift1[:], tile("cols")[:, 0:KT]))
            chain(V.scalar_tensor_tensor(gain1[:], tile("cols")[:, KT:2 * KT], 1.0, g1[:], ALU.add, ALU.mult), out_dve)
            for i in range(4):
                t, half = divmod(i, 2)
                wait_tile(dve, f"xT{i}")
                for j in range(4):
                    k = 4 * half + j
                    step(V.tensor_scalar(hT[:, k, t * P:(t + 1) * P], tile(f"xT{i}")[:, j * P:(j + 1) * P],
                                         gain1[:, k:k + 1], shift1[:, k:k + 1], ALU.mult, ALU.add), out_dve if j == 3 else None)
            dve.wait_ge(softp_ready, 1)
            dve.wait_ge(consts_ready, 1)
            chain(V.scalar_tensor_tensor(z[:], z[:], 0.0, softp[:], ALU.min, ALU.subtract))
            chain(V.tensor_tensor_scan(G[:], reset[:], z[:], 0.0, ALU.mult, ALU.add))
            Gc = G[:].rearrange("p (c i) -> p c i", i=CHUNK)
            chain(V.tensor_copy(gsum[:].rearrange("p h n -> p (h n)").unsqueeze(2), Gc[:, :, CHUNK - 1:CHUNK]), gsum_ready)
            step(V.tensor_tensor(softp[:].rearrange("p (c i) -> p c i", i=CHUNK),
                                 gsum[:].rearrange("p h n -> p (h n)").unsqueeze(2).to_broadcast([P, GH * NCH, CHUNK]), Gc,
                                 ALU.subtract), gdiff_ready)

            plan = [("sx0", 0, (0, 2, 4, 6)), ("sx1", 0, (1, 3, 5, 7)),
                    ("sy0", 1, (0, 2)), ("sy1", 1, (1, 3)), ("sy2", 1, (4, 6)), ("sy3", 1, (5, 7))]
            fresh = {0: True, 1: True}
            for n, (name, t, heads) in enumerate(plan):
                w = P if t == 0 else T
                wait_out(dve, name)
                if n == 0:
                    wait_out(dve, "wi")
                for j, h in enumerate(heads):
                    src, wcol = rel[n % 2][:, j * w:(j + 1) * w], wis[:, t, h:h + 1]
                    sig_ = rel_used if j == len(heads) - 1 else None
                    if fresh[t]:
                        chain(V.tensor_scalar(score[t][:], src, wcol, None, ALU.mult), sig_)
                        fresh[t] = False
                    else:
                        chain(V.scalar_tensor_tensor(score[t][:], src, wcol, score[t][:], ALU.mult, ALU.add), sig_)
            for t in range(TT):
                first = 2 * t * CHUNK + CHUNK
                chain(V.memset(score[t][0:CHUNK, first:first + CHUNK], HIDDEN))
            for t in range(TT):
                src = score[t]
                for r in range(CHUNK // 8):
                    dst = work[t][r % 2]
                    chain(V.max(top8[r % 2][:], src[:]))
                    chain(V.match_replace(dst[:], top8[r % 2][:], src[:], TAKEN))
                    src = dst
                chain(V.tensor_scalar(keep[t][:], src[:], TAKEN, HIDDEN, ALU.not_equal, ALU.mult))

            dve.wait_ge(gexp_ready, 1)
            for i in range(2):
                wait_tile(dve, f"qb{i}")
                step(V.scalar_tensor_tensor(qe[:, 2 * i:2 * i + 2, :], tile(f"qb{i}")[:].rearrange("p (h t) -> p h t", h=2),
                                            float(P) ** -0.5, qe[:, 2 * i:2 * i + 2, :], ALU.mult, ALU.mult), out_dve)
            dve.wait_ge(gdec_ready, 1)
            for i in range(2):
                wait_tile(dve, f"kb{i}")
                step(V.tensor_tensor(kd[:, 2 * i:2 * i + 2, :], tile(f"kb{i}")[:].rearrange("p (h t) -> p h t", h=2),
                                     softp[:].rearrange("p (h t) -> p h t", h=GH)[:, 2 * i:2 * i + 2, :], ALU.mult), kd_ready)
                step(V.tensor_tensor(ke[:, 2 * i:2 * i + 2, :], tile(f"kb{i}")[:].rearrange("p (h t) -> p h t", h=2),
                                     ke[:, 2 * i:2 * i + 2, :], ALU.mult), out_dve)

            def state(n):
                for half, name in enumerate((f"s{n}a", f"s{n}b")):
                    wait_tile(dve, name)
                    for j in range(2):
                        h = 2 * half + j
                        src = tile(name)[:, j * DV:(j + 1) * DV]
                        dst = S[n][:, h * DV:(h + 1) * DV]
                        signal = out_dve if j == 1 else None
                        if n == 1:
                            step(V.tensor_copy(dst, src), signal)
                        else:
                            step(V.scalar_tensor_tensor(dst, S[n - 1][:, h * DV:(h + 1) * DV], decay[:, h, n - 1:n], src,
                                                        ALU.mult, ALU.add), signal)
                step.settle()

            state(1)
            state(2)
            state(3)

            def logits(g):
                if g < 2:
                    n, w, t = 4, P, 0
                else:
                    n, w, t = 2, T, 1
                if g >= 4:
                    wait_tile(dve, f"pt{g - 4}")
                wait_tile(dve, f"lg{g}")
                L = prob[g % 4][:].rearrange("p (h s) -> p h s", h=n)
                chain(V.scalar_tensor_tensor(L, tile(f"lg{g}")[:].rearrange("p (h s) -> p h s", h=n), float(P) ** -0.5,
                                             keep[t][:].unsqueeze(1).to_broadcast([P, n, w]), ALU.mult, ALU.add), out_dve)
                chain(V.tensor_reduce(mx[:, 4 * g:4 * g + n], L, AX.X, ALU.max))
                chain(V.tensor_scalar(nmx[:, 4 * g:4 * g + n], mx[:, 4 * g:4 * g + n], -1.0, None, ALU.mult), nmx_ready)

            def normalize(g):
                n, w = (4, P) if g < 2 else (2, T)
                dve.wait_ge(exp_ready, g + 1)
                chain(V.reciprocal(erec[:, 4 * g:4 * g + n], esum[:, 4 * g:4 * g + n]))
                for j in range(n):
                    step(V.tensor_scalar(prob[g % 4][:, j * w:(j + 1) * w], prob[g % 4][:, j * w:(j + 1) * w],
                                         erec[:, 4 * g + j:4 * g + j + 1], None, ALU.mult), prob_ready if j == n - 1 else None)

            def gate(i):
                cc, t = divmod(i, TT)
                dst = yb[:, t, 512 * cc:512 * cc + 512]
                dve.wait_ge(gsig_ready, i + 1)
                chain(V.tensor_tensor(dst, tile(f"gb{i}")[:], dst, ALU.mult), out_dve)
                dst = dst.rearrange("p (h v) -> p h v", h=2)
                step(V.tensor_tensor(dst, dst, gng[:].unsqueeze(1).to_broadcast([P, 2, DV]), ALU.mult))

            logits(0)
            logits(1)
            normalize(0)
            normalize(1)
            dve.wait_ge(late_in, 48)
            gate(0)
            gate(1)
            logits(2)
            logits(3)
            normalize(2)
            normalize(3)
            logits(4)
            logits(5)
            normalize(4)
            normalize(5)
            gate(2)
            gate(3)
            inverse_root(8, DV, (oss_ready, 8), ovar_ready, oroot_ready)
            for i in range(4):
                t, half = divmod(i, 2)
                for j in range(2):
                    h = 2 * half + j
                    dst = yb[:, t, h * DV:(h + 1) * DV]
                    step(V.scalar_tensor_tensor(dst, tile(f"o{i}")[:, j * DV:(j + 1) * DV], rs[:, 2 * i + j:2 * i + j + 1], dst,
                                                ALU.mult, ALU.mult), out_dve if j == 1 else None)
            for r in range(8):
                dst = (gt1, sh2, sc2g, gt2)[r // 2][:, 512 * (r % 2):512 * (r % 2) + 512]
                wait_tile(dve, f"ab{r}")
                if r == 4:
                    dve.wait_ge(g2_in, 16)
                if r // 2 == 2:
                    step(V.scalar_tensor_tensor(dst, tile(f"ab{r}")[:], 1.0, dst, ALU.add, ALU.mult), out_dve)
                else:
                    step(V.tensor_copy(dst, tile(f"ab{r}")[:]), out_dve)
            for i in range(4):
                wait_tile(dve, f"wa{i}")
                wait_out(dve, f"ga{i}")
                step(V.tensor_tensor(mergedT[:, 2 * i:2 * i + 2, :].rearrange("p a b -> p (a b)"), tile(f"wa{i}")[:],
                                     gaT[:, 2 * i:2 * i + 2, :].rearrange("p a b -> p (a b)"), ALU.mult), out_dve)
            for i in range(4):
                m = mergedT[:, 2 * i:2 * i + 2, :].rearrange("p a b -> p (a b)")
                wait_tile(dve, f"wb{i}")
                chain(V.tensor_tensor(tmp[:], tile(f"wb{i}")[:], gmT[:, 2 * i:2 * i + 2, :].rearrange("p a b -> p (a b)"),
                                      ALU.mult), out_dve)
                chain(V.tensor_tensor(m, m, tmp[:], ALU.add), merged_ready)
            for i in range(4):
                cc, t = divmod(i, TT)
                xv = xs[:, t, 512 * cc:512 * cc + 512]
                wait_tile(dve, f"wo{i}")
                chain(V.tensor_tensor(tmp[:], tile(f"wo{i}")[:], gt1[:, 512 * cc:512 * cc + 512], ALU.mult), out_dve)
                chain(V.tensor_tensor(xv, xv, tmp[:], ALU.add), x2_ready if i == 3 else None)
            inverse_root(TT, D, (x2ss_ready, TT), x2var_ready, x2root_ready)
            for t in range(TT):
                chain(V.scalar_tensor_tensor(h2[:, t, :], xs[:, t, :], rs[:, t:t + 1], sc2g[:], ALU.mult, ALU.mult))
                step(V.tensor_tensor(h2[:, t, :], h2[:, t, :], sh2[:], ALU.add), h2_ready)

            step(V.memset(lg[:, :, E:E + TOP_K], PAD))
            wait_out(dve, "rl")
            for t in range(TT):
                chain(V.max(r8[:, t, :], lg[:, t, 0:E]))
                step(V.tensor_scalar(nr8[:, t:t + 1], r8[:, t, 0:1], -1.0, None, ALU.mult), rneg_ready if t == 1 else None)
                chain(V.memset(r8[:, t, TOP_K:8], PAD))
                chain(V.match_replace(lgw[:, t, :], r8[:, t, :], lg[:, t, :], TAKEN))
                step(V.tensor_scalar(chosen[:, t, :], lgw[:, t, 0:E], TAKEN, None, ALU.is_equal), chosen_ready)
            for t in range(TT):
                dve.wait_ge(rexp_ready, t + 1)
                step.settle()
                chain(V.scalar_tensor_tensor(wts[:, t, :], eexp[:, t, :], 1.0, chosen[:, t, :], ALU.mult, ALU.mult,
                                             accum_out=rt_a[:, t:t + 1]))
                chain(V.reciprocal(rt_b[:, t:t + 1], rt_a[:, t:t + 1]))
                chain(V.tensor_scalar(wts[:, t, :], wts[:, t, :], rt_b[:, t:t + 1], None, ALU.mult), wts_ready)
            wait_tile(dve, "rt")
            counts = tile("rt")[:, TT * E:TT * E + E]
            chain(V.tensor_scalar(blocks[:], counts, 0.0, None, ALU.is_gt))
            for q in range(1, T // SLOTS):
                chain(V.tensor_scalar(blk_t[:], counts, float(q * SLOTS), None, ALU.is_gt))
                chain(V.tensor_tensor(blocks[:], blocks[:], blk_t[:], ALU.add))
            chain(V.tensor_tensor_scan(cum[:], ones[:, 0:E], blocks[:], 0.0, ALU.mult, ALU.add))
            chain(V.tensor_tensor(cumx[:], cum[:], blocks[:], ALU.subtract))
            for t in range(TT):
                chain(V.scalar_tensor_tensor(slot_id[:, t, :], cumx[:], float(SLOTS), tile("rt")[:, t * E:(t + 1) * E],
                                             ALU.mult, ALU.add), out_dve if t == 1 else None)
                chain(V.scalar_tensor_tensor(slot_id[:, t, :], slot_id[:, t, :], 1.0, chosen[:, t, :], ALU.add, ALU.mult))
                chain(V.tensor_scalar(slot_id[:, t, :], slot_id[:, t, :], -1.0, None, ALU.add))
            chain(V.tensor_tensor(le[:], cum[0:1, :].unsqueeze(1).to_broadcast([1, MAXB + 1, E]),
                                  iota[0:1, 0:MAXB + 1].unsqueeze(2).to_broadcast([1, MAXB + 1, E]), ALU.is_le))
            chain(V.tensor_reduce(eof[:], le[:], AX.X, ALU.add))
            chain(V.tensor_scalar(eof[:], eof[:], float(E - 1), None, ALU.min))
            chain(V.tensor_copy(table_e[:], eof[:]))
            chain(V.tensor_scalar(need_w[:], eof[:], 16.0, 16.0, ALU.mult, ALU.add))
            chain(V.tensor_copy(table_w[:], need_w[:]))
            chain(V.tensor_scalar(usedf[:], cumx[0:1, :], 1.0, None, ALU.add))
            chain(V.tensor_copy(table_used[:], usedf[:]))
            chain(V.tensor_copy(table_n[:], cum[0:1, E - 1:E]), tables_ready)
            for n, s_ in enumerate(gu_used + dn_used + [bgu_used]):
                step(V.memset(primer[:, n:n + 1], 0.0), s_)

            def select(e, signal):
                for t in range(TT):
                    V.tensor_scalar(sel[:, t, :], iota[:], slot_id[:, t, ds(e, 1)], None, ALU.is_equal)
                for t in range(TT):
                    ins = V.tensor_scalar(selw[:, t, :, :], iota[:].unsqueeze(1).to_broadcast([P, 2, SLOTS]),
                                          slot_id[:, t, ds(e, 1)], wts[:, t, ds(e, 1)], ALU.is_equal, ALU.mult)
                ins.then_inc(signal, 1)

            e0 = dve.value_load(table_e[0:1, 0:1], min_val=0, max_val=E - 1)
            select(e0, sel_ready)
            for i in range(4):
                cc, t = divmod(i, TT)
                wait_tile(dve, f"bd{i}")
                step(V.tensor_copy(acc[:, t, 512 * cc:512 * cc + 512], tile(f"bd{i}")[:]), out_dve)
            step(V.memset(primer[:, 13:14], 0.0), acc_out)
            nb = dve.value_load(table_n[0:1, 0:1], min_val=1, max_val=MAXB)
            with dve.Fori(0, nb) as g:
                g1_ = dve.snap(g + 1)
                e = dve.value_load(table_e[0:1, ds(g + 1, 1)], min_val=0, max_val=E - 1)
                dve.wait_ge(gath_full, g1_)
                V.tensor_scalar(iota[:], iota[:], float(SLOTS), None, ALU.add).then_inc(iota_ready, 1)
                dve.wait_ge(iota_ready, g1_)
                select(e, sel_ready)
                dve.wait_ge(gu_full, g1_)
                V.tensor_scalar(gcl[:], bank[0][:], LIMIT, None, ALU.min).then_inc(gcl_ready, 1)
                V.tensor_scalar(ucl[:], bank[1][:], LIMIT, -LIMIT, ALU.min, ALU.max).then_inc(ucl_ready, 1)
                dve.wait_ge(sig_ready, g1_)
                V.tensor_tensor(gcl[:], gcl[:], sig[:], ALU.mult).then_inc(gs_ready, 1)
                dve.wait_ge(gs_ready, g1_)
                V.scalar_tensor_tensor(act_t[:], ucl[:], 1.0, gcl[:], ALU.add, ALU.mult).then_inc(act_ready, 1)
                dve.wait_ge(sc_full, g1_)
                for t, half, b in ((0, 0, 6), (0, 1, 7), (1, 0, 4), (1, 1, 5)):
                    dst = acc[:, t, 512 * half:512 * half + 512]
                    ins = V.tensor_tensor(dst, dst, bank[b][:], ALU.add)
                ins.then_inc(acc_out, 1)
            dve.wait_ge(acc_out, dve.snap(nb + 1))
            for t in range(TT):
                chain(V.tensor_tensor(acc[:, t, :], acc[:, t, :], gt2[:], ALU.mult))
                chain(V.tensor_tensor(xs[:, t, :], xs[:, t, :], acc[:, t, :], ALU.add), add_done if t == 1 else None)
            inverse_root(TT, D, (fss_ready, TT), fvar_ready, froot_ready)
            dve.wait_ge(fg_in, 16)
            for j in range(4):
                dve.wait_ge(gu_in[j], 16 * E)
            for t in range(TT):
                step(V.scalar_tensor_tensor(final[:, t, :], xs[:, t, :], rs[:, t:t + 1], fgb[:], ALU.mult, ALU.mult), fin_ready)

        @block.tensor
        def _(pe):
            M = nc.tensor.matmul
            filled = [0]

            def begin(name):
                assert PLAN[filled[0]][0] == name, (PLAN[filled[0]][0], name)
                if filled[0] >= 8:
                    wait_out(pe, PLAN[filled[0] - 8][0])
                filled[0] += 1
                return tile(name)

            def full(ins):
                ins.then_inc(tile_full, 1)

            def arrived(kind, c):
                n = PIECE_NO[kind, c]
                pe.wait_ge(piece_in[n % NP2], 16 * (n // NP2 + 1))
                return piece[n % NP2]

            def modulation_part(name, a):
                w = arrived("ada", a)
                ps = begin(name)
                M(ps[0:32, :], pick[0:NA, a, :], bada[0:NA, :], start=True, stop=False)
                for r in range(2):
                    for q in range(4):
                        k = 4 * r + q
                        ins = M(ps[32 * q:32 * q + 32, :], silc[:, k, :], w[:, k, :], start=(r == 0 and q > 0), stop=(r == 1),
                                tile_position=(0, 32 * q))
                full(ins)

            def by_feature(kind, c, src):
                w = arrived(kind, c)
                for j in range(2):
                    ps = begin(f"{kind}{2 * c + j}")
                    for f in range(2):
                        for k in range(KT):
                            a = (2 * j + f) * P
                            ins = M(ps[:, f * T:(f + 1) * T], w[:, k, a:a + P], src[:, k, :], start=(k == 0), stop=(k == KT - 1))
                    full(ins)

            def by_token(kind, c, src):
                w = arrived(kind, c)
                for t in range(TT):
                    ps = begin(f"{kind}{2 * c + t}")
                    for k in range(KT):
                        ins = M(ps[:], src[:, k, t * P:(t + 1) * P], w[:, k, :], start=(k == 0), stop=(k == KT - 1))
                    full(ins)

            def transposes(name, src, t, half):
                ps = begin(name)
                for j in range(4):
                    a = (4 * half + j) * P
                    ins = nc.tensor.transpose(ps[:, j * P:(j + 1) * P], src[:, t, a:a + P], ident[:])
                full(ins)

            pe.wait_ge(consts_ready, 1)
            pe.wait_ge(bada_in, 16)
            pe.wait_ge(silc_ready, 1)
            for i in range(4):
                modulation_part(f"ada{i}", i)
            ps = begin("cols")
            for i in range(4):
                wait_out(pe, f"ada{i}")
                for f in range(4):
                    ins = M(ps[:, 4 * i + f:4 * i + f + 1], modp[i][:, f * P:(f + 1) * P], inv32[:, 0:1], start=True, stop=True)
            full(ins)
            for i in range(4):
                t, half = divmod(i, 2)
                pe.wait_ge(xn_ready, t + 1)
                transposes(f"xT{i}", xn, t, half)
            for i in range(4):
                wait_out(pe, f"xT{i}")
            pe.wait_ge(wsm_in, 32)
            ps = begin("small")
            for half in range(2):
                for k in range(KT):
                    M(ps[half * 64:half * 64 + 64, 0:T], wsm[:, k, 0:IDX_DIM], hT[:, k, :], start=(k == 0), stop=(k == KT - 1))
            for k in range(KT):
                ins = M(ps[0:RANK, T:2 * T], wsm[:, k, IDX_DIM + IH:], hT[:, k, :], start=(k == 0), stop=(k == KT - 1))
            full(ins)
            ps = begin("wi")
            for t in range(TT):
                for k in range(KT):
                    ins = M(ps[:, t * IH:(t + 1) * IH], hT[:, k, t * P:(t + 1) * P], wsm[:, k, IDX_DIM:IDX_DIM + IH],
                            start=(k == 0), stop=(k == KT - 1))
            full(ins)
            by_feature("qi", 0, hT)
            pe.wait_ge(wgl_in, 16)
            wait_out(pe, "small")
            for i in range(2):
                ps = begin(f"z{i}")
                for j in range(2):
                    h = 2 * i + j
                    ins = M(ps[:, j * T:(j + 1) * T], wgl[:, h * P:(h + 1) * P], lrT[:], start=True, stop=True)
                full(ins)
            by_feature("qa", 0, hT)
            wait_out(pe, "qi1")
            def index_products(t, names, heads):
                w = P if t == 0 else T
                banks_ = []
                for name in names:
                    banks_.append(begin(name))
                for j in range(len(heads[0])):
                    for b_ in range(2):
                        h = heads[b_][j]
                        r = 64 * (h % 2)
                        ins = M(banks_[b_][:, j * w:(j + 1) * w], qiT[r:r + 64, h // 2, t * P:(t + 1) * P], kiT[r:r + 64, 0:w],
                                start=True, stop=True)
                        if j == len(heads[0]) - 1:
                            full(ins)
            index_products(0, ("sx0", "sx1"), ((0, 2, 4, 6), (1, 3, 5, 7)))
            index_products(1, ("sy0", "sy1"), ((0, 2), (1, 3)))
            index_products(1, ("sy2", "sy3"), ((4, 6), (5, 7)))
            by_feature("qa", 1, hT)
            by_feature("qb", 0, hT)
            by_feature("kb", 0, hT)
            by_feature("ka", 0, hT)
            for t in range(TT):
                ps = begin(f"kdT{t}")
                pe.wait_ge(kd_ready, 2)
                for h in range(GH):
                    ins = nc.tensor.transpose(ps[:, h * P:(h + 1) * P], kd[:, h, t * P:(t + 1) * P], ident[:])
                full(ins)
            ps = begin("AT")
            wait_out(pe, "kb1")
            for n in range(NCH):
                r = 64 * (n % 2)
                for h in range(GH):
                    a = (h * 2 + n // 2) * CHUNK
                    ins = M(ps[r:r + 64, a:a + CHUNK], ke[:, h, n * CHUNK:(n + 1) * CHUNK], qe[:, h, n * CHUNK:(n + 1) * CHUNK],
                            start=True, stop=True)
            full(ins)
            by_feature("ka", 1, hT)
            by_token("vb", 0, hT)
            by_token("vb", 1, hT)

            def state_step(n):
                cn = n - 1
                r, t = 64 * (cn % 2), cn // 2
                for half, name in enumerate((f"s{n}a", f"s{n}b")):
                    ps = begin(name)
                    for j in range(2):
                        h = 2 * half + j
                        ins = M(ps[:, j * DV:(j + 1) * DV], kdt[r:r + 64, t, h * P:(h + 1) * P], vb[r:r + 64, t, h * DV:(h + 1) * DV],
                                start=True, stop=True)
                    full(ins)

            wait_out(pe, "vb3")
            state_step(1)
            by_token("va", 0, hT)
            state_step(2)
            by_token("va", 1, hT)
            state_step(3)

            def logit_products(g):
                ps = begin(f"lg{g}")
                if g < 2:
                    t, w, heads = 0, P, range(4 * g, 4 * g + 4)
                else:
                    t, w, heads = 1, T, range(2 * (g - 2), 2 * (g - 2) + 2)
                for j, h in enumerate(heads):
                    ins = M(ps[:, j * w:(j + 1) * w], qaT[:, h, t * P:(t + 1) * P], kaT[:, h, 0:w], start=True, stop=True)
                full(ins)

            def prob_transposes(g):
                ps = begin(f"pt{g}")
                pe.wait_ge(prob_ready, g + 1)
                for j in range(4):
                    ins = nc.tensor.transpose(ps[:, j * P:(j + 1) * P], prob[g % 4][:, j * P:(j + 1) * P], ident[:])
                full(ins)

            def attend(i):
                ps = begin(f"ya{i}")
                t, half = divmod(i, 2)
                if t == 0:
                    wait_out(pe, f"pt{i}")
                    for j in range(4):
                        h = 4 * half + j
                        ins = M(ps[:, j * P:(j + 1) * P], va[:, 0, h * P:(h + 1) * P], probT[i][:, j * P:(j + 1) * P],
                                start=True, stop=True)
                else:
                    wait_out(pe, f"pt{3 + 2 * half}")
                    for j in range(4):
                        h = 4 * half + j
                        g = 2 + h // 2
                        for s_ in range(TT):
                            a = ((h % 2) * 2 + s_) * P
                            ins = M(ps[:, j * P:(j + 1) * P], va[:, s_, h * P:(h + 1) * P], probT[g % 4][:, a:a + P],
                                    start=(s_ == 0), stop=(s_ == TT - 1))
                full(ins)

            wait_out(pe, "va3")
            logit_products(0)
            logit_products(1)
            by_token("gb", 0, hT)
            prob_transposes(0)
            prob_transposes(1)
            logit_products(2)
            logit_products(3)
            attend(0)
            attend(1)
            logit_products(4)
            logit_products(5)
            by_token("gb", 1, hT)
            for g in range(2, 6):
                prob_transposes(g)
            pe.wait_ge(at_masked, 2)
            wait_out(pe, "s3b")
            for i in range(4):
                t, half = divmod(i, 2)
                ps = begin(f"o{i}")
                for n in (2 * t, 2 * t + 1):
                    r = 64 * (n % 2)
                    for j in range(2):
                        h = 2 * half + j
                        o_ = ps[r:r + 64, j * DV:(j + 1) * DV]
                        a = (h * 2 + n // 2) * CHUNK
                        ins = M(o_, AT[r:r + 64, a:a + CHUNK], vb[r:r + 64, t, h * DV:(h + 1) * DV], start=True, stop=(n == 0))
                        if n > 0:
                            ins = M(o_, qe[:, h, n * CHUNK:(n + 1) * CHUNK], S[n][:, h * DV:(h + 1) * DV], start=False, stop=True)
                full(ins)
            attend(2)
            attend(3)
            for cc in range(2):
                by_feature("ga", cc, hT)
            for i in range(4):
                t, half = divmod(i, 2)
                wait_out(pe, f"o{2 * t + 1}")
                transposes(f"yT{i}", yb, t, half)
            for cc in range(2):
                by_feature("gm", cc, hT)
            for r in range(8):
                modulation_part(f"ap{r}", 4 + r)
                ps = begin(f"ab{r}")
                wait_out(pe, f"ap{r}")
                full(M(ps[:], inv32[:], modq[r % 2][:], start=True, stop=True))
            for cc in range(2):
                by_feature("wa", cc, yaT)
            for cc in range(2):
                by_feature("wb", cc, ybT)
            pe.wait_ge(merged_ready, 4)
            for cc in range(2):
                by_token("wo", cc, mergedT)
            for i in range(4):
                t, half = divmod(i, 2)
                pe.wait_ge(h2_ready, t + 1)
                transposes(f"hh{i}", h2, t, half)
            ps = begin("rl")
            wait_out(pe, "hh3")
            pe.wait_ge(late_in, 48)
            for t in range(TT):
                for k in range(KT):
                    M(ps[:, t * E:(t + 1) * E], h2T[:, k, t * P:(t + 1) * P], wr[:, k, :], start=(k == 0), stop=False)
                ins = M(ps[:, t * E:(t + 1) * E], ones[0:1, :], rb[:], start=False, stop=True)
            full(ins)
            ps = begin("rt")
            pe.wait_ge(chosen_ready, TT)
            M(ps[:, 0:E], before[:], chosen[:, 0, :], start=True, stop=True)
            M(ps[:, E:2 * E], ones[:], chosen[:, 0, :], start=True, stop=False)
            M(ps[:, E:2 * E], before[:], chosen[:, 1, :], start=False, stop=True)
            M(ps[:, 2 * E:3 * E], ones[:], chosen[:, 0, :], start=True, stop=False)
            full(M(ps[:, 2 * E:3 * E], ones[:], chosen[:, 1, :], start=False, stop=True))
            ps = begin("wT")
            pe.wait_ge(wts_ready, TT)
            for t in range(TT):
                ins = nc.tensor.transpose(ps[0:E, t * P:(t + 1) * P], wts[:, t, :], ident[:])
            full(ins)
            pe.wait_ge(bdn_in, 16)
            for i in range(4):
                cc, t = divmod(i, TT)
                ps = begin(f"bd{i}")
                wait_out(pe, "wT")
                full(M(ps[:], wT[:, t * P:(t + 1) * P], bdn[:, 512 * cc:512 * cc + 512], start=True, stop=True))
            for name in ("wT", "bd3"):
                wait_out(pe, name)

            def gather(signal, also=None):
                for k in range(KT):
                    for t in range(TT):
                        ins = M(bank[2][:, k * SLOTS:(k + 1) * SLOTS], h2[:, t, k * P:(k + 1) * P], sel[:, t, :],
                                start=(t == 0), stop=(t == TT - 1))
                        if also is not None and k == 0 and t == 0:
                            ins.then_inc(also, 1)
                for t in range(TT):
                    ins = nc.tensor.transpose(bank[3][:, t * P:(t + 1) * P], selw[:, t, :, :].rearrange("p a s -> p (a s)"), ident[:])
                ins.then_inc(signal, 1)

            pe.wait_ge(sel_ready, 1)
            gather(gath_full)
            pe.wait_ge(tables_ready, 1)
            nb = pe.value_load(table_n[0:1, 0:1], min_val=1, max_val=MAXB)
            with pe.Fori(0, nb) as g:
                g1_ = pe.snap(g + 1)
                g2_ = pe.snap(g + 2)
                landed = pe.value_load(table_w[0:1, ds(g, 1)], min_val=16, max_val=16 * E)
                places = [(bank[i // 2][64 * (i % 2):64 * (i % 2) + 64, :], 512 * i) for i in range(4)]
                pe.wait_ge(bgu_in, landed)
                pe.wait_ge(xg_out, g1_)
                for o_, a in places:
                    ins = M(o_, ones[0:1, 0:SLOTS], bgu_row[0:1, a:a + 512], start=True, stop=False)
                ins.then_inc(bgu_used, 1)
                for k in range(KT):
                    pe.wait_ge(gu_in[k], landed)
                    for o_, a in places:
                        ins = M(o_, xg[:, k, :], gu_slot[k][:, a:a + 512], start=False, stop=(k == KT - 1))
                    ins.then_inc(gu_used[k] if k < KT - 1 else gu_full, 1)
                pe.wait_ge(sel_ready, g2_)
                pe.wait_ge(selw_out, g1_)
                gather(gath_full, gu_used[KT - 1])
                pe.wait_ge(acc_out, g1_)
                pe.wait_ge(act_ready, g1_)
                for q in range(4):
                    ins = nc.tensor.transpose(bank[4][:, q * P:(q + 1) * P], act_t[:, q * P:(q + 1) * P], ident[:])
                ins.then_inc(actT_full, 1)
                pe.wait_ge(actT_out, g1_)
                for f in range(KT):
                    if f % 2 == 0:
                        pe.wait_ge(dn_in[f // 2], landed)
                    s_ = 64 * (f // 4)
                    for half in range(2):
                        ins = M(bank[5][64 * half:64 * half + 64, :], actT[:, f % 4, s_:s_ + 64],
                                dn_slot[f // 2][:, f % 2, 512 * half:512 * half + 512], start=(f == 0), stop=(f == KT - 1))
                    if f % 2 == 1:
                        ins.then_inc(dn_used[f // 2] if f < KT - 1 else y_full, 1)
                pe.wait_ge(y_out, g1_)
                for t, half, b in ((0, 0, 6), (0, 1, 7), (1, 0, 4), (1, 1, 5)):
                    r = 64 * half
                    ins = M(bank[b][:], selwT[r:r + 64, t * P:(t + 1) * P], ysb[r:r + 64, :], start=True, stop=True)
                    if b == 6:
                        ins.then_inc(dn_used[3], 1)
                ins.then_inc(sc_full, 1)


_INS = ['x', 'c', 'w_ada', 'b_ada', 'norm1_g', 'w_in', 'w_gate_lr', 'b_gate', 'gla_norm_g', 'w_branch_a', 'w_branch_b',
        'w_out', 'norm2_g', 'router_w', 'router_b', 'w_gate_up', 'b_gate_up', 'w_down', 'b_down', 'final_g']


def kernel(**inputs):
    import numpy as np
    import concourse.bacc as bacc
    from concourse.bass_utils import run_bass_kernel_spmd

    nc = bacc.Bacc("TRN2", target_bir_lowering=False, num_devices=1)
    arrays, args = {}, []
    for name in _INS:
        a = np.ascontiguousarray(inputs[name])
        arrays[f"in_{name}"] = a
        args.append(nc.dram_tensor(f"in_{name}", a.shape, mybir.dt.from_np(a.dtype), kind="ExternalInput").ap())
    out = nc.dram_tensor("out_0", inputs['x'].shape, F32, kind="ExternalOutput").ap()
    hybrid_block(nc, *args, out)
    r = run_bass_kernel_spmd(nc, [arrays], core_ids=[0])
    return r.results[0]["out_0"]
```

```python
from contextlib import ExitStack

import concourse.bass as bass
from concourse import mybir

F32 = mybir.dt.float32
I32 = mybir.dt.int32
ALU = mybir.AluOpType
ACT = mybir.ActivationFunctionType
AX = mybir.AxisListType
ds = bass.ds

P = 128
CHUNK = 64
EPS = 1e-6
IDX_DIM = 64
GATE_TAU = 16.0
TOP_K = 4
LIMIT = 7.0
ALPHA = 1.702
HIDDEN = -1.0e30
GONE = -3.0e38
PAD = -2.0e38
SLOTS = 64

PLAN = (
    [("ada0", "A"), ("ada1", "A"), ("xT0", "V"), ("xT1", "A"), ("xT2", "V"), ("xT3", "A"), ("ada2", "A")]
    + [("colA", "V"), ("ada3", "A"), ("colB", "V")]
    + [("small", "A"), ("wi", "A"), ("qi0", "A"), ("qi1", "A"), ("z0", "A"), ("z1", "A"), ("qa0", "A"), ("qa1", "A")]
    + [("sx0", "A"), ("sx1", "A")] + [(f"sy{i}", "A") for i in range(4)] + [("qa2", "A"), ("qa3", "A")]
    + [("qb0", "V"), ("qb1", "V"), ("kb0", "V"), ("kb1", "V"), ("ka0", "A"), ("ka1", "A")]
    + [("kdT0", "A"), ("kdT1", "A"), ("AT", "A"), ("ka2", "A"), ("ka3", "A")]
    + [(f"vb{i}", "A") for i in range(4)] + [("s1a", "V"), ("s1b", "V"), ("va0", "A"), ("va1", "A")]
    + [("s2a", "V"), ("s2b", "V"), ("va2", "A"), ("va3", "A"), ("s3a", "V"), ("s3b", "V")]
    + [("lg0", "V"), ("lg1", "V"), ("gb0", "V"), ("gb1", "V"), ("pt0", "A"), ("pt1", "A"), ("lg2", "V"), ("lg3", "V")]
    + [("ya0", "A"), ("ya1", "A"), ("lg4", "V"), ("lg5", "V"), ("gb2", "V"), ("gb3", "V")]
    + [(f"pt{i}", "A") for i in range(2, 6)] + [(f"o{i}", "V") for i in range(4)] + [("ya2", "A"), ("ya3", "A")]
    + [(f"ga{i}", "A") for i in range(4)] + [(f"yT{i}", "A") for i in range(4)] + [(f"gm{i}", "A") for i in range(4)]
    + [t for r in range(8) for t in ((f"ap{r}", "A"), (f"ab{r}", "V"))]
    + [(f"wa{i}", "V") for i in range(4)] + [(f"wb{i}", "V") for i in range(4)] + [(f"wo{i}", "V") for i in range(4)]
    + [(f"hh{i}", "A") for i in range(4)] + [("rp", "A"), ("rl", "V"), ("rt", "V"), ("te", "V"), ("wt", "A")]
    + [(f"bs{i}", "V") for i in range(4)]
)
NUMBER = {name: n for n, (name, _) in enumerate(PLAN)}
TAKER = dict(PLAN)
TAKEN = [t for t in PLAN[:10] if t[0][:2] != "xT"] + [t for t in PLAN[:10] if t[0][:2] == "xT"] + PLAN[10:]
OUT_COUNT = {name: 1 + sum(1 for _, w in TAKEN[:n] if w == who) for n, (name, who) in enumerate(TAKEN)}

PIECES = (
    [("ada", i, f"ada{i}") for i in range(4)]
    + [("qi", 0, "qi1"), ("qa", 0, "qa1"), ("qa", 1, "qa3"), ("qb", 0, "qb1"), ("kb", 0, "kb1"), ("ka", 0, "ka1"),
       ("ka", 1, "ka3"), ("vb", 0, "vb1"), ("vb", 1, "vb3"), ("va", 0, "va1"), ("va", 1, "va3"), ("gb", 0, "gb1"),
       ("gb", 1, "gb3"), ("ga", 0, "ga1"), ("ga", 1, "ga3"), ("gm", 0, "gm1"), ("gm", 1, "gm3")]
    + [("ada", 4 + r, f"ap{r}") for r in range(8)]
    + [("wa", 0, "wa1"), ("wa", 1, "wa3"), ("wb", 0, "wb1"), ("wb", 1, "wb3"), ("wo", 0, "wo1"), ("wo", 1, "wo3")]
)
PIECE_NO = {(kind, c): n for n, (kind, c, _) in enumerate(PIECES)}


def hybrid_block(nc, x, c, w_ada, b_ada, norm1_g, w_in, w_gate_lr, b_gate, gla_norm_g, w_branch_a, w_branch_b, w_out,
                 norm2_g, router_w, router_b, w_gate_up, b_gate_up, w_down, b_down, final_g, out):
    _, T, D = x.shape
    TT, KT = T // P, D // P
    H = D // P
    IH = 8
    GH = 4
    DV = D // GH
    NCH = T // CHUNK
    RANK = w_gate_lr.shape[1]
    E = w_gate_up.shape[1]
    NA = w_ada.shape[2] // 512
    MAXB = E + T * TOP_K // SLOTS
    NP2 = 4
    assert TT == 2 and KT == 8 and D // GH // 2 == P and w_gate_lr.shape[2] == GH * P and E == 32

    sizes = dict(qa=D, ka=D, va=D, qi=IH * IDX_DIM, ki=IDX_DIM, wi=IH, qb=GH * P, kb=GH * P, vb=D, gb=D, lr=RANK, ga=D, gm=D)
    col, at = {}, 0
    for name, n in sizes.items():
        col[name] = at
        at += n

    def columns(w, a, n):
        return w[0, :, a:a + n].rearrange("(k p) n -> p k n", p=P)

    def piece_source(kind, i):
        w = {"ada": w_ada, "wa": w_branch_a, "wb": w_branch_b, "wo": w_out}.get(kind, w_in)
        return columns(w, col.get(kind, 0) + 512 * i, 512)

    with ExitStack() as ctx:
        KB = 1024
        base = 16512

        def sb(name, at_kb, shape, dt=F32):
            return nc.alloc_sbuf_tensor_at(name, shape, dt, offset=base + int(at_kb * KB))

        def sem(name):
            return ctx.enter_context(nc.semaphore(name))

        piece = [sb(f"piece{i}", 16 * i, [P, KT, 512]) for i in range(NP2)]
        gu_slot = [sb(f"gu_slot{j}", 8 * j, [P, 2048]) for j in range(8)]
        dn_slot = [sb(f"dn_slot{j}", 64 + 8 * j, [P, 2, D]) for j in range(4)]
        bias_row = sb("bias_row", 96, [1, 2 * D])
        vb = sb("vb", 64, [P, TT, D])
        G = sb("G", 72, [P, GH * T])
        qe = sb("qe", 76, [P, GH, T])
        ke = sb("ke", 80, [P, GH, T])
        kd = sb("kd", 84, [P, GH, T])
        kdt = sb("kdt", 88, [P, TT, GH * P])
        S = [None, sb("S1", 72, [P, GH * DV]), sb("S2", 84, [P, GH * DV]), sb("S3", 92, [P, GH * DV])]
        z = sb("z", 84, [P, GH * T])
        softp = sb("softp", 88, [P, GH * T])
        reset = sb("reset", 92, [P, GH * T])
        AT = sb("AT", 96, [P, 512])
        qiT = sb("qiT", 98, [P, IH // 2, T])
        kiT = sb("kiT", 102, [P, T])
        xs = sb("xs", 104, [P, TT, D])
        hT = sb("hT", 112, [P, KT, T])
        h2 = sb("h2", 112, [P, TT, D])
        modp = [sb(f"modp{i}", 120 + 2 * i, [P, 512]) for i in range(4)]
        qaT = sb("qaT", 120, [P, H, T])
        gaT = sb("gaT", 120, [P, KT, T])
        junk = sb("junk", 120, [P, D])
        kaT = sb("kaT", 128, [P, H, T])
        gmT = sb("gmT", 128, [P, KT, T])
        va = sb("va", 136, [P, TT, D])
        mergedT = sb("mergedT", 136, [P, KT, T])
        yb = sb("yb", 144, [P, TT, D])
        xn = sb("xn", 152, [P, TT, D])
        rel = [sb(f"rel{i}", 152 + 2 * i, [P, 512]) for i in range(2)]
        ojunk = sb("ojunk", 166, [P, DV])
        yaT = sb("yaT", 152, [P, H, T])
        ybT = sb("ybT", 160, [P, KT, T])
        h2T = sb("h2T", 160, [P, KT, T])
        wgl = sb("wgl", 160, [RANK, GH * P])
        wsm = sb("wsm", 162, [P, KT, IDX_DIM + IH + RANK])
        lrT = sb("lrT", 165, [RANK, T])
        prob = [sb(f"prob{i}", 168 + 2 * i, [P, 512]) for i in range(4)]
        probT = [sb(f"probT{i}", 176 + 2 * i, [P, 512]) for i in range(4)]
        gt1 = sb("gt1", 168, [P, D])
        sc2g = sb("sc2g", 172, [P, D])
        sh2 = sb("sh2", 176, [P, D])
        gt2 = sb("gt2", 180, [P, D])
        score = [sb("score0", 184, [P, P]), sb("score1", 184.5, [P, T])]
        work = [[sb("work00", 185.5, [P, P]), sb("work01", 186, [P, P])],
                [sb("work10", 186.5, [P, T]), sb("work11", 187.5, [P, T])]]
        keep = [sb("keep0", 188.5, [P, P]), sb("keep1", 189, [P, T])]
        modq = [sb(f"modq{i}", 184 + 2 * i, [P, 512]) for i in range(2)]
        tmp = sb("tmp", 184, [P, 512])
        fgb = sb("fgb", 190, [P, D])
        ident = sb("ident", 194, [P, P])
        ones = sb("ones", 194.5, [P, P])
        inv32 = sb("inv32", 195, [P, P])
        stack = sb("stack", 197.0, [P, 32])
        before = sb("before", 195.5, [P, P])
        silc = sb("silc", 196, [P, KT, 32])
        pick = sb("pick", 197.125, [NA, NA, 32])
        bada = sb("bada", 198.625, [NA, 512])
        gng = sb("gng", 200.75, [P, DV])
        wr = sb("wr", 201.75, [P, KT, E])
        rb = sb("rb", 202.75, [1, E])
        m_at = [203.0]

        def small(name, shape, dt=F32):
            n = 1
            for s in shape[1:]:
                n *= s
            t = sb(name, m_at[0], shape, dt)
            m_at[0] += (n * 4 + 31) // 32 * 32 / KB
            assert base + m_at[0] * KB <= 229368
            return t

        ccol = small("ccol", [P, KT])
        csig = small("csig", [P, KT])
        g1 = small("g1", [P, KT])
        gain1 = small("gain1", [P, KT])
        shift1 = small("shift1", [P, KT])
        wis = small("wis", [P, TT, IH])
        bg = small("bg", [P, GH])
        gsum = small("gsum", [P, GH, NCH])
        decay = small("decay", [P, GH, NCH])
        top8 = [small(f"top8_{i}", [P, 8]) for i in range(2)]
        mx = small("mx", [P, 24])
        nmx = small("nmx", [P, 24])
        esum = small("esum", [P, 24])
        erec = small("erec", [P, 24])
        sq = small("sq", [P, 8])
        sqe = small("sqe", [P, 8])
        root = small("root", [P, 8])
        rs = small("rs", [P, 8])
        rt_a = small("rt_a", [P, 8])
        rt_b = small("rt_b", [P, 8])
        lg = sb("lg", 152, [P, TT, E + TOP_K])
        lgw = sb("lgw", 152.5, [P, TT, E + TOP_K])
        r8 = sb("r8", 153, [P, TT, 8])
        nr8 = sb("nr8", 153.25, [P, TT])
        chosen = sb("chosen", 153.5, [P, TT, E])
        eexp = sb("eexp", 153.75, [P, TT, E])
        wts = sb("wts", 154, [P, TT, E])
        slot_id = sb("slot_id", 154.25, [P, TT, E])
        blocks = sb("blocks", 154.5, [P, E])
        blk_t = sb("blk_t", 154.75, [P, E])
        cum = sb("cum", 155, [P, E])
        cumx = sb("cumx", 155.25, [P, E])
        le = sb("le", 155.5, [MAXB + 1, E])
        eofc = sb("eofc", 155.75, [MAXB + 1, 1])
        steps8 = sb("steps8", 156, [P, T // SLOTS])
        over = sb("over", 156.25, [P, E, T // SLOTS])
        rpart = sb("rpart", 158, [P, T])
        eof = small("eof", [1, MAXB + 1])
        need_w = small("need_w", [1, MAXB + 1])
        table_e = small("table_e", [1, MAXB + 1], I32)
        table_w = small("table_w", [1, MAXB + 1], I32)
        table_used = small("table_used", [1, E], I32)
        table_n = small("table_n", [1, 1], I32)
        number = small("number", [P, 1])
        primer = small("primer", [P, 14])
        usedf = small("usedf", [1, E])
        iota = small("iota", [P, SLOTS])
        warm = small("warm", [P, 2])
        acc = sb("acc", 120, [P, TT, D])
        xg = sb("xg", 128, [P, 4, P])
        gx = sb("gx", 130, [P, 512])
        gcl = sb("gcl", 132, [P, 512])
        sig = sb("sig", 134, [P, 512])
        ucl = sb("ucl", 136, [P, 512])
        act_t = sb("act_t", 138, [P, 512])
        actT = sb("actT", 140, [P, 4, P])
        ysb = sb("ysb", 142, [P, 512])
        sel = sb("sel", 144, [P, TT, SLOTS])
        selw = sb("selw", 144.5, [P, TT, 2, SLOTS])
        selwT = sb("selwT", 145.5, [P, T])
        wT = sb("wT", 147, [E, T])
        bd = sb("bd", 148, [E, D])
        final = sb("final", 0, [P, TT, D])
        junk2 = sb("junk2", 160, [P, D])

        bank = [ctx.enter_context(nc.psum_tensor(f"bank{i}", [P, 512], F32)) for i in range(8)]

        sum_bank = [[bank[6], bank[7]], [bank[4], bank[5]]]

        tile_full = sem("tile_full")
        out_act = sem("out_act")
        out_dve = sem("out_dve")
        piece_in = [sem(f"piece_in{i}") for i in range(NP2)]
        x_in, c_in, g1_in, bada_in, wsm_in, wgl_in, misc_in, late_in = (
            sem(n) for n in ("x_in", "c_in", "g1_in", "bada_in", "wsm_in", "wgl_in", "misc_in", "late_in"))
        g2_in, fg_in = sem("g2_in"), sem("fg_in")
        pool_step, dve_step, act_step = sem("pool_step"), sem("dve_step"), sem("act_step")
        consts_ready, pick_ready = sem("consts_ready"), sem("pick_ready")
        gain1_ready = sem("gain1_ready")
        csig_ready, silc_ready, xss_ready, xvar_ready, xroot_ready, xn_ready = (
            sem(n) for n in ("csig_ready", "silc_ready", "xss_ready", "xvar_ready", "xroot_ready", "xn_ready"))
        softp_ready, gsum_ready, gexp_ready, gdiff_ready, gdec_ready, kd_ready = (
            sem(n) for n in ("softp_ready", "gsum_ready", "gexp_ready", "gdiff_ready", "gdec_ready", "kd_ready"))
        rel_used, at_masked, s_ready = sem("rel_used"), sem("at_masked"), sem("s_ready")
        nmx_ready, exp_ready, prob_ready, gsig_ready = sem("nmx_ready"), sem("exp_ready"), sem("prob_ready"), sem("gsig_ready")
        oss_ready, ovar_ready, oroot_ready, yb_ready = (sem(n) for n in ("oss_ready", "ovar_ready", "oroot_ready", "yb_ready"))
        merged_ready, x2_ready, x2ss_ready, x2var_ready, x2root_ready, h2_ready = (
            sem(n) for n in ("merged_ready", "x2_ready", "x2ss_ready", "x2var_ready", "x2root_ready", "h2_ready"))
        eofc_ready = sem("eofc_ready")
        rneg_ready, rexp_ready, chosen_ready, wts_ready, tables_ready = (
            sem(n) for n in ("rneg_ready", "rexp_ready", "chosen_ready", "wts_ready", "tables_ready"))
        gu_in = [sem(f"gu_in{j}") for j in range(8)]
        dn_in = [sem(f"dn_in{j}") for j in range(4)]
        bgu_in, bd_in = sem("bgu_in"), sem("bd_in")
        gu_used = [sem(f"gu_used{j}") for j in range(8)]
        dn_used = [sem(f"dn_used{j}") for j in range(4)]
        bias_used = sem("bias_used")
        sel_ready, gath_full, gx_out, gxT_full, xg_out = (
            sem(n) for n in ("sel_ready", "gath_full", "gx_out", "gxT_full", "xg_out"))
        selw_ready, selwT_full, selw_out = sem("selw_ready"), sem("selwT_full"), sem("selw_out")
        gu_full, gcl_ready, ucl_ready, sig_ready, gs_ready, act_ready = (
            sem(n) for n in ("gu_full", "gcl_ready", "ucl_ready", "sig_ready", "gs_ready", "act_ready"))
        actT_full, actT_out, y_full, y_out, sc_full, acc_out = (
            sem(n) for n in ("actT_full", "actT_out", "y_full", "y_out", "sc_full", "acc_out"))
        numbers_ready = sem("numbers_ready")
        iota_ready, add_done = sem("iota_ready"), sem("add_done")
        fss_ready, fvar_ready, froot_ready, fin_ready, stored = (
            sem(n) for n in ("fss_ready", "fvar_ready", "froot_ready", "fin_ready", "stored"))

        def tile(name):
            return bank[NUMBER[name] % 8]

        def wait_tile(eng, name):
            eng.wait_ge(tile_full, NUMBER[name] + 1)

        def wait_out(eng, name):
            eng.wait_ge(out_act if TAKER[name] == "A" else out_dve, OUT_COUNT[name])

        class Steps:

            def __init__(self, eng, own):
                self.eng, self.own, self.count, self.last = eng, own, {}, None

            def __call__(self, ins, signal=None):
                signal = signal or self.own
                ins.then_inc(signal, 1)
                self.count[signal.name] = self.count.get(signal.name, 0) + 1
                self.last = (signal, self.count[signal.name])

            def settle(self):
                self.eng.wait_ge(*self.last)

        block = ctx.enter_context(nc.Block())

        @block.sync
        def _(sp):
            def load_expert_piece(e, j):
                if j < 8:
                    sp.dma_start(gu_slot[j][:], w_gate_up[0, e, j * P:(j + 1) * P, :] if isinstance(e, int) else
                                 w_gate_up[0, ds(e, 1), j * P:(j + 1) * P, :].rearrange("a p n -> p (a n)")).then_inc(gu_in[j], 16)
                elif j < 12:
                    i = j - 8
                    rows = slice(2 * i * P, 2 * (i + 1) * P)
                    sp.dma_start(dn_slot[i][:], w_down[0, e, rows, :].rearrange("(i p) n -> p i n", p=P) if isinstance(e, int) else
                                 w_down[0, ds(e, 1), rows, :].rearrange("a (i p) n -> p (a i) n", p=P)).then_inc(dn_in[i], 16)
                else:
                    one = slice(e, e + 1) if isinstance(e, int) else ds(e, 1)
                    sp.dma_start(bias_row[:], b_gate_up[0, one, :]).then_inc(bgu_in, 16)

            for n, (kind, i, last) in enumerate(PIECES):
                if n >= NP2:
                    wait_tile(sp, PIECES[n - NP2][2])
                sp.dma_start(piece[n % NP2][:], piece_source(kind, i)).then_inc(piece_in[n % NP2], 16)
                if n == PIECE_NO["ada", 9]:
                    wait_tile(sp, "o3")
                    for j in (12, 8, 9, 10, 11):
                        load_expert_piece(0, j)
            for j in range(8):
                user = [last for n, (_, _, last) in enumerate(PIECES) if n % NP2 == j // 2][-1]
                wait_tile(sp, user)
                load_expert_piece(0, j)
            sp.wait_ge(tables_ready, 1)
            with sp.Fori(1, E) as e:
                free = sp.value_load(table_used[0:1, ds(e, 1)], min_val=1, max_val=MAXB + 1)
                for j in (12, 0, 1, 2, 3, 4, 5, 6, 7, 8, 9, 10, 11):
                    here, used = ((gu_in[j], gu_used[j]) if j < 8 else (dn_in[j - 8], dn_used[j - 8]) if j < 12 else
                                  (bgu_in, bias_used))
                    sp.wait_ge(here, 16 * e)
                    sp.wait_ge(used, free)
                    load_expert_piece(e, j)
            sp.wait_ge(fin_ready, TT)
            sp.dma_start(out[0].rearrange("(t p) n -> p t n", p=P), final[:]).then_inc(stored, 16)
            sp.wait_ge(stored, 16)

        @block.gpsimd
        def _(pool):
            step = Steps(pool, pool_step)
            step(nc.gpsimd.memset(ident[:], 0.0))
            step(nc.gpsimd.memset(ones[:], 1.0))
            step(nc.gpsimd.memset(inv32[:], 1.0 / 32))
            step(nc.gpsimd.memset(pick[:], 0.0))
            step(nc.gpsimd.memset(stack[:], 0.0))
            step(nc.gpsimd.iota(iota[:], [[1, SLOTS]], base=0, channel_multiplier=0, allow_small_or_imprecise_dtypes=True))
            step.settle()
            step(nc.gpsimd.affine_select(out=ident[:], in_=ident[:], compare_op=ALU.not_equal, fill=1.0, base=0,
                                         pattern=[[-1, P]], channel_multiplier=1))
            for q in range(4):
                v = stack[32 * q:32 * q + 32, :]
                step.settle()
                step(nc.gpsimd.affine_select(out=v, in_=v, compare_op=ALU.not_equal, fill=1.0, base=0,
                                             pattern=[[-1, 32]], channel_multiplier=1))
            step.settle()
            step(nc.gpsimd.affine_select(out=pick[:], in_=pick[:], compare_op=ALU.not_equal, fill=1.0, base=0,
                                         pattern=[[-1, NA], [0, 32]], channel_multiplier=1))
            step(nc.gpsimd.affine_select(out=before[:], in_=ones[:], compare_op=ALU.is_gt, fill=0.0, base=0,
                                         pattern=[[1, P]], channel_multiplier=-1))
            step(nc.gpsimd.memset(reset[:], 1.0))
            step.settle()
            step(nc.gpsimd.memset(reset[:].rearrange("p (c i) -> p c i", i=CHUNK)[:, :, 0:1], 0.0), consts_ready)
            wait_out(pool, "AT")
            for half in range(2):
                v = AT[64 * half:64 * half + 64, :].rearrange("p (c i) -> p c i", i=CHUNK)
                step(nc.gpsimd.affine_select(out=v, in_=v, compare_op=ALU.is_ge, fill=0.0, base=0,
                                             pattern=[[0, 2 * GH], [1, CHUNK]], channel_multiplier=-1), at_masked)
            wait_tile(pool, "ya3")
            pool.dma_start(sc2g[:], norm2_g[0:1, :].to_broadcast([P, D])).then_inc(g2_in, 16)
            wait_tile(pool, "yT3")
            pool.dma_start(bd[:], b_down[0]).then_inc(bd_in, 16)
            wait_tile(pool, "wa3")
            step(nc.gpsimd.iota(steps8[:], [[SLOTS, T // SLOTS]], base=0, channel_multiplier=0,
                                allow_small_or_imprecise_dtypes=True))
            step(nc.gpsimd.iota(number[:], [[0, 1]], base=0, channel_multiplier=1,
                                allow_small_or_imprecise_dtypes=True), numbers_ready)

        @block.scalar
        def _(act):
            step = Steps(act, act_step)
            A = nc.scalar.activation

            act.dma_start(xs[:], x[0].rearrange("(t p) n -> p t n", p=P)).then_inc(x_in, 16)
            act.dma_start(ccol[:], c[0].rearrange("(k p) -> p k", p=P), allow_slow_non_contiguous=True).then_inc(c_in, 16)
            act.dma_start(bada[:], b_ada[0].rearrange("(a n) -> a n", n=512)).then_inc(bada_in, 16)
            act.dma_start(g1[:], norm1_g[0].rearrange("(k p) -> p k", p=P), allow_slow_non_contiguous=True).then_inc(g1_in, 16)
            act.dma_start(wsm[:, :, 0:IDX_DIM + IH], columns(w_in, col["ki"], IDX_DIM + IH)).then_inc(wsm_in, 16)
            act.dma_start(wsm[:, :, IDX_DIM + IH:], columns(w_in, col["lr"], RANK)).then_inc(wsm_in, 16)
            act.dma_start(wgl[:], w_gate_lr[0]).then_inc(wgl_in, 16)
            act.dma_start(bg[:], b_gate[0].rearrange("(h p) -> p h", p=P), allow_slow_non_contiguous=True).then_inc(misc_in, 16)
            act.dma_start(gng[:], gla_norm_g[0:1, :].to_broadcast([P, DV])).then_inc(late_in, 16)
            act.dma_start(wr[:], router_w[0].rearrange("(k p) n -> p k n", p=P)).then_inc(late_in, 16)
            act.dma_start(rb[:], router_b[0:1, :]).then_inc(late_in, 16)
            act.dma_start(fgb[:], final_g.rearrange("(a n) -> a n", a=1).to_broadcast([P, D])).then_inc(fg_in, 16)

            def take(name, *ops):
                wait_tile(act, name)
                for n, (o, i, f, kw) in enumerate(ops):
                    ins = A(o, i, f, **kw)
                    if n == len(ops) - 1:
                        step(ins, out_act)
                    else:
                        step(ins)

            act.wait_ge(c_in, 16)
            step(A(csig[:], ccol[:], ACT.Sigmoid), csig_ready)
            act.wait_ge(x_in, 16)
            for t in range(TT):
                step(A(xn[:, t, :], xs[:, t, :], ACT.Square, accum_out=sq[:, t:t + 1]), xss_ready)
            act.wait_ge(xvar_ready, 1)
            step(A(root[:, 0:TT], sqe[:, 0:TT], ACT.Sqrt), xroot_ready)

            for i in range(4):
                take(f"ada{i}", (modp[i][:], tile(f"ada{i}")[:], ACT.Copy, {}))
            act.wait_ge(gain1_ready, 1)
            for i in (1, 3):
                t, half = divmod(i, 2)
                take(f"xT{i}", *[(hT[:, k, t * P:(t + 1) * P], tile(f"xT{i}")[:, (k % 4) * P:(k % 4 + 1) * P], ACT.Identity,
                                  dict(scale=gain1[:, k:k + 1], bias=shift1[:, k:k + 1])) for k in range(4 * half, 4 * half + 4)])
            take("small", (kiT[:], tile("small")[:, 0:T], ACT.Copy, {}),
                 (lrT[:], tile("small")[0:RANK, T:2 * T], ACT.Copy, {}))
            take("wi", (wis[:].rearrange("p t h -> p (t h)"), tile("wi")[:, 0:TT * IH], ACT.Copy, dict(scale=float(IH) ** -0.5)))
            for i in range(2):
                take(f"qi{i}", (qiT[:, 2 * i:2 * i + 2, :].rearrange("p a b -> p (a b)"), tile(f"qi{i}")[:], ACT.Copy,
                                dict(scale=IDX_DIM ** -0.5)))
            act.wait_ge(misc_in, 16)
            for i in range(2):
                take(f"z{i}", *[(z[:, (2 * i + j) * T:(2 * i + j + 1) * T], tile(f"z{i}")[:, j * T:(j + 1) * T], ACT.Identity,
                                 dict(bias=bg[:, 2 * i + j:2 * i + j + 1])) for j in range(2)])
            step.settle()
            step(A(softp[:], z[:], ACT.Abs))
            step.settle()
            step(A(softp[:], softp[:], ACT.Exp, scale=-1.0))
            step.settle()
            step(A(softp[:], softp[:], ACT.Ln, bias=1.0), softp_ready)

            def take_qk(dst, kind, i):
                take(f"{kind}{i}", (dst[:, 2 * i:2 * i + 2, :].rearrange("p a b -> p (a b)"), tile(f"{kind}{i}")[:], ACT.Copy, {}))

            def take_rows(dst, kind, i):
                cc, t = divmod(i, TT)
                take(f"{kind}{i}", (dst[:, t, 512 * cc:512 * cc + 512], tile(f"{kind}{i}")[:], ACT.Copy, {}))

            take_qk(qaT, "qa", 0)
            take_qk(qaT, "qa", 1)
            for n, name in enumerate(["sx0", "sx1", "sy0", "sy1", "sy2", "sy3"]):
                if n >= 2:
                    act.wait_ge(rel_used, n - 1)
                take(name, (rel[n % 2][:], tile(name)[:], ACT.Relu, {}))
            take_qk(qaT, "qa", 2)
            take_qk(qaT, "qa", 3)
            act.wait_ge(gsum_ready, 1)
            step(A(qe[:].rearrange("p h t -> p (h t)"), G[:], ACT.Exp, scale=1.0 / GATE_TAU))
            step(A(ke[:].rearrange("p h t -> p (h t)"), G[:], ACT.Exp, scale=-1.0 / GATE_TAU), gexp_ready)
            act.wait_ge(gdiff_ready, 1)
            step(A(softp[:], softp[:], ACT.Exp, scale=1.0 / GATE_TAU))
            step(A(decay[:].rearrange("p h n -> p (h n)"), gsum[:].rearrange("p h n -> p (h n)"), ACT.Exp,
                   scale=1.0 / GATE_TAU), gdec_ready)
            take_qk(kaT, "ka", 0)
            take_qk(kaT, "ka", 1)
            for t in range(TT):
                take(f"kdT{t}", (kdt[:, t, :], tile(f"kdT{t}")[:], ACT.Copy, {}))
            take("AT", (AT[:], tile("AT")[:], ACT.Copy, {}))
            take_qk(kaT, "ka", 2)
            take_qk(kaT, "ka", 3)
            for i in range(4):
                take_rows(vb, "vb", i)
            for i in range(4):
                take_rows(va, "va", i)

            def exps(g):
                n, w = (4, P) if g < 2 else (2, 2 * P)
                act.wait_ge(nmx_ready, g + 1)
                for j in range(n):
                    ins = A(prob[g % 4][:, j * w:(j + 1) * w], prob[g % 4][:, j * w:(j + 1) * w], ACT.Exp,
                            bias=nmx[:, 4 * g + j:4 * g + j + 1], accum_out=esum[:, 4 * g + j:4 * g + j + 1])
                    step(ins, exp_ready if j == n - 1 else None)

            def gate_sig(i):
                cc, t = divmod(i, TT)
                wait_tile(act, f"gb{i}")
                step(A(yb[:, t, 512 * cc:512 * cc + 512], tile(f"gb{i}")[:], ACT.Sigmoid), gsig_ready)

            def take_probT(g):
                if g >= 4:
                    wait_tile(act, f"ya{g - 4}")
                take(f"pt{g}", (probT[g % 4][:], tile(f"pt{g}")[:], ACT.Copy, {}))

            def take_ya(i):
                t, half = divmod(i, 2)
                take(f"ya{i}", (yaT[:, 4 * half:4 * half + 4, t * P:(t + 1) * P],
                                tile(f"ya{i}")[:].rearrange("p (h q) -> p h q", h=4), ACT.Copy, {}))

            exps(0)
            exps(1)
            gate_sig(0)
            gate_sig(1)
            take_probT(0)
            take_probT(1)
            exps(2)
            exps(3)
            take_ya(0)
            take_ya(1)
            exps(4)
            exps(5)
            gate_sig(2)
            gate_sig(3)
            for g in range(2, 6):
                take_probT(g)
            for i in range(4):
                wait_tile(act, f"o{i}")
                for j in range(2):
                    step(A(ojunk[:], tile(f"o{i}")[:, j * DV:(j + 1) * DV], ACT.Square,
                           accum_out=sq[:, 2 * i + j:2 * i + j + 1]), oss_ready)
                    step.settle()
            act.wait_ge(ovar_ready, 1)
            step(A(root[:], sqe[:], ACT.Sqrt), oroot_ready)
            take_ya(2)
            take_ya(3)

            def take_sig(dst, kind, i):
                take(f"{kind}{i}", (dst[:, 2 * i:2 * i + 2, :].rearrange("p a b -> p (a b)"), tile(f"{kind}{i}")[:], ACT.Sigmoid, {}))

            def take_T(dst, kind, i):
                t, half = divmod(i, 2)
                take(f"{kind}{i}", (dst[:, 4 * half:4 * half + 4, t * P:(t + 1) * P],
                                    tile(f"{kind}{i}")[:].rearrange("p (h q) -> p h q", h=4), ACT.Copy, {}))

            for i in range(4):
                take_sig(gaT, "ga", i)
            for i in range(4):
                take_T(ybT, "yT", i)
            for i in range(4):
                take_sig(gmT, "gm", i)
            for r in range(8):
                if r >= 2:
                    wait_tile(act, f"ab{r - 2}")
                take(f"ap{r}", (modq[r % 2][:], tile(f"ap{r}")[:], ACT.Copy, {}))
            step(A(warm[:, 0:1], ident[:, 0:1], ACT.Sqrt))
            for i in range(4):
                cc, t = divmod(i, TT)
                act.wait_ge(x2_ready, i + 1)
                step.settle()
                step(A(junk[:, 0:512], xs[:, t, 512 * cc:512 * cc + 512], ACT.Square, accum_out=sq[:, 2 * cc + t:2 * cc + t + 1]),
                     x2ss_ready)
            act.wait_ge(x2var_ready, 1)
            step(A(root[:, 0:TT], sqe[:, 0:TT], ACT.Sqrt), x2root_ready)
            step(A(warm[:, 1:2], ident[:, 0:1], ACT.Exp))
            for i in range(4):
                take_T(h2T, "hh", i)
            take("rp", (rpart[:], tile("rp")[:, 0:T], ACT.Copy, {}))
            act.wait_ge(rneg_ready, 1)
            for t in range(TT):
                step(A(eexp[:, t, :], lg[:, t, 0:E], ACT.Exp, bias=nr8[:, t:t + 1]), rexp_ready)

            take("wt", (wT[:], tile("wt")[0:E, 0:T], ACT.Copy, {}))

            act.wait_ge(gath_full, 1)
            step(A(gx[:], bank[2][:], ACT.Copy), gx_out)
            act.wait_ge(gxT_full, 1)
            step(A(xg[:].rearrange("p j s -> p (j s)"), bank[3][:], ACT.Copy), xg_out)
            act.wait_ge(tables_ready, 1)
            nb = act.value_load(table_n[0:1, 0:1], min_val=1, max_val=MAXB)
            with act.Fori(0, nb) as g:
                g1_ = act.snap(g + 1)
                g2_ = act.snap(g + 2)
                act.wait_ge(gcl_ready, g1_)
                A(sig[:], gcl[:], ACT.Sigmoid, scale=ALPHA).then_inc(sig_ready, 1)
                act.wait_ge(gath_full, g2_)
                A(gx[:], bank[2][:], ACT.Copy).then_inc(gx_out, 1)
                act.wait_ge(actT_full, g1_)
                A(actT[:].rearrange("p c s -> p (c s)"), bank[4][:], ACT.Copy).then_inc(actT_out, 1)
                act.wait_ge(selwT_full, g1_)
                act.wait_ge(acc_out, g1_)
                A(selwT[:], bank[1][:, 0:T], ACT.Copy).then_inc(selw_out, 1)
                act.wait_ge(gxT_full, g2_)
                A(xg[:].rearrange("p j s -> p (j s)"), bank[3][:], ACT.Copy).then_inc(xg_out, 1)
                act.wait_ge(y_full, g1_)
                A(ysb[:], bank[5][:], ACT.Copy).then_inc(y_out, 1)
            act.wait_ge(add_done, 1)
            for t in range(TT):
                step(A(junk2[:], xs[:, t, :], ACT.Square, accum_out=sq[:, t:t + 1]), fss_ready)
                step.settle()
            act.wait_ge(fvar_ready, 1)
            step(A(root[:, 0:TT], sqe[:, 0:TT], ACT.Sqrt), froot_ready)

        @block.vector
        def _(dve):
            V = nc.vector
            step = Steps(dve, dve_step)

            def chain(ins, signal=None):
                step(ins, signal)
                step.settle()

            def inverse_root(n, count, seen, var_ready, root_ready):
                dve.wait_ge(*seen)
                chain(V.tensor_scalar(sqe[:, 0:n], sq[:, 0:n], 1.0 / count, EPS, ALU.mult, ALU.add), var_ready)
                dve.wait_ge(root_ready, 1)
                chain(V.reciprocal(rt_a[:, 0:n], root[:, 0:n]))
                chain(V.tensor_tensor(rt_b[:, 0:n], rt_a[:, 0:n], rt_a[:, 0:n], ALU.mult))
                chain(V.tensor_tensor(rt_b[:, 0:n], rt_b[:, 0:n], sqe[:, 0:n], ALU.mult))
                chain(V.tensor_scalar(rt_b[:, 0:n], rt_b[:, 0:n], -0.5, 1.5, ALU.mult, ALU.add))
                chain(V.tensor_tensor(rs[:, 0:n], rt_a[:, 0:n], rt_b[:, 0:n], ALU.mult))

            dve.wait_ge(csig_ready, 1)
            chain(V.tensor_tensor(csig[:], csig[:], ccol[:], ALU.mult))
            step(V.tensor_copy(silc[:], csig[:].unsqueeze(2).to_broadcast([P, KT, 32])), silc_ready)
            inverse_root(TT, D, (xss_ready, TT), xvar_ready, xroot_ready)
            for t in range(TT):
                step(V.tensor_scalar(xn[:, t, :], xs[:, t, :], rs[:, t:t + 1], None, ALU.mult), xn_ready)
            wait_tile(dve, "colA")
            step(V.tensor_copy(shift1[:], tile("colA")[:, 0:KT]))
            dve.wait_ge(g1_in, 16)
            step(V.scalar_tensor_tensor(gain1[:, 0:4], tile("colA")[:, KT:KT + 4], 1.0, g1[:, 0:4], ALU.add, ALU.mult), out_dve)
            wait_tile(dve, "colB")
            chain(V.scalar_tensor_tensor(gain1[:, 4:8], tile("colB")[:, 0:4], 1.0, g1[:, 4:8], ALU.add, ALU.mult), out_dve)
            step(V.memset(primer[:, 0:1], 0.0), gain1_ready)
            for i in (0, 2):
                t, half = divmod(i, 2)
                wait_tile(dve, f"xT{i}")
                for j in range(4):
                    k = 4 * half + j
                    step(V.tensor_scalar(hT[:, k, t * P:(t + 1) * P], tile(f"xT{i}")[:, j * P:(j + 1) * P],
                                         gain1[:, k:k + 1], shift1[:, k:k + 1], ALU.mult, ALU.add), out_dve if j == 3 else None)
            dve.wait_ge(softp_ready, 1)
            dve.wait_ge(consts_ready, 1)
            chain(V.scalar_tensor_tensor(z[:], z[:], 0.0, softp[:], ALU.min, ALU.subtract))
            chain(V.tensor_tensor_scan(G[:], reset[:], z[:], 0.0, ALU.mult, ALU.add))
            Gc = G[:].rearrange("p (c i) -> p c i", i=CHUNK)
            chain(V.tensor_copy(gsum[:].rearrange("p h n -> p (h n)").unsqueeze(2), Gc[:, :, CHUNK - 1:CHUNK]), gsum_ready)
            step(V.tensor_tensor(softp[:].rearrange("p (c i) -> p c i", i=CHUNK),
                                 gsum[:].rearrange("p h n -> p (h n)").unsqueeze(2).to_broadcast([P, GH * NCH, CHUNK]), Gc,
                                 ALU.subtract), gdiff_ready)

            plan = [("sx0", 0, (0, 2, 4, 6)), ("sx1", 0, (1, 3, 5, 7)),
                    ("sy0", 1, (0, 2)), ("sy1", 1, (1, 3)), ("sy2", 1, (4, 6)), ("sy3", 1, (5, 7))]
            fresh = {0: True, 1: True}
            for n, (name, t, heads) in enumerate(plan):
                w = P if t == 0 else T
                wait_out(dve, name)
                if n == 0:
                    wait_out(dve, "wi")
                for j, h in enumerate(heads):
                    src, wcol = rel[n % 2][:, j * w:(j + 1) * w], wis[:, t, h:h + 1]
                    sig_ = rel_used if j == len(heads) - 1 else None
                    if fresh[t]:
                        chain(V.tensor_scalar(score[t][:], src, wcol, None, ALU.mult), sig_)
                        fresh[t] = False
                    else:
                        chain(V.scalar_tensor_tensor(score[t][:], src, wcol, score[t][:], ALU.mult, ALU.add), sig_)
            for t in range(TT):
                first = 2 * t * CHUNK + CHUNK
                chain(V.memset(score[t][0:CHUNK, first:first + CHUNK], HIDDEN))
            for t in range(TT):
                src = score[t]
                for r in range(CHUNK // 8):
                    dst = work[t][r % 2]
                    chain(V.max(top8[r % 2][:], src[:]))
                    chain(V.match_replace(dst[:], top8[r % 2][:], src[:], GONE))
                    src = dst
                chain(V.tensor_scalar(keep[t][:], src[:], GONE, HIDDEN, ALU.not_equal, ALU.mult))

            dve.wait_ge(gexp_ready, 1)
            for i in range(2):
                wait_tile(dve, f"qb{i}")
                step(V.scalar_tensor_tensor(qe[:, 2 * i:2 * i + 2, :], tile(f"qb{i}")[:].rearrange("p (h t) -> p h t", h=2),
                                            float(P) ** -0.5, qe[:, 2 * i:2 * i + 2, :], ALU.mult, ALU.mult), out_dve)
            dve.wait_ge(gdec_ready, 1)
            for i in range(2):
                wait_tile(dve, f"kb{i}")
                step(V.tensor_tensor(kd[:, 2 * i:2 * i + 2, :], tile(f"kb{i}")[:].rearrange("p (h t) -> p h t", h=2),
                                     softp[:].rearrange("p (h t) -> p h t", h=GH)[:, 2 * i:2 * i + 2, :], ALU.mult), kd_ready)
                step(V.tensor_tensor(ke[:, 2 * i:2 * i + 2, :], tile(f"kb{i}")[:].rearrange("p (h t) -> p h t", h=2),
                                     ke[:, 2 * i:2 * i + 2, :], ALU.mult), out_dve)

            def state(n):
                for half, name in enumerate((f"s{n}a", f"s{n}b")):
                    wait_tile(dve, name)
                    for j in range(2):
                        h = 2 * half + j
                        src = tile(name)[:, j * DV:(j + 1) * DV]
                        dst = S[n][:, h * DV:(h + 1) * DV]
                        signal = out_dve if j == 1 else None
                        if n == 1:
                            step(V.tensor_copy(dst, src), signal)
                        else:
                            step(V.scalar_tensor_tensor(dst, S[n - 1][:, h * DV:(h + 1) * DV], decay[:, h, n - 1:n], src,
                                                        ALU.mult, ALU.add), signal)
                step.settle()

            state(1)
            state(2)
            state(3)

            def logits(g):
                if g < 2:
                    n, w, t = 4, P, 0
                else:
                    n, w, t = 2, T, 1
                if g >= 4:
                    wait_tile(dve, f"pt{g - 4}")
                wait_tile(dve, f"lg{g}")
                L = prob[g % 4][:].rearrange("p (h s) -> p h s", h=n)
                chain(V.scalar_tensor_tensor(L, tile(f"lg{g}")[:].rearrange("p (h s) -> p h s", h=n), float(P) ** -0.5,
                                             keep[t][:].unsqueeze(1).to_broadcast([P, n, w]), ALU.mult, ALU.add), out_dve)
                chain(V.tensor_reduce(mx[:, 4 * g:4 * g + n], L, AX.X, ALU.max))
                chain(V.tensor_scalar(nmx[:, 4 * g:4 * g + n], mx[:, 4 * g:4 * g + n], -1.0, None, ALU.mult), nmx_ready)

            def normalize(g):
                n, w = (4, P) if g < 2 else (2, T)
                dve.wait_ge(exp_ready, g + 1)
                chain(V.reciprocal(erec[:, 4 * g:4 * g + n], esum[:, 4 * g:4 * g + n]))
                for j in range(n):
                    step(V.tensor_scalar(prob[g % 4][:, j * w:(j + 1) * w], prob[g % 4][:, j * w:(j + 1) * w],
                                         erec[:, 4 * g + j:4 * g + j + 1], None, ALU.mult), prob_ready if j == n - 1 else None)

            def gate(i):
                cc, t = divmod(i, TT)
                dst = yb[:, t, 512 * cc:512 * cc + 512]
                dve.wait_ge(gsig_ready, i + 1)
                chain(V.tensor_tensor(dst, tile(f"gb{i}")[:], dst, ALU.mult), out_dve)
                dst = dst.rearrange("p (h v) -> p h v", h=2)
                step(V.tensor_tensor(dst, dst, gng[:].unsqueeze(1).to_broadcast([P, 2, DV]), ALU.mult))

            logits(0)
            logits(1)
            normalize(0)
            normalize(1)
            dve.wait_ge(late_in, 48)
            gate(0)
            gate(1)
            logits(2)
            logits(3)
            normalize(2)
            normalize(3)
            logits(4)
            logits(5)
            normalize(4)
            normalize(5)
            gate(2)
            gate(3)
            inverse_root(8, DV, (oss_ready, 8), ovar_ready, oroot_ready)
            for i in range(4):
                t, half = divmod(i, 2)
                for j in range(2):
                    h = 2 * half + j
                    dst = yb[:, t, h * DV:(h + 1) * DV]
                    step(V.scalar_tensor_tensor(dst, tile(f"o{i}")[:, j * DV:(j + 1) * DV], rs[:, 2 * i + j:2 * i + j + 1], dst,
                                                ALU.mult, ALU.mult), out_dve if j == 1 else None)
            for r in range(8):
                dst = (gt1, sh2, sc2g, gt2)[r // 2][:, 512 * (r % 2):512 * (r % 2) + 512]
                wait_tile(dve, f"ab{r}")
                if r == 4:
                    dve.wait_ge(g2_in, 16)
                if r // 2 == 2:
                    step(V.scalar_tensor_tensor(dst, tile(f"ab{r}")[:], 1.0, dst, ALU.add, ALU.mult), out_dve)
                else:
                    step(V.tensor_copy(dst, tile(f"ab{r}")[:]), out_dve)
            for i in range(4):
                wait_tile(dve, f"wa{i}")
                wait_out(dve, f"ga{i}")
                step(V.tensor_tensor(mergedT[:, 2 * i:2 * i + 2, :].rearrange("p a b -> p (a b)"), tile(f"wa{i}")[:],
                                     gaT[:, 2 * i:2 * i + 2, :].rearrange("p a b -> p (a b)"), ALU.mult), out_dve)
            for i in range(4):
                m = mergedT[:, 2 * i:2 * i + 2, :].rearrange("p a b -> p (a b)")
                wait_tile(dve, f"wb{i}")
                chain(V.tensor_tensor(tmp[:], tile(f"wb{i}")[:], gmT[:, 2 * i:2 * i + 2, :].rearrange("p a b -> p (a b)"),
                                      ALU.mult), out_dve)
                chain(V.tensor_tensor(m, m, tmp[:], ALU.add), merged_ready)
            for i in range(4):
                cc, t = divmod(i, TT)
                xv = xs[:, t, 512 * cc:512 * cc + 512]
                wait_tile(dve, f"wo{i}")
                chain(V.tensor_tensor(tmp[:], tile(f"wo{i}")[:], gt1[:, 512 * cc:512 * cc + 512], ALU.mult), out_dve)
                chain(V.tensor_tensor(xv, xv, tmp[:], ALU.add), x2_ready)
            dve.wait_ge(x2ss_ready, 4)
            chain(V.tensor_tensor(sq[:, 0:TT], sq[:, 0:TT], sq[:, TT:2 * TT], ALU.add))
            inverse_root(TT, D, (x2ss_ready, 4), x2var_ready, x2root_ready)
            for t in range(TT):
                for half in range(2):
                    cols_ = slice(512 * half, 512 * half + 512)
                    chain(V.scalar_tensor_tensor(h2[:, t, cols_], xs[:, t, cols_], rs[:, t:t + 1], sc2g[:, cols_],
                                                 ALU.mult, ALU.mult))
                    step(V.tensor_tensor(h2[:, t, cols_], h2[:, t, cols_], sh2[:, cols_], ALU.add), h2_ready)

            step(V.memset(lg[:, :, E:E + TOP_K], PAD))
            wait_tile(dve, "rl")
            chain(V.tensor_copy(lg[:, :, 0:E], tile("rl")[:, 0:TT * E].rearrange("p (t e) -> p t e", e=E)), out_dve)
            for t in range(TT):
                chain(V.max(r8[:, t, :], lg[:, t, 0:E]))
                step(V.tensor_scalar(nr8[:, t:t + 1], r8[:, t, 0:1], -1.0, None, ALU.mult), rneg_ready if t == 1 else None)
                chain(V.memset(r8[:, t, TOP_K:8], PAD))
                chain(V.match_replace(lgw[:, t, :], r8[:, t, :], lg[:, t, :], GONE))
                step(V.tensor_scalar(chosen[:, t, :], lgw[:, t, 0:E], GONE, None, ALU.is_equal), chosen_ready)
            for t in range(TT):
                dve.wait_ge(rexp_ready, t + 1)
                step.settle()
                chain(V.scalar_tensor_tensor(wts[:, t, :], eexp[:, t, :], 1.0, chosen[:, t, :], ALU.mult, ALU.mult,
                                             accum_out=rt_a[:, t:t + 1]))
                chain(V.reciprocal(rt_b[:, t:t + 1], rt_a[:, t:t + 1]))
                chain(V.tensor_scalar(wts[:, t, :], wts[:, t, :], rt_b[:, t:t + 1], None, ALU.mult), wts_ready)
            wait_tile(dve, "rt")
            counts = tile("rt")[:, TT * E:TT * E + E]
            dve.wait_ge(numbers_ready, 1)
            chain(V.tensor_tensor(over[:], counts.unsqueeze(2).to_broadcast([P, E, T // SLOTS]),
                                  steps8[:].unsqueeze(1).to_broadcast([P, E, T // SLOTS]), ALU.is_gt))
            chain(V.tensor_reduce(blocks[:], over[:], AX.X, ALU.add))
            chain(V.tensor_tensor_scan(cum[:], ones[:, 0:E], blocks[:], 0.0, ALU.mult, ALU.add))
            chain(V.tensor_scalar(le[:], cum[0:MAXB + 1, :], number[0:MAXB + 1, :], None, ALU.is_le))
            chain(V.tensor_reduce(eofc[:], le[:], AX.X, ALU.add), eofc_ready)
            chain(V.tensor_tensor(cumx[:], cum[:], blocks[:], ALU.subtract))
            for t in range(TT):
                chain(V.scalar_tensor_tensor(slot_id[:, t, :], cumx[:], float(SLOTS), tile("rt")[:, t * E:(t + 1) * E],
                                             ALU.mult, ALU.add), out_dve if t == 1 else None)
                chain(V.scalar_tensor_tensor(slot_id[:, t, :], slot_id[:, t, :], 1.0, chosen[:, t, :], ALU.add, ALU.mult))
                chain(V.tensor_scalar(slot_id[:, t, :], slot_id[:, t, :], -1.0, None, ALU.add))
            wait_tile(dve, "te")
            chain(V.tensor_scalar(eof[:], tile("te")[0:1, 0:MAXB + 1], float(E - 1), None, ALU.min), out_dve)
            step(V.tensor_copy(table_e[:], eof[:]))
            step(V.tensor_scalar(need_w[:], eof[:], 16.0, 16.0, ALU.mult, ALU.add))
            chain(V.tensor_scalar(usedf[:], cumx[0:1, :], 1.0, None, ALU.add))
            step(V.tensor_copy(table_w[:], need_w[:]))
            step(V.tensor_copy(table_used[:], usedf[:]))
            chain(V.tensor_copy(table_n[:], cum[0:1, E - 1:E]), tables_ready)

            def select(e):
                for t in range(TT):
                    ins = V.tensor_scalar(sel[:, t, :], iota[:], slot_id[:, t, ds(e, 1)], None, ALU.is_equal)
                ins.then_inc(sel_ready, 1)

            def select_weights(e):
                for t in range(TT):
                    ins = V.tensor_scalar(selw[:, t, :, :], iota[:].unsqueeze(1).to_broadcast([P, 2, SLOTS]),
                                          slot_id[:, t, ds(e, 1)], wts[:, t, ds(e, 1)], ALU.is_equal, ALU.mult)
                ins.then_inc(selw_ready, 1)

            e0 = dve.value_load(table_e[0:1, 0:1], min_val=0, max_val=E - 1)
            select(e0)
            select_weights(e0)
            for n, s_ in enumerate(gu_used + dn_used + [bias_used]):
                step(V.memset(primer[:, n:n + 1], 0.0), s_)
            for i in range(4):
                t, half = divmod(i, 2)
                wait_tile(dve, f"bs{i}")
                step(V.tensor_copy(acc[:, t, 512 * half:512 * half + 512], tile(f"bs{i}")[:]), out_dve)
            step(V.memset(primer[:, 13:14], 0.0), acc_out)
            nb = dve.value_load(table_n[0:1, 0:1], min_val=1, max_val=MAXB)
            with dve.Fori(0, nb) as g:
                g1_ = dve.snap(g + 1)
                e = dve.value_load(table_e[0:1, ds(g + 1, 1)], min_val=0, max_val=E - 1)
                dve.wait_ge(gath_full, g1_)
                dve.wait_ge(selw_ready, g1_)
                V.tensor_scalar(iota[:], iota[:], float(SLOTS), None, ALU.add).then_inc(iota_ready, 1)
                dve.wait_ge(iota_ready, g1_)
                select(e)
                dve.wait_ge(gu_full, g1_)
                V.tensor_scalar(gcl[:], bank[0][:], LIMIT, None, ALU.min).then_inc(gcl_ready, 1)
                V.tensor_scalar(ucl[:], bank[1][:], LIMIT, -LIMIT, ALU.min, ALU.max).then_inc(ucl_ready, 1)
                dve.wait_ge(sig_ready, g1_)
                V.tensor_tensor(gcl[:], gcl[:], sig[:], ALU.mult).then_inc(gs_ready, 1)
                dve.wait_ge(gs_ready, g1_)
                V.scalar_tensor_tensor(act_t[:], ucl[:], 1.0, gcl[:], ALU.add, ALU.mult).then_inc(act_ready, 1)
                dve.wait_ge(selwT_full, g1_)
                select_weights(e)
                dve.wait_ge(sc_full, g1_)
                for t in range(TT):
                    for q in range(2):
                        dst = acc[:, t, 512 * q:512 * q + 512]
                        ins = V.tensor_tensor(dst, dst, sum_bank[t][q][:], ALU.add)
                ins.then_inc(acc_out, 1)
            dve.wait_ge(acc_out, dve.snap(nb + 1))
            for t in range(TT):
                chain(V.tensor_tensor(acc[:, t, :], acc[:, t, :], gt2[:], ALU.mult))
                chain(V.tensor_tensor(xs[:, t, :], xs[:, t, :], acc[:, t, :], ALU.add), add_done if t == 1 else None)
            inverse_root(TT, D, (fss_ready, TT), fvar_ready, froot_ready)
            dve.wait_ge(fg_in, 16)
            for j in range(4):
                dve.wait_ge(gu_in[j], 16 * E)
            for t in range(TT):
                step(V.scalar_tensor_tensor(final[:, t, :], xs[:, t, :], rs[:, t:t + 1], fgb[:], ALU.mult, ALU.mult), fin_ready)

        @block.tensor
        def _(pe):
            M = nc.tensor.matmul
            filled = [0]

            def begin(name):
                assert PLAN[filled[0]][0] == name, (PLAN[filled[0]][0], name)
                if filled[0] >= 8:
                    wait_out(pe, PLAN[filled[0] - 8][0])
                filled[0] += 1
                return tile(name)

            def full(ins):
                ins.then_inc(tile_full, 1)

            def arrived(kind, c):
                n = PIECE_NO[kind, c]
                pe.wait_ge(piece_in[n % NP2], 16 * (n // NP2 + 1))
                return piece[n % NP2]

            def modulation_part(name, a):
                w = arrived("ada", a)
                ps = begin(name)
                M(ps[0:32, :], pick[0:NA, a, :], bada[0:NA, :], start=True, stop=False)
                for r in range(2):
                    for q in range(4):
                        k = 4 * r + q
                        ins = M(ps[32 * q:32 * q + 32, :], silc[:, k, :], w[:, k, :], start=(r == 0 and q > 0), stop=(r == 1),
                                tile_position=(0, 32 * q))
                full(ins)

            def by_feature(kind, c, src):
                w = arrived(kind, c)
                for j in range(2):
                    ps = begin(f"{kind}{2 * c + j}")
                    for f in range(2):
                        for k in range(KT):
                            a = (2 * j + f) * P
                            ins = M(ps[:, f * T:(f + 1) * T], w[:, k, a:a + P], src[:, k, :], start=(k == 0), stop=(k == KT - 1))
                    full(ins)

            def by_token(kind, c, src):
                w = arrived(kind, c)
                for t in range(TT):
                    ps = begin(f"{kind}{2 * c + t}")
                    for k in range(KT):
                        ins = M(ps[:], src[:, k, t * P:(t + 1) * P], w[:, k, :], start=(k == 0), stop=(k == KT - 1))
                    full(ins)

            def transposes(name, src, t, half):
                ps = begin(name)
                for j in range(4):
                    a = (4 * half + j) * P
                    ins = nc.tensor.transpose(ps[:, j * P:(j + 1) * P], src[:, t, a:a + P], ident[:])
                full(ins)

            pe.wait_ge(consts_ready, 1)
            pe.wait_ge(bada_in, 16)
            pe.wait_ge(silc_ready, 1)

            def modulation_columns(ps, a, i):
                wait_out(pe, f"ada{i}")
                for f in range(4):
                    ins = M(ps[:, a + f:a + f + 1], modp[i][:, f * P:(f + 1) * P], inv32[:, 0:1], start=True, stop=True)
                return ins

            modulation_part("ada0", 0)
            modulation_part("ada1", 1)
            for i in range(4):
                t, half = divmod(i, 2)
                pe.wait_ge(xn_ready, t + 1)
                transposes(f"xT{i}", xn, t, half)
            modulation_part("ada2", 2)
            ps = begin("colA")
            for i in range(3):
                ins = modulation_columns(ps, 4 * i, i)
            full(ins)
            modulation_part("ada3", 3)
            full(modulation_columns(begin("colB"), 0, 3))
            for i in range(4):
                wait_out(pe, f"xT{i}")
            pe.wait_ge(wsm_in, 32)
            ps = begin("small")
            for half in range(2):
                for k in range(KT):
                    M(ps[half * 64:half * 64 + 64, 0:T], wsm[:, k, 0:IDX_DIM], hT[:, k, :], start=(k == 0), stop=(k == KT - 1))
            for k in range(KT):
                ins = M(ps[0:RANK, T:2 * T], wsm[:, k, IDX_DIM + IH:], hT[:, k, :], start=(k == 0), stop=(k == KT - 1))
            full(ins)
            ps = begin("wi")
            for t in range(TT):
                for k in range(KT):
                    ins = M(ps[:, t * IH:(t + 1) * IH], hT[:, k, t * P:(t + 1) * P], wsm[:, k, IDX_DIM:IDX_DIM + IH],
                            start=(k == 0), stop=(k == KT - 1))
            full(ins)
            by_feature("qi", 0, hT)
            pe.wait_ge(wgl_in, 16)
            wait_out(pe, "small")
            for i in range(2):
                ps = begin(f"z{i}")
                for j in range(2):
                    h = 2 * i + j
                    ins = M(ps[:, j * T:(j + 1) * T], wgl[:, h * P:(h + 1) * P], lrT[:], start=True, stop=True)
                full(ins)
            by_feature("qa", 0, hT)
            wait_out(pe, "qi1")
            def index_products(t, names, heads):
                w = P if t == 0 else T
                banks_ = []
                for name in names:
                    banks_.append(begin(name))
                for j in range(len(heads[0])):
                    for b_ in range(2):
                        h = heads[b_][j]
                        r = 64 * (h % 2)
                        ins = M(banks_[b_][:, j * w:(j + 1) * w], qiT[r:r + 64, h // 2, t * P:(t + 1) * P], kiT[r:r + 64, 0:w],
                                start=True, stop=True)
                        if j == len(heads[0]) - 1:
                            full(ins)
            index_products(0, ("sx0", "sx1"), ((0, 2, 4, 6), (1, 3, 5, 7)))
            index_products(1, ("sy0", "sy1"), ((0, 2), (1, 3)))
            index_products(1, ("sy2", "sy3"), ((4, 6), (5, 7)))
            by_feature("qa", 1, hT)
            by_feature("qb", 0, hT)
            by_feature("kb", 0, hT)
            by_feature("ka", 0, hT)
            for t in range(TT):
                ps = begin(f"kdT{t}")
                pe.wait_ge(kd_ready, 2)
                for h in range(GH):
                    ins = nc.tensor.transpose(ps[:, h * P:(h + 1) * P], kd[:, h, t * P:(t + 1) * P], ident[:])
                full(ins)
            ps = begin("AT")
            wait_out(pe, "kb1")
            for n in range(NCH):
                r = 64 * (n % 2)
                for h in range(GH):
                    a = (h * 2 + n // 2) * CHUNK
                    ins = M(ps[r:r + 64, a:a + CHUNK], ke[:, h, n * CHUNK:(n + 1) * CHUNK], qe[:, h, n * CHUNK:(n + 1) * CHUNK],
                            start=True, stop=True)
            full(ins)
            by_feature("ka", 1, hT)
            by_token("vb", 0, hT)
            by_token("vb", 1, hT)

            def state_step(n):
                cn = n - 1
                r, t = 64 * (cn % 2), cn // 2
                for half, name in enumerate((f"s{n}a", f"s{n}b")):
                    ps = begin(name)
                    for j in range(2):
                        h = 2 * half + j
                        ins = M(ps[:, j * DV:(j + 1) * DV], kdt[r:r + 64, t, h * P:(h + 1) * P], vb[r:r + 64, t, h * DV:(h + 1) * DV],
                                start=True, stop=True)
                    full(ins)

            wait_out(pe, "vb3")
            state_step(1)
            by_token("va", 0, hT)
            state_step(2)
            by_token("va", 1, hT)
            state_step(3)

            def logit_products(g):
                ps = begin(f"lg{g}")
                if g < 2:
                    t, w, heads = 0, P, range(4 * g, 4 * g + 4)
                else:
                    t, w, heads = 1, T, range(2 * (g - 2), 2 * (g - 2) + 2)
                for j, h in enumerate(heads):
                    ins = M(ps[:, j * w:(j + 1) * w], qaT[:, h, t * P:(t + 1) * P], kaT[:, h, 0:w], start=True, stop=True)
                full(ins)

            def prob_transposes(g):
                ps = begin(f"pt{g}")
                pe.wait_ge(prob_ready, g + 1)
                for j in range(4):
                    ins = nc.tensor.transpose(ps[:, j * P:(j + 1) * P], prob[g % 4][:, j * P:(j + 1) * P], ident[:])
                full(ins)

            def attend(i):
                ps = begin(f"ya{i}")
                t, half = divmod(i, 2)
                if t == 0:
                    wait_out(pe, f"pt{i}")
                    for j in range(4):
                        h = 4 * half + j
                        ins = M(ps[:, j * P:(j + 1) * P], va[:, 0, h * P:(h + 1) * P], probT[i][:, j * P:(j + 1) * P],
                                start=True, stop=True)
                else:
                    wait_out(pe, f"pt{3 + 2 * half}")
                    for j in range(4):
                        h = 4 * half + j
                        g = 2 + h // 2
                        for s_ in range(TT):
                            a = ((h % 2) * 2 + s_) * P
                            ins = M(ps[:, j * P:(j + 1) * P], va[:, s_, h * P:(h + 1) * P], probT[g % 4][:, a:a + P],
                                    start=(s_ == 0), stop=(s_ == TT - 1))
                full(ins)

            wait_out(pe, "va3")
            logit_products(0)
            logit_products(1)
            by_token("gb", 0, hT)
            prob_transposes(0)
            prob_transposes(1)
            logit_products(2)
            logit_products(3)
            attend(0)
            attend(1)
            logit_products(4)
            logit_products(5)
            by_token("gb", 1, hT)
            for g in range(2, 6):
                prob_transposes(g)
            pe.wait_ge(at_masked, 2)
            wait_out(pe, "s3b")
            for i in range(4):
                t, half = divmod(i, 2)
                ps = begin(f"o{i}")
                for n in (2 * t, 2 * t + 1):
                    r = 64 * (n % 2)
                    for j in range(2):
                        h = 2 * half + j
                        o_ = ps[r:r + 64, j * DV:(j + 1) * DV]
                        a = (h * 2 + n // 2) * CHUNK
                        ins = M(o_, AT[r:r + 64, a:a + CHUNK], vb[r:r + 64, t, h * DV:(h + 1) * DV], start=True, stop=(n == 0))
                        if n > 0:
                            ins = M(o_, qe[:, h, n * CHUNK:(n + 1) * CHUNK], S[n][:, h * DV:(h + 1) * DV], start=False, stop=True)
                full(ins)
            attend(2)
            attend(3)
            for cc in range(2):
                by_feature("ga", cc, hT)
            for i in range(4):
                t, half = divmod(i, 2)
                wait_out(pe, f"o{2 * t + 1}")
                transposes(f"yT{i}", yb, t, half)
            for cc in range(2):
                by_feature("gm", cc, hT)
            for r in range(8):
                modulation_part(f"ap{r}", 4 + r)
                ps = begin(f"ab{r}")
                wait_out(pe, f"ap{r}")
                full(M(ps[:], inv32[:], modq[r % 2][:], start=True, stop=True))
            for cc in range(2):
                by_feature("wa", cc, yaT)
            for cc in range(2):
                by_feature("wb", cc, ybT)
            pe.wait_ge(merged_ready, 4)
            for cc in range(2):
                by_token("wo", cc, mergedT)
            for i in range(4):
                t, half = divmod(i, 2)
                pe.wait_ge(h2_ready, i + 1)
                transposes(f"hh{i}", h2, t, half)
            ps = begin("rp")
            wait_out(pe, "hh3")
            pe.wait_ge(late_in, 48)
            for r in range(2):
                for q in range(4):
                    k = 4 * r + q
                    ins = M(ps[32 * q:32 * q + 32, 0:T], wr[:, k, :], h2T[:, k, :], start=(r == 0), stop=(r == 1))
            full(ins)
            ps = begin("rl")
            wait_out(pe, "rp")
            for t in range(TT):
                M(ps[:, t * E:(t + 1) * E], rpart[:, t * P:(t + 1) * P], stack[:], start=True, stop=False)
                ins = M(ps[:, t * E:(t + 1) * E], ones[0:1, :], rb[:], start=False, stop=True)
            full(ins)
            ps = begin("rt")
            pe.wait_ge(chosen_ready, TT)
            M(ps[:, 0:E], before[:], chosen[:, 0, :], start=True, stop=True)
            M(ps[:, E:2 * E], ones[:], chosen[:, 0, :], start=True, stop=False)
            M(ps[:, E:2 * E], before[:], chosen[:, 1, :], start=False, stop=True)
            M(ps[:, 2 * E:3 * E], ones[:], chosen[:, 0, :], start=True, stop=False)
            full(M(ps[:, 2 * E:3 * E], ones[:], chosen[:, 1, :], start=False, stop=True))
            ps = begin("te")
            pe.wait_ge(eofc_ready, 1)
            full(M(ps[0:1, 0:MAXB + 1], eofc[:], ident[0:MAXB + 1, 0:MAXB + 1], start=True, stop=True))

            ps = begin("wt")
            pe.wait_ge(wts_ready, TT)
            for t in range(TT):
                ins = nc.tensor.transpose(ps[0:E, t * P:(t + 1) * P], wts[:, t, :], ident[:])
            full(ins)
            pe.wait_ge(bd_in, 16)
            wait_out(pe, "wt")
            for i in range(4):
                t, half = divmod(i, 2)
                full(M(begin(f"bs{i}")[:], wT[:, t * P:(t + 1) * P], bd[:, 512 * half:512 * half + 512], start=True, stop=True))

            def gather(also=None):
                for t in range(TT):
                    for q in range(2):
                        ins = M(bank[2][64 * q:64 * q + 64, :], sel[:, t, :], h2[:, t, 512 * q:512 * q + 512],
                                start=(t == 0), stop=(t == TT - 1))
                        if also is not None and t == 0 and q == 0:
                            ins.then_inc(also, 1)
                ins.then_inc(gath_full, 1)

            def gather_transposes():
                for j in range(4):
                    ins = nc.tensor.transpose(bank[3][:, j * P:(j + 1) * P], gx[:, j * P:(j + 1) * P], ident[:])
                ins.then_inc(gxT_full, 1)

            wait_out(pe, "te")
            pe.wait_ge(sel_ready, 1)
            gather()
            pe.wait_ge(gx_out, 1)
            gather_transposes()
            pe.wait_ge(tables_ready, 1)
            nb = pe.value_load(table_n[0:1, 0:1], min_val=1, max_val=MAXB)
            with pe.Fori(0, nb) as g:
                g1_ = pe.snap(g + 1)
                g2_ = pe.snap(g + 2)
                landed = pe.value_load(table_w[0:1, ds(g, 1)], min_val=16, max_val=16 * E)
                pe.wait_ge(bgu_in, landed)
                pe.wait_ge(xg_out, g1_)
                for k in range(KT):
                    pe.wait_ge(gu_in[k], landed)
                    for u in range(2):
                        for q in range(2):
                            cols_ = slice(1024 * u + 512 * q, 1024 * u + 512 * q + 512)
                            ins = M(bank[u][64 * q:64 * q + 64, :], xg[:, k % 4, 64 * (k // 4):64 * (k // 4) + 64],
                                    gu_slot[k][:, cols_], start=(k == 0), stop=(k == KT - 1))
                    ins.then_inc(gu_used[k] if k < KT - 1 else gu_full, 1)
                    if k == 0:
                        for u in range(2):
                            for q in range(2):
                                cols_ = slice(1024 * u + 512 * q, 1024 * u + 512 * q + 512)
                                ins = M(bank[u][64 * q:64 * q + 64, :], ones[0:1, 0:SLOTS], bias_row[0:1, cols_],
                                        start=False, stop=False)
                        ins.then_inc(bias_used, 1)
                pe.wait_ge(sel_ready, g2_)
                gather(gu_used[KT - 1])
                pe.wait_ge(acc_out, g1_)
                pe.wait_ge(act_ready, g1_)
                for j in range(4):
                    ins = nc.tensor.transpose(bank[4][:, j * P:(j + 1) * P], act_t[:, j * P:(j + 1) * P], ident[:])
                ins.then_inc(actT_full, 1)
                pe.wait_ge(selw_ready, g1_)
                for t in range(TT):
                    ins = nc.tensor.transpose(bank[1][:, t * P:(t + 1) * P], selw[:, t, :, :].rearrange("p a s -> p (a s)"), ident[:])
                ins.then_inc(selwT_full, 1)
                pe.wait_ge(gx_out, g2_)
                gather_transposes()
                pe.wait_ge(actT_out, g1_)
                for f in range(KT):
                    if f % 2 == 0:
                        pe.wait_ge(dn_in[f // 2], landed)
                    for q in range(2):
                        ins = M(bank[5][64 * q:64 * q + 64, :], actT[:, f % 4, 64 * (f // 4):64 * (f // 4) + 64],
                                dn_slot[f // 2][:, f % 2, 512 * q:512 * q + 512], start=(f == 0), stop=(f == KT - 1))
                    if f % 2 == 1:
                        ins.then_inc(dn_used[f // 2] if f < KT - 1 else y_full, 1)
                pe.wait_ge(selw_out, g1_)
                pe.wait_ge(y_out, g1_)
                for t in range(TT):
                    for q in range(2):
                        ins = M(sum_bank[t][q][:], selwT[64 * q:64 * q + 64, t * P:(t + 1) * P], ysb[64 * q:64 * q + 64, :],
                                start=True, stop=True)
                        if t == 0 and q == 0:
                            ins.then_inc(dn_used[3], 1)
                ins.then_inc(sc_full, 1)


_INS = ['x', 'c', 'w_ada', 'b_ada', 'norm1_g', 'w_in', 'w_gate_lr', 'b_gate', 'gla_norm_g', 'w_branch_a', 'w_branch_b',
        'w_out', 'norm2_g', 'router_w', 'router_b', 'w_gate_up', 'b_gate_up', 'w_down', 'b_down', 'final_g']


def kernel(**inputs):
    import numpy as np
    import concourse.bacc as bacc
    from concourse.bass_utils import run_bass_kernel_spmd

    nc = bacc.Bacc("TRN2", target_bir_lowering=False, num_devices=1)
    arrays, args = {}, []
    for name in _INS:
        a = np.ascontiguousarray(inputs[name])
        arrays[f"in_{name}"] = a
        args.append(nc.dram_tensor(f"in_{name}", a.shape, mybir.dt.from_np(a.dtype), kind="ExternalInput").ap())
    out = nc.dram_tensor("out_0", inputs['x'].shape, F32, kind="ExternalOutput").ap()
    hybrid_block(nc, *args, out)
    r = run_bass_kernel_spmd(nc, [arrays], core_ids=[0])
    return r.results[0]["out_0"]
```

```python
from contextlib import ExitStack

import concourse.bass as bass
from concourse import mybir

F32 = mybir.dt.float32
I32 = mybir.dt.int32
BF16 = mybir.dt.bfloat16
ALU = mybir.AluOpType
ACT = mybir.ActivationFunctionType
AX = mybir.AxisListType
ds = bass.ds

P = 128
CHUNK = 64
EPS = 1e-6
IDX_DIM = 64
GATE_TAU = 16.0
TOP_K = 4
LIMIT = 7.0
ALPHA = 1.702
HIDDEN = -1.0e30
GONE = -3.0e38
PAD = -2.0e38
SLOTS = 64

PLAN = (
    [("ada0", "A"), ("ada1", "A"), ("xT0", "V"), ("xT1", "A"), ("xT2", "V"), ("xT3", "V"), ("ada2", "A")]
    + [("colA", "V"), ("ada3", "A"), ("colB", "V")]
    + [("small", "A"), ("qi0", "A"), ("qi1", "A"), ("wi", "A"), ("z0", "A"), ("z1", "A"), ("qa0", "A"), ("qa1", "A")]
    + [("sx0", "A"), ("sx1", "A")] + [(f"sy{i}", "A") for i in range(4)] + [("qa2", "A"), ("qa3", "A")]
    + [("qb0", "V"), ("qb1", "V"), ("kb0", "V"), ("kb1", "V"), ("ka0", "A"), ("ka1", "A")]
    + [("kdT0", "A"), ("kdT1", "A"), ("AT", "A"), ("ka2", "A"), ("ka3", "A")]
    + [(f"vb{i}", "A") for i in range(4)] + [("s1a", "V"), ("s1b", "V"), ("va0", "A"), ("va1", "A")]
    + [("s2a", "V"), ("s2b", "V"), ("va2", "A"), ("va3", "A"), ("s3a", "V"), ("s3b", "V")]
    + [("lg0", "V"), ("lg1", "V"), ("gb0", "V"), ("gb1", "V"), ("pt0", "A"), ("pt1", "A"), ("lg2", "V"), ("lg3", "V")]
    + [("ya0", "A"), ("ya1", "A"), ("lg4", "V"), ("lg5", "V"), ("gb2", "V"), ("gb3", "V")]
    + [(f"pt{i}", "A") for i in range(2, 6)] + [(f"o{i}", "V") for i in range(4)] + [("ya2", "A"), ("ya3", "A")]
    + [("ga0", "A"), ("ga1", "A"), ("ap0", "A"), ("ga2", "A"), ("ga3", "A"), ("ap1", "A"), ("ab0", "V")]
    + [(f"yT{i}", "A") for i in range(4)] + [("gm0", "A"), ("gm1", "A"), ("ap2", "A"), ("ab1", "V")]
    + [("gm2", "A"), ("gm3", "A"), ("ap3", "A"), ("ab2", "V"), ("wa0", "V"), ("wa1", "V"), ("ap4", "A"), ("ab3", "V")]
    + [("wa2", "V"), ("wa3", "V"), ("ap5", "A"), ("ab4", "V"), ("wb0", "V"), ("wb1", "V"), ("ap6", "A"), ("ab5", "V")]
    + [("wb2", "V"), ("wb3", "V"), ("ap7", "A"), ("ab6", "V"), ("wo0", "V"), ("wo1", "V"), ("ab7", "V"), ("wo2", "V"), ("wo3", "V")]
    + [(f"hh{i}", "A") for i in range(4)] + [("rp", "A"), ("rl", "V"), ("rt", "V"), ("te", "V"), ("wt", "A")]
)
NUMBER = {name: n for n, (name, _) in enumerate(PLAN)}
TAKER = dict(PLAN)
FIRST = ["ada0", "ada1", "ada2", "colA", "xT0", "xT2", "ada3", "colB", "xT1", "xT3"]
TAKEN = [(name, TAKER[name]) for name in FIRST] + PLAN[10:]
OUT_COUNT = {name: 1 + sum(1 for _, w in TAKEN[:n] if w == who) for n, (name, who) in enumerate(TAKEN)}

PIECES = (
    [("ada", i, f"ada{i}") for i in range(4)]
    + [("qi", 0, "qi1"), ("qa", 0, "qa1"), ("qa", 1, "qa3"), ("qb", 0, "qb1"), ("kb", 0, "kb1"), ("ka", 0, "ka1"),
       ("ka", 1, "ka3"), ("vb", 0, "vb1"), ("vb", 1, "vb3"), ("va", 0, "va1"), ("va", 1, "va3"), ("gb", 0, "gb1"),
       ("gb", 1, "gb3")]
    + [p for r, (kind, c) in enumerate((k, c) for k in ("ga", "gm", "wa", "wb") for c in range(2))
       for p in ((kind, c, f"{kind}{2 * c + 1}"), ("ada", 4 + r, f"ap{r}"))]
    + [("wo", 0, "wo1"), ("wo", 1, "wo3")]
)
PIECE_NO = {(kind, c): n for n, (kind, c, _) in enumerate(PIECES)}


def hybrid_block(nc, x, c, w_ada, b_ada, norm1_g, w_in, w_gate_lr, b_gate, gla_norm_g, w_branch_a, w_branch_b, w_out,
                 norm2_g, router_w, router_b, w_gate_up, b_gate_up, w_down, b_down, final_g, out):
    _, T, D = x.shape
    TT, KT = T // P, D // P
    H = D // P
    IH = 8
    GH = 4
    DV = D // GH
    NCH = T // CHUNK
    RANK = w_gate_lr.shape[1]
    E = w_gate_up.shape[1]
    MAXB = E + T * TOP_K // SLOTS
    NP2 = 4
    assert TT == 2 and KT == 8 and D // GH // 2 == P and w_gate_lr.shape[2] == GH * P and E == 32

    sizes = dict(qa=D, ka=D, va=D, qi=IH * IDX_DIM, ki=IDX_DIM, wi=IH, qb=GH * P, kb=GH * P, vb=D, gb=D, lr=RANK, ga=D, gm=D)
    col, at = {}, 0
    for name, n in sizes.items():
        col[name] = at
        at += n

    def columns(w, a, n):
        return w[0, :, a:a + n].rearrange("(k p) n -> p k n", p=P)

    def piece_source(kind, i):
        w = {"ada": w_ada, "wa": w_branch_a, "wb": w_branch_b, "wo": w_out}.get(kind, w_in)
        return columns(w, col.get(kind, 0) + 512 * i, 512)

    with ExitStack() as ctx:
        KB = 1024
        base = 16512

        def sb(name, at_kb, shape, dt=F32):
            return nc.alloc_sbuf_tensor_at(name, shape, dt, offset=base + int(at_kb * KB))

        def sem(name):
            return ctx.enter_context(nc.semaphore(name))

        piece = [sb(f"piece{i}", 16 * i, [P, KT, 512]) for i in range(NP2)]
        gu_slot = [sb(f"gu_slot{j}", 8 * j, [P, 2048]) for j in range(8)]
        dn_slot = [sb(f"dn_slot{j}", 64 + 8 * j, [P, 2, D]) for j in range(4)]
        bd = sb("bd", 96, [E, D])
        bias3 = sb("bias3", 100, [3 * E, 2 * D], BF16)
        vb = sb("vb", 64, [P, TT, D])
        G = sb("G", 72, [P, GH * T])
        qe = sb("qe", 76, [P, GH, T])
        ke = sb("ke", 80, [P, GH, T])
        kd = sb("kd", 84, [P, GH, T])
        kdt = sb("kdt", 88, [P, TT, GH * P])
        S = [None, sb("S1", 72, [P, GH * DV]), sb("S2", 84, [P, GH * DV]), sb("S3", 92, [P, GH * DV])]
        z = sb("z", 84, [P, GH * T])
        wiT = sb("wiT", 88, [IH, T])
        softp = sb("softp", 88, [P, GH * T])
        reset = sb("reset", 92, [P, GH * T])
        AT = sb("AT", 96, [P, 512])
        qiT = sb("qiT", 98, [P, IH // 2, T])
        kiT = sb("kiT", 102, [P, T])
        xs = sb("xs", 104, [P, TT, D])
        hT = sb("hT", 112, [P, KT, T])
        h2 = sb("h2", 112, [P, TT, D])
        modp = [sb(f"modp{i}", 120 + 2 * i, [P, 512]) for i in range(4)]
        qaT = sb("qaT", 120, [P, H, T])
        gaT = sb("gaT", 120, [P, KT, T])
        junk = sb("junk", 120, [P, D])
        kaT = sb("kaT", 128, [P, H, T])
        gmT = sb("gmT", 128, [P, KT, T])
        va = sb("va", 136, [P, TT, D])
        mergedT = sb("mergedT", 136, [P, KT, T])
        yb = sb("yb", 144, [P, TT, D])
        bgu = sb("bgu", 144, [3 * E, 2 * D])
        xn = sb("xn", 152, [P, TT, D])
        rel = [sb(f"rel{i}", 152 + 2 * i, [P, 512]) for i in range(2)]
        ojunk = sb("ojunk", 166, [P, DV])
        yaT = sb("yaT", 152, [P, H, T])
        ybT = sb("ybT", 160, [P, KT, T])
        h2T = sb("h2T", 160, [P, KT, T])
        wgl = sb("wgl", 160, [RANK, GH * P])
        wsm = sb("wsm", 162, [P, KT, P])
        lrT = sb("lrT", 167, [RANK, T])
        prob = [sb(f"prob{i}", 168 + 2 * i, [P, 512]) for i in range(4)]
        probT = [sb(f"probT{i}", 176 + 2 * i, [P, 512]) for i in range(4)]
        gt1 = sb("gt1", 168, [P, D])
        sc2g = sb("sc2g", 172, [P, D])
        sh2 = sb("sh2", 176, [P, D])
        gt2 = sb("gt2", 180, [P, D])
        score = [sb("score0", 184, [P, P]), sb("score1", 184.5, [P, T])]
        work = [[sb("work00", 185.5, [P, P]), sb("work01", 186, [P, P])],
                [sb("work10", 186.5, [P, T]), sb("work11", 187.5, [P, T])]]
        keep = [sb("keep0", 188.5, [P, P]), sb("keep1", 189, [P, T])]
        modq = [sb(f"modq{i}", 184 + 2 * i, [P, 512]) for i in range(2)]
        tmp = sb("tmp", 188, [P, 512])
        fgb = sb("fgb", 190, [P, D])
        ident = sb("ident", 194, [P, P])
        ones = sb("ones", 194.5, [P, P])
        inv32 = sb("inv32", 195, [P, P])
        stack = sb("stack", 197.0, [P, 32])
        before = sb("before", 195.5, [P, P])
        silc = sb("silc", 196, [P, KT, 32])
        gng = sb("gng", 200.75, [P, DV])
        wr = sb("wr", 201.75, [P, KT, E])
        rb = sb("rb", 202.75, [1, E])
        m_at = [203.0]

        def small(name, shape, dt=F32):
            n = 1
            for s in shape[1:]:
                n *= s
            t = sb(name, m_at[0], shape, dt)
            m_at[0] += (n * 4 + 31) // 32 * 32 / KB
            assert base + m_at[0] * KB <= 229368
            return t

        bcol = small("bcol", [P, 2 * KT])
        ccol = small("ccol", [P, KT])
        csig = small("csig", [P, KT])
        g1 = small("g1", [P, KT])
        gain1 = small("gain1", [P, KT])
        shift1 = small("shift1", [P, KT])
        wis = small("wis", [P, TT, IH])
        bg = small("bg", [P, GH])
        gsum = small("gsum", [P, GH, NCH])
        decay = small("decay", [P, GH, NCH])
        top8 = [small(f"top8_{i}", [P, 8]) for i in range(2)]
        mx = small("mx", [P, 24])
        nmx = small("nmx", [P, 24])
        esum = small("esum", [P, 24])
        erec = small("erec", [P, 24])
        sq = small("sq", [P, 8])
        sqe = small("sqe", [P, 8])
        root = small("root", [P, 8])
        rs = small("rs", [P, 8])
        rt_a = small("rt_a", [P, 8])
        rt_b = small("rt_b", [P, 8])
        lg = sb("lg", 184, [P, TT, E + TOP_K])
        lgw = sb("lgw", 184.5, [P, TT, E + TOP_K])
        r8 = sb("r8", 185, [P, TT, 8])
        nr8 = sb("nr8", 185.25, [P, TT])
        chosen = sb("chosen", 185.5, [P, TT, E])
        eexp = sb("eexp", 185.75, [P, TT, E])
        wts = sb("wts", 186, [P, TT, E])
        slot_id = sb("slot_id", 186.25, [P, TT, E])
        blocks = sb("blocks", 186.5, [P, E])
        blk_t = sb("blk_t", 186.75, [P, E])
        cum = sb("cum", 187, [P, E])
        cumx = sb("cumx", 187.25, [P, E])
        le = sb("le", 187.5, [MAXB + 1, E])
        eofc = sb("eofc", 187.75, [MAXB + 1, 1])
        eofw = sb("eofw", 177, [MAXB + 1, 3 * E])
        steps8 = small("steps8", [P, T // SLOTS])
        over = sb("over", 188.25, [P, E, T // SLOTS])
        rpart = sb("rpart", 176, [P, T])
        eof = small("eof", [1, MAXB + 1])
        need_w = small("need_w", [1, MAXB + 1])
        table_e = small("table_e", [1, MAXB + 1], I32)
        table_w = small("table_w", [1, MAXB + 1], I32)
        table_used = small("table_used", [1, E], I32)
        table_n = small("table_n", [1, 1], I32)
        number = small("number", [P, 1])
        expert_no = small("expert_no", [3 * E, 1])
        of_block = small("of_block", [3 * E, MAXB + 1])
        primer = small("primer", [P, 14])
        usedf = small("usedf", [1, E])
        iota = small("iota", [P, SLOTS])
        warm = small("warm", [P, 2])
        rowt = sb("rowt", 176, [P, TT, 512])
        xg = sb("xg", 128, [P, 4, P])
        gx = sb("gx", 130, [P, 512])
        gcl = sb("gcl", 132, [P, 512])
        sig = sb("sig", 134, [P, 512])
        ucl = sb("ucl", 136, [P, 512])
        act_t = sb("act_t", 138, [P, 512])
        actT = sb("actT", 140, [P, 4, P])
        ysb = sb("ysb", 142, [P, 512])
        sel = sb("sel", 144, [P, TT, SLOTS])
        selw = sb("selw", 144.5, [P, TT, 2, SLOTS])
        selwT = sb("selwT", 145.5, [P, T])
        wT = sb("wT", 147, [E, T])
        esel = sb("esel", 148, [3 * E, SLOTS], BF16)
        final = sb("final", 0, [P, TT, D])
        junk2 = sb("junk2", 132, [P, D])

        bank = [ctx.enter_context(nc.psum_tensor(f"bank{i}", [P, 512], F32)) for i in range(8)]

        sum_bank = [[bank[6], bank[7]], [bank[4], bank[5]]]

        tile_full = sem("tile_full")
        out_act = sem("out_act")
        out_dve = sem("out_dve")
        piece_in = [sem(f"piece_in{i}") for i in range(NP2)]
        x_in, c_in, g1_in, bcol_in, wsm_in, wgl_in, misc_in, late_in = (
            sem(n) for n in ("x_in", "c_in", "g1_in", "bcol_in", "wsm_in", "wgl_in", "misc_in", "late_in"))
        g2_in, fg_in, brow_in = sem("g2_in"), sem("fg_in"), sem("brow_in")
        pool_step, dve_step, act_step = sem("pool_step"), sem("dve_step"), sem("act_step")
        consts_ready = sem("consts_ready")
        gain1_ready = sem("gain1_ready")
        csig_ready, silc_ready, xss_ready, xvar_ready, xroot_ready, xn_ready = (
            sem(n) for n in ("csig_ready", "silc_ready", "xss_ready", "xvar_ready", "xroot_ready", "xn_ready"))
        softp_ready, gsum_ready, gexp_ready, gdiff_ready, gdec_ready, kd_ready = (
            sem(n) for n in ("softp_ready", "gsum_ready", "gexp_ready", "gdiff_ready", "gdec_ready", "kd_ready"))
        rel_used, at_masked, s_ready = sem("rel_used"), sem("at_masked"), sem("s_ready")
        nmx_ready, exp_ready, prob_ready, gsig_ready = sem("nmx_ready"), sem("exp_ready"), sem("prob_ready"), sem("gsig_ready")
        oss_ready, ovar_ready, oroot_ready, yb_ready = (sem(n) for n in ("oss_ready", "ovar_ready", "oroot_ready", "yb_ready"))
        merged_ready, x2_ready, x2ss_ready, x2var_ready, x2root_ready, h2_ready = (
            sem(n) for n in ("merged_ready", "x2_ready", "x2ss_ready", "x2var_ready", "x2root_ready", "h2_ready"))
        eofc_ready = sem("eofc_ready")
        rneg_ready, rexp_ready, chosen_ready, wts_ready, tables_ready = (
            sem(n) for n in ("rneg_ready", "rexp_ready", "chosen_ready", "wts_ready", "tables_ready"))
        gu_in = [sem(f"gu_in{j}") for j in range(8)]
        dn_in = [sem(f"dn_in{j}") for j in range(4)]
        bgu_in, bd_in = sem("bgu_in"), sem("bd_in")
        gu_used = [sem(f"gu_used{j}") for j in range(8)]
        dn_used = [sem(f"dn_used{j}") for j in range(3)]
        bias3_ready = sem("bias3_ready")
        row_scaled, row_added = [sem(f"row_scaled{q}") for q in range(2)], sem("row_added")
        sel_ready, gath_full, gx_out, gxT_full, xg_out = (
            sem(n) for n in ("sel_ready", "gath_full", "gx_out", "gxT_full", "xg_out"))
        selw_ready, selwT_full, selw_out = sem("selw_ready"), sem("selwT_full"), sem("selw_out")
        gu_full, gcl_ready, ucl_ready, sig_ready, gs_ready, act_ready = (
            sem(n) for n in ("gu_full", "gcl_ready", "ucl_ready", "sig_ready", "gs_ready", "act_ready"))
        actT_full, actT_out, y_full, y_out, sc_full, acc_out = (
            sem(n) for n in ("actT_full", "actT_out", "y_full", "y_out", "sc_full", "acc_out"))
        numbers_ready = sem("numbers_ready")
        iota_ready, add_done, last_full = sem("iota_ready"), sem("add_done"), sem("last_full")
        fss_ready, fvar_ready, froot_ready, fin_ready, stored = (
            sem(n) for n in ("fss_ready", "fvar_ready", "froot_ready", "fin_ready", "stored"))

        def tile(name):
            return bank[NUMBER[name] % 8]

        def wait_tile(eng, name):
            eng.wait_ge(tile_full, NUMBER[name] + 1)

        def wait_out(eng, name):
            eng.wait_ge(out_act if TAKER[name] == "A" else out_dve, OUT_COUNT[name])

        class Steps:

            def __init__(self, eng, own):
                self.eng, self.own, self.count, self.last = eng, own, {}, None

            def __call__(self, ins, signal=None):
                signal = signal or self.own
                ins.then_inc(signal, 1)
                self.count[signal.name] = self.count.get(signal.name, 0) + 1
                self.last = (signal, self.count[signal.name])

            def settle(self):
                self.eng.wait_ge(*self.last)

        block = ctx.enter_context(nc.Block())

        @block.sync
        def _(sp):
            def load_expert_piece(e, j):
                if j < 8:
                    sp.dma_start(gu_slot[j][:], w_gate_up[0, e, j * P:(j + 1) * P, :] if isinstance(e, int) else
                                 w_gate_up[0, ds(e, 1), j * P:(j + 1) * P, :].rearrange("a p n -> p (a n)")).then_inc(gu_in[j], 16)
                else:
                    i = j - 8
                    rows = slice(2 * i * P, 2 * (i + 1) * P)
                    sp.dma_start(dn_slot[i][:], w_down[0, e, rows, :].rearrange("(i p) n -> p i n", p=P) if isinstance(e, int) else
                                 w_down[0, ds(e, 1), rows, :].rearrange("a (i p) n -> p (a i) n", p=P)).then_inc(dn_in[i], 16)

            for n, (kind, i, last) in enumerate(PIECES):
                if n >= NP2:
                    wait_tile(sp, PIECES[n - NP2][2])
                sp.dma_start(piece[n % NP2][:], piece_source(kind, i)).then_inc(piece_in[n % NP2], 16)
                if kind in ("wa", "wb"):
                    wait_tile(sp, "o3")
                    load_expert_piece(0, 8 + 2 * (kind == "wb") + i)
            for j in range(8):
                user = [last for n, (_, _, last) in enumerate(PIECES) if n % NP2 == j // 2][-1]
                wait_tile(sp, user)
                load_expert_piece(0, j)
            sp.wait_ge(tables_ready, 1)
            with sp.Fori(1, E) as e:
                free = sp.value_load(table_used[0:1, ds(e, 1)], min_val=1, max_val=MAXB + 1)
                for j in range(12):
                    here, used = (gu_in[j], gu_used[j]) if j < 8 else (dn_in[j - 8], (dn_used + [y_full])[j - 8])
                    sp.wait_ge(here, 16 * e)
                    sp.wait_ge(used, free)
                    load_expert_piece(e, j)
            for t in range(TT):
                sp.wait_ge(fin_ready, t + 1)
                sp.dma_start(out[0, t * P:(t + 1) * P, :], final[:, t, :]).then_inc(stored, 16)
            sp.wait_ge(stored, 16 * TT)

        @block.gpsimd
        def _(pool):
            step = Steps(pool, pool_step)
            step(nc.gpsimd.memset(ident[:], 0.0))
            step(nc.gpsimd.memset(ones[:], 1.0))
            step(nc.gpsimd.memset(inv32[:], 1.0 / 32))
            step(nc.gpsimd.memset(stack[:], 0.0))
            step(nc.gpsimd.iota(iota[:], [[1, SLOTS]], base=0, channel_multiplier=0, allow_small_or_imprecise_dtypes=True))
            step.settle()
            step(nc.gpsimd.affine_select(out=ident[:], in_=ident[:], compare_op=ALU.not_equal, fill=1.0, base=0,
                                         pattern=[[-1, P]], channel_multiplier=1))
            for q in range(4):
                v = stack[32 * q:32 * q + 32, :]
                step.settle()
                step(nc.gpsimd.affine_select(out=v, in_=v, compare_op=ALU.not_equal, fill=1.0, base=0,
                                             pattern=[[-1, 32]], channel_multiplier=1))
            step.settle()
            step(nc.gpsimd.affine_select(out=before[:], in_=ones[:], compare_op=ALU.is_gt, fill=0.0, base=0,
                                         pattern=[[1, P]], channel_multiplier=-1))
            step(nc.gpsimd.memset(reset[:], 1.0))
            step.settle()
            step(nc.gpsimd.memset(reset[:].rearrange("p (c i) -> p c i", i=CHUNK)[:, :, 0:1], 0.0), consts_ready)
            wait_out(pool, "AT")
            for half in range(2):
                v = AT[64 * half:64 * half + 64, :].rearrange("p (c i) -> p c i", i=CHUNK)
                step(nc.gpsimd.affine_select(out=v, in_=v, compare_op=ALU.is_ge, fill=0.0, base=0,
                                             pattern=[[0, 2 * GH], [1, CHUNK]], channel_multiplier=-1), at_masked)
            wait_tile(pool, "ya3")
            pool.dma_start(sc2g[:], norm2_g[0:1, :].to_broadcast([P, D])).then_inc(g2_in, 16)
            for part, dst in ((2, gt1), (3, sh2), (5, gt2), (4, fgb)):
                pool.dma_start(dst[:], b_ada[0:1, part * D:(part + 1) * D].to_broadcast([P, D])).then_inc(brow_in, 16)
            wait_tile(pool, "yT3")
            for i in range(3):
                pool.dma_start(bgu[E * i:E * (i + 1), :], b_gate_up[0]).then_inc(bgu_in, 16)
            pool.dma_start(bd[:], b_down[0]).then_inc(bd_in, 16)
            wait_out(pool, "ab5")
            pool.dma_start(fgb[:], final_g.rearrange("(a n) -> a n", a=1).to_broadcast([P, D])).then_inc(fg_in, 16)
            step(nc.gpsimd.iota(steps8[:], [[SLOTS, T // SLOTS]], base=0, channel_multiplier=0,
                                allow_small_or_imprecise_dtypes=True))
            for i in range(3):
                step(nc.gpsimd.iota(expert_no[E * i:E * (i + 1), :], [[0, 1]], base=0, channel_multiplier=1,
                                    allow_small_or_imprecise_dtypes=True))
                step.settle()
            step(nc.gpsimd.iota(number[:], [[0, 1]], base=0, channel_multiplier=1,
                                allow_small_or_imprecise_dtypes=True), numbers_ready)

        @block.scalar
        def _(act):
            step = Steps(act, act_step)
            A = nc.scalar.activation

            act.dma_start(ccol[:], c[0].rearrange("(k p) -> p k", p=P), allow_slow_non_contiguous=True).then_inc(c_in, 16)
            act.dma_start(xs[:], x[0].rearrange("(t p) n -> p t n", p=P)).then_inc(x_in, 16)
            act.dma_start(bcol[:], b_ada[0, 0:2 * D].rearrange("(k p) -> p k", p=P), allow_slow_non_contiguous=True).then_inc(bcol_in, 16)
            act.dma_start(g1[:], norm1_g[0].rearrange("(k p) -> p k", p=P), allow_slow_non_contiguous=True).then_inc(g1_in, 16)
            act.dma_start(wsm[:, :, 0:96], columns(w_in, col["ki"], 96)).then_inc(wsm_in, 16)
            act.dma_start(wsm[:, :, 96:P], columns(w_in, col["lr"], 32)).then_inc(wsm_in, 16)
            act.dma_start(wgl[:], w_gate_lr[0]).then_inc(wgl_in, 16)
            act.dma_start(bg[:], b_gate[0].rearrange("(h p) -> p h", p=P), allow_slow_non_contiguous=True).then_inc(misc_in, 16)
            act.dma_start(gng[:], gla_norm_g[0:1, :].to_broadcast([P, DV])).then_inc(late_in, 16)
            act.dma_start(wr[:], router_w[0].rearrange("(k p) n -> p k n", p=P)).then_inc(late_in, 16)
            act.dma_start(rb[:], router_b[0:1, :]).then_inc(late_in, 16)

            def take(name, *ops):
                wait_tile(act, name)
                for n, (o, i, f, kw) in enumerate(ops):
                    ins = A(o, i, f, **kw)
                    if n == len(ops) - 1:
                        step(ins, out_act)
                    else:
                        step(ins)

            act.wait_ge(c_in, 16)
            step(A(csig[:], ccol[:], ACT.Sigmoid), csig_ready)
            act.wait_ge(x_in, 16)
            for t in range(TT):
                step(A(xn[:, t, :], xs[:, t, :], ACT.Square, accum_out=sq[:, t:t + 1]), xss_ready)
            act.wait_ge(xvar_ready, 1)
            step(A(root[:, 0:TT], sqe[:, 0:TT], ACT.Sqrt), xroot_ready)

            for i in range(4):
                take(f"ada{i}", (modp[i][:], tile(f"ada{i}")[:], ACT.Copy, {}))
            act.wait_ge(gain1_ready, 1)
            take("xT1", *[(hT[:, k, 0:P], tile("xT1")[:, (k % 4) * P:(k % 4 + 1) * P], ACT.Identity,
                           dict(scale=gain1[:, k:k + 1], bias=shift1[:, k:k + 1])) for k in range(4, 8)])
            take("small", (kiT[0:64, :], tile("small")[0:64, 0:T], ACT.Copy, {}),
                 (kiT[64:P, :], tile("small")[0:64, 0:T], ACT.Copy, {}),
                 (wiT[:], tile("small")[64:64 + IH, 0:T], ACT.Copy, dict(scale=float(IH) ** -0.5)),
                 (lrT[:], tile("small")[96:96 + RANK, 0:T], ACT.Copy, {}))
            for i in range(2):
                take(f"qi{i}", (qiT[:, 2 * i:2 * i + 2, :].rearrange("p a b -> p (a b)"), tile(f"qi{i}")[:], ACT.Copy,
                                dict(scale=IDX_DIM ** -0.5)))
            take("wi", (wis[:].rearrange("p t h -> p (t h)"), tile("wi")[:, 0:TT * IH], ACT.Copy, {}))
            act.wait_ge(misc_in, 16)
            for i in range(2):
                take(f"z{i}", *[(z[:, (2 * i + j) * T:(2 * i + j + 1) * T], tile(f"z{i}")[:, j * T:(j + 1) * T], ACT.Identity,
                                 dict(bias=bg[:, 2 * i + j:2 * i + j + 1])) for j in range(2)])
            step.settle()
            step(A(softp[:], z[:], ACT.Abs))
            step.settle()
            step(A(softp[:], softp[:], ACT.Exp, scale=-1.0))
            step.settle()
            step(A(softp[:], softp[:], ACT.Ln, bias=1.0), softp_ready)

            def take_qk(dst, kind, i):
                take(f"{kind}{i}", (dst[:, 2 * i:2 * i + 2, :].rearrange("p a b -> p (a b)"), tile(f"{kind}{i}")[:], ACT.Copy, {}))

            def take_rows(dst, kind, i):
                cc, t = divmod(i, TT)
                take(f"{kind}{i}", (dst[:, t, 512 * cc:512 * cc + 512], tile(f"{kind}{i}")[:], ACT.Copy, {}))

            take_qk(qaT, "qa", 0)
            take_qk(qaT, "qa", 1)
            for n, name in enumerate(["sx0", "sx1", "sy0", "sy1", "sy2", "sy3"]):
                if n >= 2:
                    act.wait_ge(rel_used, n - 1)
                take(name, (rel[n % 2][:], tile(name)[:], ACT.Relu, {}))
            take_qk(qaT, "qa", 2)
            take_qk(qaT, "qa", 3)
            act.wait_ge(gsum_ready, 1)
            step(A(qe[:].rearrange("p h t -> p (h t)"), G[:], ACT.Exp, scale=1.0 / GATE_TAU))
            step(A(ke[:].rearrange("p h t -> p (h t)"), G[:], ACT.Exp, scale=-1.0 / GATE_TAU), gexp_ready)
            act.wait_ge(gdiff_ready, 1)
            step(A(softp[:], softp[:], ACT.Exp, scale=1.0 / GATE_TAU))
            step(A(decay[:].rearrange("p h n -> p (h n)"), gsum[:].rearrange("p h n -> p (h n)"), ACT.Exp,
                   scale=1.0 / GATE_TAU), gdec_ready)
            take_qk(kaT, "ka", 0)
            take_qk(kaT, "ka", 1)
            for t in range(TT):
                take(f"kdT{t}", (kdt[:, t, :], tile(f"kdT{t}")[:], ACT.Copy, {}))
            take("AT", (AT[:], tile("AT")[:], ACT.Copy, {}))
            take_qk(kaT, "ka", 2)
            take_qk(kaT, "ka", 3)
            for i in range(4):
                take_rows(vb, "vb", i)
            for i in range(4):
                take_rows(va, "va", i)

            def exps(g):
                n, w = (4, P) if g < 2 else (2, 2 * P)
                act.wait_ge(nmx_ready, g + 1)
                for j in range(n):
                    ins = A(prob[g % 4][:, j * w:(j + 1) * w], prob[g % 4][:, j * w:(j + 1) * w], ACT.Exp,
                            bias=nmx[:, 4 * g + j:4 * g + j + 1], accum_out=esum[:, 4 * g + j:4 * g + j + 1])
                    step(ins, exp_ready if j == n - 1 else None)

            def gate_sig(i):
                cc, t = divmod(i, TT)
                wait_tile(act, f"gb{i}")
                step(A(yb[:, t, 512 * cc:512 * cc + 512], tile(f"gb{i}")[:], ACT.Sigmoid), gsig_ready)

            def take_probT(g):
                if g >= 4:
                    wait_tile(act, f"ya{g - 4}")
                take(f"pt{g}", (probT[g % 4][:], tile(f"pt{g}")[:], ACT.Copy, {}))

            def take_ya(i):
                t, half = divmod(i, 2)
                take(f"ya{i}", (yaT[:, 4 * half:4 * half + 4, t * P:(t + 1) * P],
                                tile(f"ya{i}")[:].rearrange("p (h q) -> p h q", h=4), ACT.Copy, {}))

            exps(0)
            exps(1)
            gate_sig(0)
            gate_sig(1)
            take_probT(0)
            take_probT(1)
            exps(2)
            exps(3)
            take_ya(0)
            take_ya(1)
            exps(4)
            exps(5)
            gate_sig(2)
            gate_sig(3)
            for g in range(2, 6):
                take_probT(g)
            for i in range(4):
                wait_tile(act, f"o{i}")
                for j in range(2):
                    step(A(ojunk[:], tile(f"o{i}")[:, j * DV:(j + 1) * DV], ACT.Square,
                           accum_out=sq[:, 2 * i + j:2 * i + j + 1]), oss_ready)
                    step.settle()
            act.wait_ge(ovar_ready, 1)
            step(A(root[:], sqe[:], ACT.Sqrt), oroot_ready)
            take_ya(2)
            take_ya(3)

            def take_sig(dst, kind, i):
                take(f"{kind}{i}", (dst[:, 2 * i:2 * i + 2, :].rearrange("p a b -> p (a b)"), tile(f"{kind}{i}")[:], ACT.Sigmoid, {}))

            def take_T(dst, kind, i):
                t, half = divmod(i, 2)
                take(f"{kind}{i}", (dst[:, 4 * half:4 * half + 4, t * P:(t + 1) * P],
                                    tile(f"{kind}{i}")[:].rearrange("p (h q) -> p h q", h=4), ACT.Copy, {}))

            def take_part(r):
                if r >= 2:
                    wait_tile(act, f"ab{r - 2}")
                take(f"ap{r}", (modq[r % 2][:], tile(f"ap{r}")[:], ACT.Copy, {}))

            take_sig(gaT, "ga", 0)
            take_sig(gaT, "ga", 1)
            take_part(0)
            take_sig(gaT, "ga", 2)
            take_sig(gaT, "ga", 3)
            take_part(1)
            for i in range(4):
                take_T(ybT, "yT", i)
            take_sig(gmT, "gm", 0)
            take_sig(gmT, "gm", 1)
            take_part(2)
            take_sig(gmT, "gm", 2)
            take_sig(gmT, "gm", 3)
            for r in range(3, 8):
                take_part(r)
            step(A(warm[:, 0:1], ident[:, 0:1], ACT.Sqrt))
            for i in range(4):
                cc, t = divmod(i, TT)
                act.wait_ge(x2_ready, i + 1)
                step.settle()
                step(A(junk[:, 0:512], xs[:, t, 512 * cc:512 * cc + 512], ACT.Square, accum_out=sq[:, 2 * cc + t:2 * cc + t + 1]),
                     x2ss_ready)
                if cc == 1:
                    act.wait_ge(x2var_ready, t + 1)
                    step(A(root[:, t:t + 1], sqe[:, t:t + 1], ACT.Sqrt), x2root_ready)
            step(A(warm[:, 1:2], ident[:, 0:1], ACT.Exp))
            for i in range(4):
                take_T(h2T, "hh", i)
            take("rp", (rpart[:], tile("rp")[:, 0:T], ACT.Copy, {}))
            act.wait_ge(rneg_ready, 1)
            for t in range(TT):
                step(A(eexp[:, t, :], lg[:, t, 0:E], ACT.Exp, bias=nr8[:, t:t + 1]), rexp_ready)

            take("wt", (wT[:], tile("wt")[0:E, 0:T], ACT.Copy, {}))

            act.wait_ge(gath_full, 1)
            step(A(gx[:], bank[2][:], ACT.Copy), gx_out)
            act.wait_ge(gxT_full, 1)
            step(A(xg[:].rearrange("p j s -> p (j s)"), bank[3][:], ACT.Copy), xg_out)
            act.wait_ge(tables_ready, 1)
            nb = act.value_load(table_n[0:1, 0:1], min_val=1, max_val=MAXB)
            with act.Fori(0, nb) as g:
                g1_ = act.snap(g + 1)
                g2_ = act.snap(g + 2)
                act.wait_ge(gcl_ready, g1_)
                A(sig[:], gcl[:], ACT.Sigmoid, scale=ALPHA).then_inc(sig_ready, 1)
                act.wait_ge(gath_full, g2_)
                A(gx[:], bank[2][:], ACT.Copy).then_inc(gx_out, 1)
                act.wait_ge(gxT_full, g2_)
                A(xg[:].rearrange("p j s -> p (j s)"), bank[3][:], ACT.Copy).then_inc(xg_out, 1)
                act.wait_ge(actT_full, g1_)
                A(actT[:].rearrange("p c s -> p (c s)"), bank[4][:], ACT.Copy).then_inc(actT_out, 1)
                act.wait_ge(selwT_full, g1_)
                A(selwT[:], bank[1][:, 0:T], ACT.Copy).then_inc(selw_out, 1)
                act.wait_ge(y_full, g2_)
                A(ysb[:], bank[5][:], ACT.Copy).then_inc(y_out, 1)
            step(A(warm[:, 0:1], ident[:, 0:1], ACT.Sqrt))
            for t in range(TT):
                act.wait_ge(add_done, t + 1)
                step(A(junk2[:], xs[:, t, :], ACT.Square, accum_out=sq[:, t:t + 1]), fss_ready)
                step.settle()
            act.wait_ge(fvar_ready, 1)
            step(A(root[:, 0:TT], sqe[:, 0:TT], ACT.Sqrt), froot_ready)

        @block.vector
        def _(dve):
            V = nc.vector
            step = Steps(dve, dve_step)

            def chain(ins, signal=None):
                step(ins, signal)
                step.settle()

            def inverse_root(n, count, seen, var_ready, root_ready, first=0):
                c_ = slice(first, first + n)
                dve.wait_ge(*seen)
                chain(V.tensor_scalar(sqe[:, c_], sq[:, c_], 1.0 / count, EPS, ALU.mult, ALU.add), var_ready)
                dve.wait_ge(root_ready, 1 if n > 1 else first + 1)
                chain(V.reciprocal(rt_a[:, c_], root[:, c_]))
                chain(V.tensor_tensor(rt_b[:, c_], rt_a[:, c_], rt_a[:, c_], ALU.mult))
                chain(V.tensor_tensor(rt_b[:, c_], rt_b[:, c_], sqe[:, c_], ALU.mult))
                chain(V.tensor_scalar(rt_b[:, c_], rt_b[:, c_], -0.5, 1.5, ALU.mult, ALU.add))
                chain(V.tensor_tensor(rs[:, c_], rt_a[:, c_], rt_b[:, c_], ALU.mult))

            dve.wait_ge(csig_ready, 1)
            chain(V.tensor_tensor(csig[:], csig[:], ccol[:], ALU.mult))
            step(V.tensor_copy(silc[:], csig[:].unsqueeze(2).to_broadcast([P, KT, 32])), silc_ready)
            inverse_root(TT, D, (xss_ready, TT), xvar_ready, xroot_ready)
            for t in range(TT):
                step(V.tensor_scalar(xn[:, t, :], xs[:, t, :], rs[:, t:t + 1], None, ALU.mult), xn_ready)
            dve.wait_ge(g1_in, 16)
            dve.wait_ge(bcol_in, 16)
            chain(V.tensor_scalar(bcol[:, KT:2 * KT], bcol[:, KT:2 * KT], 1.0, None, ALU.add))
            wait_tile(dve, "colA")
            step(V.tensor_tensor(shift1[:], tile("colA")[:, 0:KT], bcol[:, 0:KT], ALU.add))
            chain(V.tensor_tensor(gain1[:, 0:4], tile("colA")[:, KT:KT + 4], bcol[:, KT:KT + 4], ALU.add), out_dve)
            chain(V.tensor_tensor(gain1[:, 0:4], gain1[:, 0:4], g1[:, 0:4], ALU.mult))

            def take_xT(i):
                t, half = divmod(i, 2)
                wait_tile(dve, f"xT{i}")
                for j in range(4):
                    k = 4 * half + j
                    step(V.tensor_scalar(hT[:, k, t * P:(t + 1) * P], tile(f"xT{i}")[:, j * P:(j + 1) * P],
                                         gain1[:, k:k + 1], shift1[:, k:k + 1], ALU.mult, ALU.add), out_dve if j == 3 else None)

            take_xT(0)
            take_xT(2)
            wait_tile(dve, "colB")
            chain(V.tensor_tensor(gain1[:, 4:8], tile("colB")[:, 0:4], bcol[:, KT + 4:2 * KT], ALU.add), out_dve)
            chain(V.tensor_tensor(gain1[:, 4:8], gain1[:, 4:8], g1[:, 4:8], ALU.mult), gain1_ready)
            take_xT(3)
            dve.wait_ge(softp_ready, 1)
            dve.wait_ge(consts_ready, 1)
            chain(V.scalar_tensor_tensor(z[:], z[:], 0.0, softp[:], ALU.min, ALU.subtract))
            chain(V.tensor_tensor_scan(G[:], reset[:], z[:], 0.0, ALU.mult, ALU.add))
            Gc = G[:].rearrange("p (c i) -> p c i", i=CHUNK)
            chain(V.tensor_copy(gsum[:].rearrange("p h n -> p (h n)").unsqueeze(2), Gc[:, :, CHUNK - 1:CHUNK]), gsum_ready)
            step(V.tensor_tensor(softp[:].rearrange("p (c i) -> p c i", i=CHUNK),
                                 gsum[:].rearrange("p h n -> p (h n)").unsqueeze(2).to_broadcast([P, GH * NCH, CHUNK]), Gc,
                                 ALU.subtract), gdiff_ready)

            plan = [("sx0", 0, (0, 2, 4, 6)), ("sx1", 0, (1, 3, 5, 7)),
                    ("sy0", 1, (0, 2)), ("sy1", 1, (1, 3)), ("sy2", 1, (4, 6)), ("sy3", 1, (5, 7))]
            fresh = {0: True, 1: True}
            for n, (name, t, heads) in enumerate(plan):
                w = P if t == 0 else T
                wait_out(dve, name)
                if n == 0:
                    wait_out(dve, "wi")
                for j, h in enumerate(heads):
                    src, wcol = rel[n % 2][:, j * w:(j + 1) * w], wis[:, t, h:h + 1]
                    sig_ = rel_used if j == len(heads) - 1 else None
                    if fresh[t]:
                        chain(V.tensor_scalar(score[t][:], src, wcol, None, ALU.mult), sig_)
                        fresh[t] = False
                    else:
                        chain(V.scalar_tensor_tensor(score[t][:], src, wcol, score[t][:], ALU.mult, ALU.add), sig_)
            for t in range(TT):
                first = 2 * t * CHUNK + CHUNK
                chain(V.memset(score[t][0:CHUNK, first:first + CHUNK], HIDDEN))
            for t in range(TT):
                src = score[t]
                for r in range(CHUNK // 8):
                    dst = work[t][r % 2]
                    chain(V.max(top8[r % 2][:], src[:]))
                    chain(V.match_replace(dst[:], top8[r % 2][:], src[:], GONE))
                    src = dst
                chain(V.tensor_scalar(keep[t][:], src[:], GONE, HIDDEN, ALU.not_equal, ALU.mult))

            dve.wait_ge(gexp_ready, 1)
            for i in range(2):
                wait_tile(dve, f"qb{i}")
                step(V.scalar_tensor_tensor(qe[:, 2 * i:2 * i + 2, :], tile(f"qb{i}")[:].rearrange("p (h t) -> p h t", h=2),
                                            float(P) ** -0.5, qe[:, 2 * i:2 * i + 2, :], ALU.mult, ALU.mult), out_dve)
            dve.wait_ge(gdec_ready, 1)
            for i in range(2):
                wait_tile(dve, f"kb{i}")
                step(V.tensor_tensor(kd[:, 2 * i:2 * i + 2, :], tile(f"kb{i}")[:].rearrange("p (h t) -> p h t", h=2),
                                     softp[:].rearrange("p (h t) -> p h t", h=GH)[:, 2 * i:2 * i + 2, :], ALU.mult), kd_ready)
                step(V.tensor_tensor(ke[:, 2 * i:2 * i + 2, :], tile(f"kb{i}")[:].rearrange("p (h t) -> p h t", h=2),
                                     ke[:, 2 * i:2 * i + 2, :], ALU.mult), out_dve)

            def state(n):
                for half, name in enumerate((f"s{n}a", f"s{n}b")):
                    wait_tile(dve, name)
                    for j in range(2):
                        h = 2 * half + j
                        src = tile(name)[:, j * DV:(j + 1) * DV]
                        dst = S[n][:, h * DV:(h + 1) * DV]
                        signal = out_dve if j == 1 else None
                        if n == 1:
                            step(V.tensor_copy(dst, src), signal)
                        else:
                            step(V.scalar_tensor_tensor(dst, S[n - 1][:, h * DV:(h + 1) * DV], decay[:, h, n - 1:n], src,
                                                        ALU.mult, ALU.add), signal)
                step.settle()

            state(1)
            state(2)
            state(3)

            def logits(g):
                if g < 2:
                    n, w, t = 4, P, 0
                else:
                    n, w, t = 2, T, 1
                if g >= 4:
                    wait_tile(dve, f"pt{g - 4}")
                wait_tile(dve, f"lg{g}")
                L = prob[g % 4][:].rearrange("p (h s) -> p h s", h=n)
                chain(V.scalar_tensor_tensor(L, tile(f"lg{g}")[:].rearrange("p (h s) -> p h s", h=n), float(P) ** -0.5,
                                             keep[t][:].unsqueeze(1).to_broadcast([P, n, w]), ALU.mult, ALU.add), out_dve)
                chain(V.tensor_reduce(mx[:, 4 * g:4 * g + n], L, AX.X, ALU.max))
                chain(V.tensor_scalar(nmx[:, 4 * g:4 * g + n], mx[:, 4 * g:4 * g + n], -1.0, None, ALU.mult), nmx_ready)

            def normalize(g):
                n, w = (4, P) if g < 2 else (2, T)
                dve.wait_ge(exp_ready, g + 1)
                chain(V.reciprocal(erec[:, 4 * g:4 * g + n], esum[:, 4 * g:4 * g + n]))
                for j in range(n):
                    step(V.tensor_scalar(prob[g % 4][:, j * w:(j + 1) * w], prob[g % 4][:, j * w:(j + 1) * w],
                                         erec[:, 4 * g + j:4 * g + j + 1], None, ALU.mult), prob_ready if j == n - 1 else None)

            def gate(i):
                cc, t = divmod(i, TT)
                dst = yb[:, t, 512 * cc:512 * cc + 512]
                dve.wait_ge(gsig_ready, i + 1)
                chain(V.tensor_tensor(dst, tile(f"gb{i}")[:], dst, ALU.mult), out_dve)
                dst = dst.rearrange("p (h v) -> p h v", h=2)
                step(V.tensor_tensor(dst, dst, gng[:].unsqueeze(1).to_broadcast([P, 2, DV]), ALU.mult))

            logits(0)
            logits(1)
            normalize(0)
            normalize(1)
            dve.wait_ge(late_in, 48)
            gate(0)
            gate(1)
            logits(2)
            logits(3)
            normalize(2)
            normalize(3)
            logits(4)
            logits(5)
            normalize(4)
            normalize(5)
            gate(2)
            gate(3)
            inverse_root(8, DV, (oss_ready, 8), ovar_ready, oroot_ready)
            for i in range(4):
                t, half = divmod(i, 2)
                for j in range(2):
                    h = 2 * half + j
                    dst = yb[:, t, h * DV:(h + 1) * DV]
                    step(V.scalar_tensor_tensor(dst, tile(f"o{i}")[:, j * DV:(j + 1) * DV], rs[:, 2 * i + j:2 * i + j + 1], dst,
                                                ALU.mult, ALU.mult), out_dve if j == 1 else None)
            dve.wait_ge(g2_in, 16)
            dve.wait_ge(brow_in, 64)
            chain(V.scalar_tensor_tensor(fgb[:], fgb[:], 1.0, sc2g[:], ALU.add, ALU.mult))

            def take_sum(r):
                cols_ = slice(512 * (r % 2), 512 * (r % 2) + 512)
                dst = (gt1, sh2, sc2g, gt2)[r // 2][:, cols_]
                wait_tile(dve, f"ab{r}")
                if r // 2 == 2:
                    chain(V.tensor_tensor(dst, tile(f"ab{r}")[:], dst, ALU.mult))
                    step(V.tensor_tensor(dst, dst, fgb[:, cols_], ALU.add), out_dve)
                else:
                    step(V.tensor_tensor(dst, tile(f"ab{r}")[:], dst, ALU.add), out_dve)

            def take_wa(i):
                wait_tile(dve, f"wa{i}")
                wait_out(dve, f"ga{i}")
                step(V.tensor_tensor(mergedT[:, 2 * i:2 * i + 2, :].rearrange("p a b -> p (a b)"), tile(f"wa{i}")[:],
                                     gaT[:, 2 * i:2 * i + 2, :].rearrange("p a b -> p (a b)"), ALU.mult), out_dve)

            def take_wb(i):
                m = mergedT[:, 2 * i:2 * i + 2, :].rearrange("p a b -> p (a b)")
                wait_tile(dve, f"wb{i}")
                chain(V.tensor_tensor(tmp[:], tile(f"wb{i}")[:], gmT[:, 2 * i:2 * i + 2, :].rearrange("p a b -> p (a b)"),
                                      ALU.mult), out_dve)
                chain(V.tensor_tensor(m, m, tmp[:], ALU.add), merged_ready)

            def take_wo(i):
                cc, t = divmod(i, TT)
                xv = xs[:, t, 512 * cc:512 * cc + 512]
                wait_tile(dve, f"wo{i}")
                chain(V.tensor_tensor(tmp[:], tile(f"wo{i}")[:], gt1[:, 512 * cc:512 * cc + 512], ALU.mult), out_dve)
                chain(V.tensor_tensor(xv, xv, tmp[:], ALU.add), x2_ready)

            def second_norm(t):
                dve.wait_ge(x2ss_ready, 3 + t)
                chain(V.tensor_tensor(sq[:, t:t + 1], sq[:, t:t + 1], sq[:, TT + t:TT + t + 1], ALU.add))
                inverse_root(1, D, (x2ss_ready, 3 + t), x2var_ready, x2root_ready, first=t)
                for half in range(2):
                    cols_ = slice(512 * half, 512 * half + 512)
                    chain(V.scalar_tensor_tensor(h2[:, t, cols_], xs[:, t, cols_], rs[:, t:t + 1], sc2g[:, cols_],
                                                 ALU.mult, ALU.mult))
                    step(V.tensor_tensor(h2[:, t, cols_], h2[:, t, cols_], sh2[:, cols_], ALU.add), h2_ready)

            take_sum(0)
            take_sum(1)
            dve.wait_ge(bgu_in, 48)
            chain(V.tensor_copy(bias3[:], bgu[:]))
            chain(V.tensor_tensor(bgu[:], bgu[:], bias3[:], ALU.subtract))
            chain(V.tensor_copy(bias3[E:2 * E, :], bgu[E:2 * E, :]))
            take_sum(2)
            chain(V.tensor_copy(bias3[2 * E:3 * E, :], bgu[2 * E:3 * E, :]))
            chain(V.tensor_tensor(bgu[2 * E:3 * E, :], bgu[2 * E:3 * E, :], bias3[2 * E:3 * E, :], ALU.subtract))
            chain(V.tensor_copy(bias3[2 * E:3 * E, :], bgu[2 * E:3 * E, :]), bias3_ready)
            take_wa(0)
            take_wa(1)
            take_sum(3)
            take_wa(2)
            take_wa(3)
            take_sum(4)
            take_wb(0)
            take_wb(1)
            take_sum(5)
            take_wb(2)
            take_wb(3)
            take_sum(6)
            take_wo(0)
            take_wo(1)
            take_sum(7)
            take_wo(2)
            second_norm(0)
            take_wo(3)
            second_norm(1)
            step(V.memset(lg[:, :, E:E + TOP_K], PAD))
            wait_tile(dve, "rl")
            chain(V.tensor_copy(lg[:, :, 0:E], tile("rl")[:, 0:TT * E].rearrange("p (t e) -> p t e", e=E)), out_dve)
            for t in range(TT):
                chain(V.max(r8[:, t, :], lg[:, t, 0:E]))
                step(V.tensor_scalar(nr8[:, t:t + 1], r8[:, t, 0:1], -1.0, None, ALU.mult), rneg_ready if t == 1 else None)
                chain(V.memset(r8[:, t, TOP_K:8], PAD))
                chain(V.match_replace(lgw[:, t, :], r8[:, t, :], lg[:, t, :], GONE))
                step(V.tensor_scalar(chosen[:, t, :], lgw[:, t, 0:E], GONE, None, ALU.is_equal), chosen_ready)
            for t in range(TT):
                dve.wait_ge(rexp_ready, t + 1)
                step.settle()
                chain(V.scalar_tensor_tensor(wts[:, t, :], eexp[:, t, :], 1.0, chosen[:, t, :], ALU.mult, ALU.mult,
                                             accum_out=rt_a[:, t:t + 1]))
                chain(V.reciprocal(rt_b[:, t:t + 1], rt_a[:, t:t + 1]))
                chain(V.tensor_scalar(wts[:, t, :], wts[:, t, :], rt_b[:, t:t + 1], None, ALU.mult), wts_ready)
            wait_tile(dve, "rt")
            counts = tile("rt")[:, TT * E:TT * E + E]
            dve.wait_ge(numbers_ready, 1)
            chain(V.tensor_tensor(over[:], counts.unsqueeze(2).to_broadcast([P, E, T // SLOTS]),
                                  steps8[:].unsqueeze(1).to_broadcast([P, E, T // SLOTS]), ALU.is_gt))
            chain(V.tensor_reduce(blocks[:], over[:], AX.X, ALU.add))
            chain(V.tensor_tensor_scan(cum[:], ones[:, 0:E], blocks[:], 0.0, ALU.mult, ALU.add))
            chain(V.tensor_scalar(le[:], cum[0:MAXB + 1, :], number[0:MAXB + 1, :], None, ALU.is_le))
            chain(V.tensor_reduce(eofc[:], le[:], AX.X, ALU.add))
            step(V.tensor_copy(eofw[:], eofc[:].to_broadcast([MAXB + 1, 3 * E])), eofc_ready)
            chain(V.tensor_tensor(cumx[:], cum[:], blocks[:], ALU.subtract))
            for t in range(TT):
                chain(V.scalar_tensor_tensor(slot_id[:, t, :], cumx[:], float(SLOTS), tile("rt")[:, t * E:(t + 1) * E],
                                             ALU.mult, ALU.add), out_dve if t == 1 else None)
                chain(V.scalar_tensor_tensor(slot_id[:, t, :], slot_id[:, t, :], 1.0, chosen[:, t, :], ALU.add, ALU.mult))
                chain(V.tensor_scalar(slot_id[:, t, :], slot_id[:, t, :], -1.0, None, ALU.add))
            wait_tile(dve, "te")
            step(V.tensor_scalar(of_block[:], tile("te")[0:3 * E, 0:MAXB + 1], expert_no[:], None, ALU.is_equal))
            chain(V.tensor_scalar(eof[:], tile("te")[0:1, 0:MAXB + 1], float(E - 1), None, ALU.min), out_dve)
            step(V.tensor_copy(table_e[:], eof[:]))
            step(V.tensor_scalar(need_w[:], eof[:], 16.0, 16.0, ALU.mult, ALU.add))
            chain(V.tensor_scalar(usedf[:], cumx[0:1, :], 1.0, None, ALU.add))
            step(V.tensor_copy(table_w[:], need_w[:]))
            step(V.tensor_copy(table_used[:], usedf[:]))
            chain(V.tensor_copy(table_n[:], cum[0:1, E - 1:E]), tables_ready)

            def select(e):
                for t in range(TT):
                    ins = V.tensor_scalar(sel[:, t, :], iota[:], slot_id[:, t, ds(e, 1)], None, ALU.is_equal)
                ins.then_inc(sel_ready, 1)

            def select_weights(e, g):
                V.tensor_scalar(esel[:], ones[0:3 * E, 0:SLOTS], of_block[:, g], None, ALU.mult)
                for t in range(TT):
                    ins = V.tensor_scalar(selw[:, t, :, :], iota[:].unsqueeze(1).to_broadcast([P, 2, SLOTS]),
                                          slot_id[:, t, ds(e, 1)], wts[:, t, ds(e, 1)], ALU.is_equal, ALU.mult)
                ins.then_inc(selw_ready, 1)

            e0 = dve.value_load(table_e[0:1, 0:1], min_val=0, max_val=E - 1)
            select(e0)
            select_weights(e0, slice(0, 1))
            for n, s_ in enumerate(gu_used + dn_used + [y_full]):
                step(V.memset(primer[:, n:n + 1], 0.0), s_)
            step(V.memset(primer[:, 13:14], 0.0), acc_out)
            step(V.memset(selwT[:], 0.0), selw_out)
            step(V.memset(ysb[:], 0.0), y_out)

            def add_rows(g1_):
                dve.wait_ge(sc_full, g1_)
                for q in range(2):
                    cols_ = slice(512 * q, 512 * q + 512)
                    dve.wait_ge(row_added if q else acc_out, g1_)
                    for t in range(TT):
                        ins = V.tensor_tensor(rowt[:, t, :], sum_bank[t][q][:], gt2[:, cols_], ALU.mult)
                    ins.then_inc(row_scaled[q], 1)
                    dve.wait_ge(row_scaled[q], g1_)
                    for t in range(TT):
                        ins = V.tensor_tensor(xs[:, t, cols_], xs[:, t, cols_], rowt[:, t, :], ALU.add)
                    ins.then_inc(acc_out if q else row_added, 1)

            nb = dve.value_load(table_n[0:1, 0:1], min_val=1, max_val=MAXB)
            with dve.Fori(0, nb) as g:
                g1_ = dve.snap(g + 1)
                e = dve.value_load(table_e[0:1, ds(g + 1, 1)], min_val=0, max_val=E - 1)
                dve.wait_ge(gath_full, g1_)
                dve.wait_ge(selw_ready, g1_)
                V.tensor_scalar(iota[:], iota[:], float(SLOTS), None, ALU.add).then_inc(iota_ready, 1)
                dve.wait_ge(iota_ready, g1_)
                select(e)
                add_rows(g1_)
                dve.wait_ge(gu_full, g1_)
                V.tensor_scalar(gcl[:], bank[0][:], LIMIT, None, ALU.min).then_inc(gcl_ready, 1)
                V.tensor_scalar(ucl[:], bank[1][:], LIMIT, -LIMIT, ALU.min, ALU.max).then_inc(ucl_ready, 1)
                dve.wait_ge(sig_ready, g1_)
                V.tensor_tensor(gcl[:], gcl[:], sig[:], ALU.mult).then_inc(gs_ready, 1)
                dve.wait_ge(gs_ready, g1_)
                V.scalar_tensor_tensor(act_t[:], ucl[:], 1.0, gcl[:], ALU.add, ALU.mult).then_inc(act_ready, 1)
                dve.wait_ge(selwT_full, g1_)
                select_weights(e, ds(g + 1, 1))
            dve.wait_ge(acc_out, dve.snap(nb + 1))
            for t in range(TT):
                dve.wait_ge(last_full, t + 1)
                for q in range(2):
                    ins = V.tensor_tensor(rowt[:, q, :], sum_bank[t][q][:], gt2[:, 512 * q:512 * q + 512], ALU.mult)
                chain(ins)
                chain(V.tensor_tensor(xs[:, t, :], xs[:, t, :], rowt[:].rearrange("p q n -> p (q n)"), ALU.add), add_done)
            inverse_root(TT, D, (fss_ready, TT), fvar_ready, froot_ready)
            dve.wait_ge(fg_in, 16)
            dve.wait_ge(gu_in[0], 16 * E)
            for t in range(TT):
                step(V.scalar_tensor_tensor(final[:, t, :], xs[:, t, :], rs[:, t:t + 1], fgb[:], ALU.mult, ALU.mult), fin_ready)

        @block.tensor
        def _(pe):
            M = nc.tensor.matmul
            filled = [0]

            def begin(name):
                assert PLAN[filled[0]][0] == name, (PLAN[filled[0]][0], name)
                if filled[0] >= 8:
                    wait_out(pe, PLAN[filled[0] - 8][0])
                filled[0] += 1
                return tile(name)

            def full(ins):
                ins.then_inc(tile_full, 1)

            def arrived(kind, c):
                n = PIECE_NO[kind, c]
                pe.wait_ge(piece_in[n % NP2], 16 * (n // NP2 + 1))
                return piece[n % NP2]

            def modulation_part(name, a):
                w = arrived("ada", a)
                ps = begin(name)
                for r in range(2):
                    for q in range(4):
                        k = 4 * r + q
                        ins = M(ps[32 * q:32 * q + 32, :], silc[:, k, :], w[:, k, :], start=(r == 0), stop=(r == 1),
                                tile_position=(0, 32 * q))
                full(ins)

            def by_feature(kind, c, src):
                w = arrived(kind, c)
                for j in range(2):
                    ps = begin(f"{kind}{2 * c + j}")
                    for f in range(2):
                        for k in range(KT):
                            a = (2 * j + f) * P
                            ins = M(ps[:, f * T:(f + 1) * T], w[:, k, a:a + P], src[:, k, :], start=(k == 0), stop=(k == KT - 1))
                    full(ins)

            def by_token(kind, c, src):
                w = arrived(kind, c)
                for t in range(TT):
                    ps = begin(f"{kind}{2 * c + t}")
                    for k in range(KT):
                        ins = M(ps[:], src[:, k, t * P:(t + 1) * P], w[:, k, :], start=(k == 0), stop=(k == KT - 1))
                    full(ins)

            def transposes(name, src, t, half):
                ps = begin(name)
                for j in range(4):
                    a = (4 * half + j) * P
                    ins = nc.tensor.transpose(ps[:, j * P:(j + 1) * P], src[:, t, a:a + P], ident[:])
                full(ins)

            pe.wait_ge(consts_ready, 1)
            pe.wait_ge(silc_ready, 1)

            def modulation_columns(ps, a, i):
                wait_out(pe, f"ada{i}")
                for f in range(4):
                    ins = M(ps[:, a + f:a + f + 1], modp[i][:, f * P:(f + 1) * P], inv32[:, 0:1], start=True, stop=True)
                return ins

            modulation_part("ada0", 0)
            modulation_part("ada1", 1)
            for i in range(4):
                t, half = divmod(i, 2)
                pe.wait_ge(xn_ready, t + 1)
                transposes(f"xT{i}", xn, t, half)
            modulation_part("ada2", 2)
            ps = begin("colA")
            for i in range(3):
                ins = modulation_columns(ps, 4 * i, i)
            full(ins)
            modulation_part("ada3", 3)
            full(modulation_columns(begin("colB"), 0, 3))
            pe.wait_ge(wsm_in, 32)
            ps = begin("small")
            for k in range(KT):
                if k == 0:
                    wait_out(pe, "xT2")
                elif k == 4:
                    wait_out(pe, "xT1")
                    wait_out(pe, "xT3")
                ins = M(ps[:, 0:T], wsm[:, k, :], hT[:, k, :], start=(k == 0), stop=(k == KT - 1))
            full(ins)
            by_feature("qi", 0, hT)
            wait_out(pe, "small")
            ps = begin("wi")
            for t in range(TT):
                ins = M(ps[:, t * IH:(t + 1) * IH], wiT[:, t * P:(t + 1) * P], ident[0:IH, 0:IH], start=True, stop=True)
            full(ins)
            pe.wait_ge(wgl_in, 16)
            for i in range(2):
                ps = begin(f"z{i}")
                for j in range(2):
                    h = 2 * i + j
                    ins = M(ps[:, j * T:(j + 1) * T], wgl[:, h * P:(h + 1) * P], lrT[:], start=True, stop=True)
                full(ins)
            by_feature("qa", 0, hT)
            wait_out(pe, "qi1")
            def index_products(t, names, heads):
                w = P if t == 0 else T
                banks_ = []
                for name in names:
                    banks_.append(begin(name))
                for j in range(len(heads[0])):
                    for b_ in range(2):
                        h = heads[b_][j]
                        r = 64 * (h % 2)
                        ins = M(banks_[b_][:, j * w:(j + 1) * w], qiT[r:r + 64, h // 2, t * P:(t + 1) * P], kiT[r:r + 64, 0:w],
                                start=True, stop=True)
                        if j == len(heads[0]) - 1:
                            full(ins)
            index_products(0, ("sx0", "sx1"), ((0, 2, 4, 6), (1, 3, 5, 7)))
            index_products(1, ("sy0", "sy1"), ((0, 2), (1, 3)))
            index_products(1, ("sy2", "sy3"), ((4, 6), (5, 7)))
            by_feature("qa", 1, hT)
            by_feature("qb", 0, hT)
            by_feature("kb", 0, hT)
            by_feature("ka", 0, hT)
            for t in range(TT):
                ps = begin(f"kdT{t}")
                pe.wait_ge(kd_ready, 2)
                for h in range(GH):
                    ins = nc.tensor.transpose(ps[:, h * P:(h + 1) * P], kd[:, h, t * P:(t + 1) * P], ident[:])
                full(ins)
            ps = begin("AT")
            wait_out(pe, "kb1")
            for n in range(NCH):
                r = 64 * (n % 2)
                for h in range(GH):
                    a = (h * 2 + n // 2) * CHUNK
                    ins = M(ps[r:r + 64, a:a + CHUNK], ke[:, h, n * CHUNK:(n + 1) * CHUNK], qe[:, h, n * CHUNK:(n + 1) * CHUNK],
                            start=True, stop=True)
            full(ins)
            by_feature("ka", 1, hT)
            by_token("vb", 0, hT)
            by_token("vb", 1, hT)

            def state_step(n):
                cn = n - 1
                r, t = 64 * (cn % 2), cn // 2
                for half, name in enumerate((f"s{n}a", f"s{n}b")):
                    ps = begin(name)
                    for j in range(2):
                        h = 2 * half + j
                        ins = M(ps[:, j * DV:(j + 1) * DV], kdt[r:r + 64, t, h * P:(h + 1) * P], vb[r:r + 64, t, h * DV:(h + 1) * DV],
                                start=True, stop=True)
                    full(ins)

            wait_out(pe, "vb3")
            state_step(1)
            by_token("va", 0, hT)
            state_step(2)
            by_token("va", 1, hT)
            state_step(3)

            def logit_products(g):
                ps = begin(f"lg{g}")
                if g < 2:
                    t, w, heads = 0, P, range(4 * g, 4 * g + 4)
                else:
                    t, w, heads = 1, T, range(2 * (g - 2), 2 * (g - 2) + 2)
                for j, h in enumerate(heads):
                    ins = M(ps[:, j * w:(j + 1) * w], qaT[:, h, t * P:(t + 1) * P], kaT[:, h, 0:w], start=True, stop=True)
                full(ins)

            def prob_transposes(g):
                ps = begin(f"pt{g}")
                pe.wait_ge(prob_ready, g + 1)
                for j in range(4):
                    ins = nc.tensor.transpose(ps[:, j * P:(j + 1) * P], prob[g % 4][:, j * P:(j + 1) * P], ident[:])
                full(ins)

            def attend(i):
                ps = begin(f"ya{i}")
                t, half = divmod(i, 2)
                if t == 0:
                    wait_out(pe, f"pt{i}")
                    for j in range(4):
                        h = 4 * half + j
                        ins = M(ps[:, j * P:(j + 1) * P], va[:, 0, h * P:(h + 1) * P], probT[i][:, j * P:(j + 1) * P],
                                start=True, stop=True)
                else:
                    wait_out(pe, f"pt{3 + 2 * half}")
                    for j in range(4):
                        h = 4 * half + j
                        g = 2 + h // 2
                        for s_ in range(TT):
                            a = ((h % 2) * 2 + s_) * P
                            ins = M(ps[:, j * P:(j + 1) * P], va[:, s_, h * P:(h + 1) * P], probT[g % 4][:, a:a + P],
                                    start=(s_ == 0), stop=(s_ == TT - 1))
                full(ins)

            wait_out(pe, "va3")
            logit_products(0)
            logit_products(1)
            by_token("gb", 0, hT)
            prob_transposes(0)
            prob_transposes(1)
            logit_products(2)
            logit_products(3)
            attend(0)
            attend(1)
            logit_products(4)
            logit_products(5)
            by_token("gb", 1, hT)
            for g in range(2, 6):
                prob_transposes(g)
            pe.wait_ge(at_masked, 2)
            wait_out(pe, "s3b")
            for i in range(4):
                t, half = divmod(i, 2)
                ps = begin(f"o{i}")
                for n in (2 * t, 2 * t + 1):
                    r = 64 * (n % 2)
                    for j in range(2):
                        h = 2 * half + j
                        o_ = ps[r:r + 64, j * DV:(j + 1) * DV]
                        a = (h * 2 + n // 2) * CHUNK
                        ins = M(o_, AT[r:r + 64, a:a + CHUNK], vb[r:r + 64, t, h * DV:(h + 1) * DV], start=True, stop=(n == 0))
                        if n > 0:
                            ins = M(o_, qe[:, h, n * CHUNK:(n + 1) * CHUNK], S[n][:, h * DV:(h + 1) * DV], start=False, stop=True)
                full(ins)
            attend(2)
            attend(3)

            def add_parts(r):
                ps = begin(f"ab{r}")
                wait_out(pe, f"ap{r}")
                full(M(ps[:], inv32[:], modq[r % 2][:], start=True, stop=True))

            by_feature("ga", 0, hT)
            modulation_part("ap0", 4)
            by_feature("ga", 1, hT)
            modulation_part("ap1", 5)
            add_parts(0)
            for i in range(4):
                t, half = divmod(i, 2)
                wait_out(pe, f"o{2 * t + 1}")
                transposes(f"yT{i}", yb, t, half)
            r = 2
            for kind, src in (("gm", hT), ("wa", yaT), ("wb", ybT)):
                for cc in range(2):
                    by_feature(kind, cc, src)
                    modulation_part(f"ap{r}", 4 + r)
                    add_parts(r - 1)
                    r += 1
            pe.wait_ge(merged_ready, 4)
            by_token("wo", 0, mergedT)
            add_parts(7)
            by_token("wo", 1, mergedT)
            for i in range(4):
                t, half = divmod(i, 2)
                pe.wait_ge(h2_ready, i + 1)
                transposes(f"hh{i}", h2, t, half)
            ps = begin("rp")
            wait_out(pe, "hh3")
            pe.wait_ge(late_in, 48)
            for r in range(2):
                for q in range(4):
                    k = 4 * r + q
                    ins = M(ps[32 * q:32 * q + 32, 0:T], wr[:, k, :], h2T[:, k, :], start=(r == 0), stop=(r == 1))
            full(ins)
            ps = begin("rl")
            wait_out(pe, "rp")
            for t in range(TT):
                M(ps[:, t * E:(t + 1) * E], rpart[:, t * P:(t + 1) * P], stack[:], start=True, stop=False)
                ins = M(ps[:, t * E:(t + 1) * E], ones[0:1, :], rb[:], start=False, stop=True)
            full(ins)
            ps = begin("rt")
            pe.wait_ge(chosen_ready, TT)
            M(ps[:, 0:E], before[:], chosen[:, 0, :], start=True, stop=True)
            M(ps[:, E:2 * E], ones[:], chosen[:, 0, :], start=True, stop=False)
            M(ps[:, E:2 * E], before[:], chosen[:, 1, :], start=False, stop=True)
            M(ps[:, 2 * E:3 * E], ones[:], chosen[:, 0, :], start=True, stop=False)
            full(M(ps[:, 2 * E:3 * E], ones[:], chosen[:, 1, :], start=False, stop=True))
            ps = begin("te")
            pe.wait_ge(eofc_ready, 1)
            full(M(ps[0:3 * E, 0:MAXB + 1], eofw[:], ident[0:MAXB + 1, 0:MAXB + 1], start=True, stop=True))

            ps = begin("wt")
            pe.wait_ge(wts_ready, TT)
            for t in range(TT):
                ins = nc.tensor.transpose(ps[0:E, t * P:(t + 1) * P], wts[:, t, :], ident[:])
            full(ins)

            def gather(also=None):
                for t in range(TT):
                    for q in range(2):
                        ins = M(bank[2][64 * q:64 * q + 64, :], sel[:, t, :], h2[:, t, 512 * q:512 * q + 512],
                                start=(t == 0), stop=(t == TT - 1))
                        if also is not None and t == 0 and q == 0:
                            ins.then_inc(also, 1)
                ins.then_inc(gath_full, 1)

            def gather_transposes():
                for j in range(4):
                    ins = nc.tensor.transpose(bank[3][:, j * P:(j + 1) * P], gx[:, j * P:(j + 1) * P], ident[:])
                ins.then_inc(gxT_full, 1)

            def scatter():
                for t in range(TT):
                    for q in range(2):
                        ins = M(sum_bank[t][q][:], selwT[64 * q:64 * q + 64, t * P:(t + 1) * P], ysb[64 * q:64 * q + 64, :],
                                start=True, stop=True)
                ins.then_inc(sc_full, 1)

            pe.wait_ge(bias3_ready, 1)
            pe.wait_ge(tables_ready, 1)
            nb = pe.value_load(table_n[0:1, 0:1], min_val=1, max_val=MAXB)
            wait_out(pe, "te")
            pe.wait_ge(sel_ready, 1)
            gather()
            pe.wait_ge(gx_out, 1)
            gather_transposes()
            with pe.Fori(0, nb) as g:
                g1_ = pe.snap(g + 1)
                g2_ = pe.snap(g + 2)
                landed = pe.value_load(table_w[0:1, ds(g, 1)], min_val=16, max_val=16 * E)
                pe.wait_ge(xg_out, g1_)
                pe.wait_ge(selw_ready, g1_)
                pe.wait_ge(selw_out, g1_)
                for k in range(KT):
                    pe.wait_ge(gu_in[k], landed)
                    for u in range(2):
                        for q in range(2):
                            cols_ = slice(1024 * u + 512 * q, 1024 * u + 512 * q + 512)
                            ins = M(bank[u][64 * q:64 * q + 64, :], xg[:, k % 4, 64 * (k // 4):64 * (k // 4) + 64],
                                    gu_slot[k][:, cols_], start=(k == 0), stop=(k == KT - 1))
                    ins.then_inc(gu_used[k] if k < KT - 1 else gu_full, 1)
                    if k == 0:
                        for u in range(2):
                            for q in range(2):
                                cols_ = slice(1024 * u + 512 * q, 1024 * u + 512 * q + 512)
                                M(bank[u][64 * q:64 * q + 64, :], esel[:], bias3[:, cols_], start=False, stop=False)
                        pe.wait_ge(y_out, g1_)
                        scatter()
                pe.wait_ge(sel_ready, g2_)
                gather(gu_used[KT - 1])
                pe.wait_ge(ucl_ready, g1_)
                for t in range(TT):
                    ins = nc.tensor.transpose(bank[1][:, t * P:(t + 1) * P], selw[:, t, :, :].rearrange("p a s -> p (a s)"), ident[:])
                ins.then_inc(selwT_full, 1)
                pe.wait_ge(gx_out, g2_)
                gather_transposes()
                pe.wait_ge(acc_out, g2_)
                pe.wait_ge(act_ready, g1_)
                for j in range(4):
                    ins = nc.tensor.transpose(bank[4][:, j * P:(j + 1) * P], act_t[:, j * P:(j + 1) * P], ident[:])
                ins.then_inc(actT_full, 1)
                pe.wait_ge(actT_out, g1_)
                for f in range(KT):
                    if f % 2 == 0:
                        pe.wait_ge(dn_in[f // 2], landed)
                    for q in range(2):
                        ins = M(bank[5][64 * q:64 * q + 64, :], actT[:, f % 4, 64 * (f // 4):64 * (f // 4) + 64],
                                dn_slot[f // 2][:, f % 2, 512 * q:512 * q + 512], start=(f == 0), stop=(f == KT - 1))
                    if f % 2 == 1:
                        ins.then_inc(dn_used[f // 2] if f < KT - 1 else y_full, 1)
            pe.wait_ge(bd_in, 16)
            wait_out(pe, "wt")
            pe.wait_ge(acc_out, pe.snap(nb + 1))

            def bias_rows(t):
                for q in range(2):
                    M(sum_bank[t][q][:], wT[:, t * P:(t + 1) * P], bd[:, 512 * q:512 * q + 512], start=True, stop=False)

            def last_rows(t):
                for q in range(2):
                    ins = M(sum_bank[t][q][:], selwT[64 * q:64 * q + 64, t * P:(t + 1) * P], ysb[64 * q:64 * q + 64, :],
                            start=False, stop=True)
                ins.then_inc(last_full, 1)

            bias_rows(0)
            pe.wait_ge(selw_out, pe.snap(nb + 1))
            pe.wait_ge(y_out, pe.snap(nb + 1))
            last_rows(0)
            bias_rows(1)
            last_rows(1)


_INS = ['x', 'c', 'w_ada', 'b_ada', 'norm1_g', 'w_in', 'w_gate_lr', 'b_gate', 'gla_norm_g', 'w_branch_a', 'w_branch_b',
        'w_out', 'norm2_g', 'router_w', 'router_b', 'w_gate_up', 'b_gate_up', 'w_down', 'b_down', 'final_g']


def kernel(**inputs):
    import numpy as np
    import concourse.bacc as bacc
    from concourse.bass_utils import run_bass_kernel_spmd

    nc = bacc.Bacc("TRN2", target_bir_lowering=False, num_devices=1)
    arrays, args = {}, []
    for name in _INS:
        a = np.ascontiguousarray(inputs[name])
        arrays[f"in_{name}"] = a
        args.append(nc.dram_tensor(f"in_{name}", a.shape, mybir.dt.from_np(a.dtype), kind="ExternalInput").ap())
    out = nc.dram_tensor("out_0", inputs['x'].shape, F32, kind="ExternalOutput").ap()
    hybrid_block(nc, *args, out)
    r = run_bass_kernel_spmd(nc, [arrays], core_ids=[0])
    return r.results[0]["out_0"]
```
